# Optimizing a Trainium2 kernel written in Bass

```python
import math
import jax
import jax.numpy as jnp
from jax import lax
import numpy as np
import jax, jax.numpy as jnp

D_MODEL = 2048
BATCH = 1
SEQ = 256
DEPTH = 1

HEAD_DIM = 64
NSA_HEADS = 16
NSA_KV_HEADS = 2
NSA_HPG = NSA_HEADS // NSA_KV_HEADS
CMP_LEN = 32
CMP_STRIDE = 16
CMP_HIDDEN = 128
SLC_BLOCK = 64
N_SELECT = 16
NSA_WINDOW = 512
FORCE_BONUS = 1e4
SWA_HEADS = 16
SWA_KV_HEADS = 2
SWA_HPG = SWA_HEADS // SWA_KV_HEADS
SWA_WINDOW = 128
REL_BUCKETS = 32
REL_EXACT = 16
REL_MAX_DIST = 2048
PEER_HEADS = 8
PEER_NKEYS = 128
PEER_EXPERTS = PEER_NKEYS * PEER_NKEYS
PEER_QDIM = 256
PEER_TOPK = 16
PEER_CHUNK = 128

Q_BLOCK = 128
NEG = -1e30
RMS_EPS = 1e-6
NSA_Q_W = NSA_HEADS * HEAD_DIM
NSA_KV_W = NSA_KV_HEADS * HEAD_DIM
NSA_GATE_W = NSA_HEADS * 3
SWA_Q_W = SWA_HEADS * HEAD_DIM
SWA_KV_W = SWA_KV_HEADS * HEAD_DIM
MIX_WIDTH = NSA_Q_W + SWA_Q_W
PROJ_SPLITS = (NSA_Q_W, NSA_KV_W, NSA_KV_W, NSA_KV_W, NSA_KV_W, NSA_KV_W, NSA_KV_W, NSA_GATE_W, SWA_Q_W, SWA_KV_W, SWA_KV_W)
PROJ_WIDTH = sum(PROJ_SPLITS)
SLC_OFFSETS = (-1, 0, 1, 2, 3)
SLC_WEIGHTS = (1.0, 2.0, 2.0, 2.0, 1.0)


def rmsnorm(x, g):
    xf = x.astype(jnp.float32)
    y = xf * lax.rsqrt(jnp.mean(xf * xf, axis=-1, keepdims=True) + RMS_EPS)
    return (y * g.astype(jnp.float32)).astype(x.dtype)

def rel_bucket(dist):
    d = jnp.maximum(dist, 0)
    n_log = REL_BUCKETS - REL_EXACT
    large = REL_EXACT + (jnp.log(jnp.maximum(d, 1).astype(jnp.float32) / REL_EXACT)
                         / math.log(REL_MAX_DIST / REL_EXACT) * n_log).astype(jnp.int32)
    large = jnp.minimum(large, REL_BUCKETS - 1)
    return jnp.where(d < REL_EXACT, d, large)

def masked_softmax(logits, valid):
    p = jax.nn.softmax(jnp.where(valid, logits, NEG), axis=-1)
    return jnp.where(valid, p, 0.0)

def compress(k, pos, w1, w2):
    B, S, G, Dh = k.shape
    chunks = k.reshape(B, S // CMP_STRIDE, CMP_STRIDE, G, Dh)
    blocks = jnp.concatenate([chunks[:, :-1], chunks[:, 1:]], axis=2)
    blocks = blocks + pos[None, None, :, None, :]
    flat = jnp.moveaxis(blocks, 3, 2).reshape(B, blocks.shape[1], G, CMP_LEN * Dh)
    return jax.nn.gelu(flat @ w1) @ w2

def hybrid_mixer(xn, w_in, cmp_pos_k, cmp_w1_k, cmp_w2_k, cmp_pos_v, cmp_w1_v, cmp_w2_v,
                 sinks, rel_bias, w_out):
    B, S, _ = xn.shape
    f32 = jnp.float32
    GA, GB = NSA_KV_HEADS, SWA_KV_HEADS
    NS = S // SLC_BLOCK
    n_sel = min(N_SELECT, NS)
    scale = HEAD_DIM ** -0.5
    offs = [int(c) for c in np.cumsum(PROJ_SPLITS)[:-1]]
    (q_a, kc, vc, ks, vs, kw, vw, gate_a, q_b, k_b, v_b) = jnp.split(xn @ w_in, offs, axis=-1)

    q_a = q_a.reshape(B, S, GA, NSA_HPG, HEAD_DIM)
    q_b = q_b.reshape(B, S, GB, SWA_HPG, HEAD_DIM)
    gate_a = jax.nn.sigmoid(gate_a).reshape(B, S, GA, NSA_HPG, 3)
    kc_c = compress(kc.reshape(B, S, GA, HEAD_DIM), cmp_pos_k, cmp_w1_k, cmp_w2_k)
    vc_c = compress(vc.reshape(B, S, GA, HEAD_DIM), cmp_pos_v, cmp_w1_v, cmp_w2_v)
    n_cmp = kc_c.shape[1]
    cmp_end = jnp.arange(n_cmp) * CMP_STRIDE + CMP_LEN - 1
    ks_blk = ks.reshape(B, NS, SLC_BLOCK, GA, HEAD_DIM).transpose(0, 3, 1, 2, 4)
    vs_blk = vs.reshape(B, NS, SLC_BLOCK, GA, HEAD_DIM).transpose(0, 3, 1, 2, 4)
    pad_a = ((0, 0), (NSA_WINDOW, 0), (0, 0), (0, 0))
    kw_pad = jnp.pad(kw.reshape(B, S, GA, HEAD_DIM), pad_a)
    vw_pad = jnp.pad(vw.reshape(B, S, GA, HEAD_DIM), pad_a)
    pad_b = ((0, 0), (SWA_WINDOW, 0), (0, 0), (0, 0))
    kb_pad = jnp.pad(k_b.reshape(B, S, GB, HEAD_DIM), pad_b)
    vb_pad = jnp.pad(v_b.reshape(B, S, GB, HEAD_DIM), pad_b)

    bias_a = rel_bias[:, :NSA_HEADS].reshape(REL_BUCKETS, GA, NSA_HPG).astype(f32)
    bias_b = rel_bias[:, NSA_HEADS:].reshape(REL_BUCKETS, GB, SWA_HPG).astype(f32)
    sink = sinks.astype(f32).reshape(1, GB, SWA_HPG, 1, 1)
    b_idx = jnp.arange(B)[:, None, None, None]
    g_idx = jnp.arange(GA)[None, :, None, None]
    blk_ids = jnp.arange(NS)
    slc_tok = jnp.arange(SLC_BLOCK)

    def token_bias(table, dist):
        return table[rel_bucket(dist)].transpose(2, 3, 0, 1)

    def query_block(i):
        q0 = i * Q_BLOCK
        pos_q = q0 + jnp.arange(Q_BLOCK)
        qa = lax.dynamic_slice_in_dim(q_a, q0, Q_BLOCK, axis=1)
        dt = qa.dtype

        dist_c = pos_q[:, None] - cmp_end[None, :]
        lg_c = jnp.einsum('bqghd,bcgd->bghqc', qa, kc_c, preferred_element_type=f32) * scale
        p_cmp = masked_softmax(lg_c + token_bias(bias_a, dist_c), dist_c >= 0)
        o_cmp = jnp.einsum('bghqc,bcgd->bqghd', p_cmp.astype(dt), vc_c)

        imp = jnp.pad(p_cmp.sum(axis=2), ((0, 0), (0, 0), (0, 0), (1, 1)))
        imp_s = jnp.zeros(imp.shape[:-1] + (NS,), f32)
        for r, w in zip(SLC_OFFSETS, SLC_WEIGHTS):
            imp_s = imp_s + w * imp[..., r + 1: r + 2 + 4 * (NS - 1): 4]
        cb = pos_q[:, None] // SLC_BLOCK
        j = blk_ids[None, :]
        forced = (j == 0) | (j == cb) | (j == cb - 1)
        score = jnp.where(j > cb, NEG, imp_s + jnp.where(forced, FORCE_BONUS, 0.0))
        _, sel = lax.top_k(score, n_sel)
        ks_g = ks_blk[b_idx, g_idx, sel].reshape(B, GA, Q_BLOCK, n_sel * SLC_BLOCK, HEAD_DIM)
        vs_g = vs_blk[b_idx, g_idx, sel].reshape(B, GA, Q_BLOCK, n_sel * SLC_BLOCK, HEAD_DIM)
        kpos = (sel[..., None] * SLC_BLOCK + slc_tok).reshape(B, GA, Q_BLOCK, n_sel * SLC_BLOCK)
        dist_s = pos_q[:, None] - kpos
        bias_s = jnp.moveaxis(bias_a[rel_bucket(dist_s), g_idx], -1, 2)
        lg_s = jnp.einsum('bqghd,bgqkd->bghqk', qa, ks_g, preferred_element_type=f32) * scale
        p_s = masked_softmax(lg_s + bias_s, (dist_s >= 0)[:, :, None])
        o_slc = jnp.einsum('bghqk,bgqkd->bqghd', p_s.astype(dt), vs_g)

        La = Q_BLOCK + NSA_WINDOW
        kwin = lax.dynamic_slice_in_dim(kw_pad, q0, La, axis=1)
        vwin = lax.dynamic_slice_in_dim(vw_pad, q0, La, axis=1)
        kpos_w = q0 - NSA_WINDOW + jnp.arange(La)
        dist_w = pos_q[:, None] - kpos_w[None, :]
        valid_w = (dist_w >= 0) & (dist_w < NSA_WINDOW) & (kpos_w[None, :] >= 0)
        lg_w = jnp.einsum('bqghd,blgd->bghql', qa, kwin, preferred_element_type=f32) * scale
        p_w = masked_softmax(lg_w + token_bias(bias_a, dist_w), valid_w)
        o_win = jnp.einsum('bghql,blgd->bqghd', p_w.astype(dt), vwin)

        g = lax.dynamic_slice_in_dim(gate_a, q0, Q_BLOCK, axis=1)
        o_a = g[..., 0:1] * o_cmp + g[..., 1:2] * o_slc + g[..., 2:3] * o_win

        qb = lax.dynamic_slice_in_dim(q_b, q0, Q_BLOCK, axis=1)
        Lb = Q_BLOCK + SWA_WINDOW
        kbw = lax.dynamic_slice_in_dim(kb_pad, q0, Lb, axis=1)
        vbw = lax.dynamic_slice_in_dim(vb_pad, q0, Lb, axis=1)
        kpos_b = q0 - SWA_WINDOW + jnp.arange(Lb)
        dist_b = pos_q[:, None] - kpos_b[None, :]
        valid_b = (dist_b >= 0) & (dist_b < SWA_WINDOW) & (kpos_b[None, :] >= 0)
        lg_b = jnp.einsum('bqghd,blgd->bghql', qb, kbw, preferred_element_type=f32) * scale
        lg_b = jnp.where(valid_b, lg_b + token_bias(bias_b, dist_b), NEG)
        m = jnp.maximum(lg_b.max(axis=-1, keepdims=True), sink)
        e = jnp.exp(lg_b - m)
        p_b = e / (e.sum(axis=-1, keepdims=True) + jnp.exp(sink - m))
        o_b = jnp.einsum('bghql,blgd->bqghd', p_b.astype(dt), vbw)

        return jnp.concatenate([o_a.reshape(B, Q_BLOCK, NSA_Q_W),
                                o_b.reshape(B, Q_BLOCK, SWA_Q_W)], axis=-1)

    out = lax.map(query_block, jnp.arange(S // Q_BLOCK))
    out = out.transpose(1, 0, 2, 3).reshape(B, S, MIX_WIDTH)
    return out @ w_out

def peer(xn, wq, subkeys, u, v):
    B, S, D = xn.shape
    T = B * S
    xt = xn.reshape(T, D)
    q = (xt @ wq).reshape(T, PEER_HEADS, 2, PEER_QDIM // 2).astype(jnp.float32)
    s1 = jnp.einsum('thd,nd->thn', q[:, :, 0], subkeys[0].astype(jnp.float32))
    s2 = jnp.einsum('thd,nd->thn', q[:, :, 1], subkeys[1].astype(jnp.float32))
    v1, i1 = lax.top_k(s1, PEER_TOPK)
    v2, i2 = lax.top_k(s2, PEER_TOPK)
    cand = (v1[..., :, None] + v2[..., None, :]).reshape(T, PEER_HEADS, PEER_TOPK * PEER_TOPK)
    sc, ci = lax.top_k(cand, PEER_TOPK)
    e1 = jnp.take_along_axis(i1, ci // PEER_TOPK, axis=-1)
    e2 = jnp.take_along_axis(i2, ci % PEER_TOPK, axis=-1)
    idx = e1 * PEER_NKEYS + e2
    gate = jax.nn.softmax(sc, axis=-1).astype(xn.dtype)
    n_ch = T // PEER_CHUNK

    def chunk(args):
        xc, ic, gc = args
        h = jax.nn.gelu(jnp.einsum('cd,chkd->chk', xc, u[ic]))
        return jnp.einsum('chk,chkd->cd', gc * h, v[ic])

    out = lax.map(chunk, (xt.reshape(n_ch, PEER_CHUNK, D),
                          idx.reshape(n_ch, PEER_CHUNK, PEER_HEADS, PEER_TOPK),
                          gate.reshape(n_ch, PEER_CHUNK, PEER_HEADS, PEER_TOPK)))
    return out.reshape(B, S, D)

def first_inputs(seed: int = 0) -> dict:
    key = jax.random.key(seed)
    ks = jax.random.split(key, 18)

    def nrm(k, shape, s):
        return jax.random.normal(k, shape, jnp.float32) * s

    return {
        'x': nrm(ks[0], (BATCH, SEQ, D_MODEL), 1.0),
        'attn_norm': 1.0 + nrm(ks[1], (DEPTH, D_MODEL), 0.02),
        'w_in': nrm(ks[2], (DEPTH, D_MODEL, PROJ_WIDTH), D_MODEL ** -0.5),
        'cmp_pos_k': nrm(ks[3], (DEPTH, CMP_LEN, HEAD_DIM), 0.1),
        'cmp_w1_k': nrm(ks[4], (DEPTH, CMP_LEN * HEAD_DIM, CMP_HIDDEN), (CMP_LEN * HEAD_DIM) ** -0.5),
        'cmp_w2_k': nrm(ks[5], (DEPTH, CMP_HIDDEN, HEAD_DIM), CMP_HIDDEN ** -0.5),
        'cmp_pos_v': nrm(ks[6], (DEPTH, CMP_LEN, HEAD_DIM), 0.1),
        'cmp_w1_v': nrm(ks[7], (DEPTH, CMP_LEN * HEAD_DIM, CMP_HIDDEN), (CMP_LEN * HEAD_DIM) ** -0.5),
        'cmp_w2_v': nrm(ks[8], (DEPTH, CMP_HIDDEN, HEAD_DIM), CMP_HIDDEN ** -0.5),
        'sinks': nrm(ks[9], (DEPTH, SWA_HEADS), 0.5),
        'w_out': nrm(ks[10], (DEPTH, MIX_WIDTH, D_MODEL), MIX_WIDTH ** -0.5),
        'ffn_norm': 1.0 + nrm(ks[11], (DEPTH, D_MODEL), 0.02),
        'peer_wq': nrm(ks[12], (DEPTH, D_MODEL, PEER_HEADS * PEER_QDIM), D_MODEL ** -0.5),
        'peer_subkeys': nrm(ks[13], (DEPTH, 2, PEER_NKEYS, PEER_QDIM // 2), (PEER_QDIM // 2) ** -0.5),
        'peer_u': nrm(ks[14], (DEPTH, PEER_EXPERTS, D_MODEL), D_MODEL ** -0.5),
        'peer_v': nrm(ks[15], (DEPTH, PEER_EXPERTS, D_MODEL), (PEER_HEADS * PEER_TOPK) ** -0.5),
        'rel_bias': nrm(ks[16], (REL_BUCKETS, NSA_HEADS + SWA_HEADS), 0.5),
        'final_norm': 1.0 + nrm(ks[17], (D_MODEL,), 0.02),
    }

def first_block(x, attn_norm, w_in, cmp_pos_k, cmp_w1_k, cmp_w2_k, cmp_pos_v, cmp_w1_v, cmp_w2_v,
              sinks, w_out, ffn_norm, peer_wq, peer_subkeys, peer_u, peer_v, rel_bias, final_norm):
    h = x
    for l in range(DEPTH):
        h = h + hybrid_mixer(rmsnorm(h, attn_norm[l]), w_in[l],
                             cmp_pos_k[l], cmp_w1_k[l], cmp_w2_k[l],
                             cmp_pos_v[l], cmp_w1_v[l], cmp_w2_v[l],
                             sinks[l], rel_bias, w_out[l])
        h = h + peer(rmsnorm(h, ffn_norm[l]), peer_wq[l], peer_subkeys[l], peer_u[l], peer_v[l])
    return rmsnorm(h, final_norm)


MIX_WIDTH_2 = D_MODEL
ATTN_WIDTH = MIX_WIDTH_2 // 2
SSM_WIDTH = MIX_WIDTH_2 - ATTN_WIDTH
ATTN_HEAD_DIM = 128
ATTN_HEADS = ATTN_WIDTH // ATTN_HEAD_DIM
MOBA_BLOCK = 256
MOBA_TOPK = 3
Q_CHUNK = 32
SSM_HEAD_DIM = 64
SSM_HEADS = SSM_WIDTH // SSM_HEAD_DIM
SSM_GROUPS = 2
SSM_HEADS_PER_GROUP = SSM_HEADS // SSM_GROUPS
SSM_STATE = 128
SSM_CONV = 4
SSD_CHUNK = 128
XBC_WIDTH = SSM_WIDTH + 2 * SSM_GROUPS * SSM_STATE
IN_COLS = 3 * ATTN_WIDTH + SSM_WIDTH + XBC_WIDTH + SSM_HEADS
SPLIT_POINTS = (ATTN_WIDTH, 2 * ATTN_WIDTH, 3 * ATTN_WIDTH,
                3 * ATTN_WIDTH + SSM_WIDTH, 3 * ATTN_WIDTH + SSM_WIDTH + XBC_WIDTH)
D_FF = 5632
FFN_CONV = 3
EPS = 1e-6


def rms_norm(x, w):
    xf = x.astype(jnp.float32)
    y = xf * lax.rsqrt(jnp.mean(xf * xf, axis=-1, keepdims=True) + EPS)
    return (y * w.astype(jnp.float32)).astype(x.dtype)

def causal_dwconv(u, w, bias):
    k_width = w.shape[0]
    s = u.shape[1]
    up = jnp.pad(u, ((0, 0), (k_width - 1, 0), (0, 0)))
    out = bias + up[:, 0:s] * w[0]
    for j in range(1, k_width):
        out = out + up[:, j:j + s] * w[j]
    return out

def moba_attention(q, k, v):
    b, h, s, dh = q.shape
    nb = -(-s // MOBA_BLOCK)
    pad = nb * MOBA_BLOCK - s
    kb = jnp.pad(k, ((0, 0), (0, 0), (0, pad), (0, 0))).reshape(b, h, nb, MOBA_BLOCK, dh)
    vb = jnp.pad(v, ((0, 0), (0, 0), (0, pad), (0, 0))).reshape(b, h, nb, MOBA_BLOCK, dh)
    k_mean = jnp.mean(kb, axis=3)
    n_sel = min(MOBA_TOPK, nb - 1)
    scale = dh ** -0.5
    blk_ids = jnp.arange(nb, dtype=jnp.int32)
    key_off = jnp.arange(MOBA_BLOCK, dtype=jnp.int32)
    gather_blocks = jax.vmap(jax.vmap(lambda blocks, idx: blocks[idx]))
    nq = s // Q_CHUNK
    q_chunks = q.reshape(b, h, nq, Q_CHUNK, dh).transpose(2, 0, 1, 3, 4)

    def chunk_attend(args):
        qc, c = args
        q_pos = c * Q_CHUNK + jnp.arange(Q_CHUNK, dtype=jnp.int32)
        own = (c * Q_CHUNK) // MOBA_BLOCK
        k_own = lax.dynamic_index_in_dim(kb, own, axis=2, keepdims=False)
        v_own = lax.dynamic_index_in_dim(vb, own, axis=2, keepdims=False)
        k_pos = own * MOBA_BLOCK + key_off
        s_own = jnp.einsum('bhqd,bhkd->bhqk', qc, k_own).astype(jnp.float32) * scale
        s_own = jnp.where(k_pos[None, :] <= q_pos[:, None], s_own, -jnp.inf)
        if n_sel == 0:
            p_own = jax.nn.softmax(s_own, axis=-1).astype(v.dtype)
            return jnp.einsum('bhqk,bhkd->bhqd', p_own, v_own)
        gate = jnp.einsum('bhqd,bhnd->bhqn', qc, k_mean).astype(jnp.float32)
        gate = jnp.where(blk_ids < own, gate, -jnp.inf)
        _, sel = lax.top_k(gate, n_sel)
        valid = sel < own
        k_sel = gather_blocks(kb, sel)
        v_sel = gather_blocks(vb, sel)
        s_sel = jnp.einsum('bhqd,bhqjkd->bhqjk', qc, k_sel).astype(jnp.float32) * scale
        s_sel = jnp.where(valid[..., None], s_sel, -jnp.inf).reshape(b, h, Q_CHUNK, n_sel * MOBA_BLOCK)
        p = jax.nn.softmax(jnp.concatenate([s_sel, s_own], axis=-1), axis=-1).astype(v.dtype)
        p_sel = p[..., :n_sel * MOBA_BLOCK].reshape(b, h, Q_CHUNK, n_sel, MOBA_BLOCK)
        p_own = p[..., n_sel * MOBA_BLOCK:]
        return (jnp.einsum('bhqjk,bhqjkd->bhqd', p_sel, v_sel)
                + jnp.einsum('bhqk,bhkd->bhqd', p_own, v_own))

    out = lax.map(chunk_attend, (q_chunks, jnp.arange(nq, dtype=jnp.int32)))
    return out.transpose(1, 2, 0, 3, 4).reshape(b, h, s, dh)

def ssd_chunked_scan(xs, dt, a, bm, cm):
    b, s, g, r, p = xs.shape
    n = bm.shape[-1]
    nc = s // SSD_CHUNK
    L = SSD_CHUNK
    log_a = (dt * a).reshape(b, nc, L, g, r).transpose(0, 3, 4, 1, 2)
    xdt = (xs * dt[..., None]).reshape(b, nc, L, g, r, p)
    bc = bm.reshape(b, nc, L, g, n)
    cc = cm.reshape(b, nc, L, g, n)
    a_cum = jnp.cumsum(log_a, axis=-1)
    tril = jnp.tril(jnp.ones((L, L), dtype=bool))
    seg = a_cum[..., :, None] - a_cum[..., None, :]
    decay = jnp.where(tril, jnp.exp(jnp.where(tril, seg, 0.0)), 0.0)
    cb = jnp.einsum('bclgn,bcsgn->bgcls', cc, bc)
    y_diag = jnp.einsum('bgrcls,bcsgrp->bclgrp', cb[:, :, None] * decay, xdt)
    decay_to_end = jnp.exp(a_cum[..., -1:] - a_cum)
    chunk_states = jnp.einsum('bclgn,bgrcl,bclgrp->cbgrpn', bc, decay_to_end, xdt)
    chunk_decay = jnp.exp(a_cum[..., -1]).transpose(3, 0, 1, 2)

    def carry_state(h, inputs):
        st, dec = inputs
        return h * dec[..., None, None] + st, h

    h0 = jnp.zeros((b, g, r, p, n), xs.dtype)
    _, h_in = lax.scan(carry_state, h0, (chunk_states, chunk_decay))
    y_off = jnp.einsum('bclgn,cbgrpn,bgrcl->bclgrp', cc, h_in, jnp.exp(a_cum))
    return (y_diag + y_off).reshape(b, s, g, r, p)

def hybrid_layer(x, norm1_w, w_in, q_norm_w, k_norm_w, ssm_conv_w, ssm_conv_b, dt_bias, a_log,
                 d_skip, ssm_norm_w, w_out, norm2_w, w_up, ffn_conv_w, ffn_conv_b, w_down):
    b, s, _ = x.shape
    h = rms_norm(x, norm1_w)
    proj = h @ w_in
    q, k, v, z, xbc, dt_raw = jnp.split(proj, SPLIT_POINTS, axis=-1)

    q = rms_norm(q.reshape(b, s, ATTN_HEADS, ATTN_HEAD_DIM), q_norm_w).transpose(0, 2, 1, 3)
    k = rms_norm(k.reshape(b, s, ATTN_HEADS, ATTN_HEAD_DIM), k_norm_w).transpose(0, 2, 1, 3)
    v = v.reshape(b, s, ATTN_HEADS, ATTN_HEAD_DIM).transpose(0, 2, 1, 3)
    attn = moba_attention(q, k, v).transpose(0, 2, 1, 3).reshape(b, s, ATTN_WIDTH)

    xbc = jax.nn.silu(causal_dwconv(xbc, ssm_conv_w, ssm_conv_b))
    xs, bm, cm = jnp.split(xbc, (SSM_WIDTH, SSM_WIDTH + SSM_GROUPS * SSM_STATE), axis=-1)
    xs = xs.astype(jnp.float32).reshape(b, s, SSM_GROUPS, SSM_HEADS_PER_GROUP, SSM_HEAD_DIM)
    bm = bm.astype(jnp.float32).reshape(b, s, SSM_GROUPS, SSM_STATE)
    cm = cm.astype(jnp.float32).reshape(b, s, SSM_GROUPS, SSM_STATE)
    dt = jax.nn.softplus(dt_raw.astype(jnp.float32) + dt_bias.astype(jnp.float32))
    dt = dt.reshape(b, s, SSM_GROUPS, SSM_HEADS_PER_GROUP)
    a = -jnp.exp(a_log.astype(jnp.float32)).reshape(SSM_GROUPS, SSM_HEADS_PER_GROUP)
    y = ssd_chunked_scan(xs, dt, a, bm, cm)
    y = y + d_skip.astype(jnp.float32).reshape(SSM_GROUPS, SSM_HEADS_PER_GROUP)[:, :, None] * xs
    gate = jax.nn.silu(z.astype(jnp.float32)).reshape(b, s, SSM_GROUPS, SSM_HEADS_PER_GROUP * SSM_HEAD_DIM)
    y = y.reshape(b, s, SSM_GROUPS, SSM_HEADS_PER_GROUP * SSM_HEAD_DIM) * gate
    y = rms_norm(y, ssm_norm_w.reshape(SSM_GROUPS, SSM_HEADS_PER_GROUP * SSM_HEAD_DIM))
    ssm = y.reshape(b, s, SSM_WIDTH).astype(x.dtype)

    x = x + jnp.concatenate([attn, ssm], axis=-1) @ w_out

    h = rms_norm(x, norm2_w)
    u = causal_dwconv(h @ w_up, ffn_conv_w, ffn_conv_b)
    u_gate, u_val = jnp.split(u, 2, axis=-1)
    return x + (jax.nn.silu(u_gate) * u_val) @ w_down

def second_inputs(seed: int = 0) -> dict:
    key = jax.random.key(seed)
    ks = jax.random.split(key, 17)

    def nrm(k, shape, scale):
        return jax.random.normal(k, shape, jnp.float32) * scale

    x = nrm(ks[0], (BATCH, SEQ, D_MODEL), 1.0)
    norm1_w = 1.0 + nrm(ks[1], (DEPTH, D_MODEL), 0.02)
    w_in = nrm(ks[2], (DEPTH, D_MODEL, IN_COLS), D_MODEL ** -0.5)
    q_norm_w = 1.0 + nrm(ks[3], (DEPTH, ATTN_HEAD_DIM), 0.02)
    k_norm_w = 1.0 + nrm(ks[4], (DEPTH, ATTN_HEAD_DIM), 0.02)
    ssm_conv_w = nrm(ks[5], (DEPTH, SSM_CONV, XBC_WIDTH), SSM_CONV ** -0.5)
    ssm_conv_b = nrm(ks[6], (DEPTH, XBC_WIDTH), 0.02)
    dt0 = jnp.exp(jax.random.uniform(ks[7], (DEPTH, SSM_HEADS), jnp.float32,
                                     minval=math.log(1e-3), maxval=math.log(1e-1)))
    dt_bias = dt0 + jnp.log(-jnp.expm1(-dt0))
    a_log = jnp.log(jax.random.uniform(ks[8], (DEPTH, SSM_HEADS), jnp.float32, minval=1.0, maxval=16.0))
    d_skip = 1.0 + nrm(ks[9], (DEPTH, SSM_HEADS), 0.1)
    ssm_norm_w = 1.0 + nrm(ks[10], (DEPTH, SSM_WIDTH), 0.02)
    w_out = nrm(ks[11], (DEPTH, MIX_WIDTH_2, D_MODEL), MIX_WIDTH_2 ** -0.5)
    norm2_w = 1.0 + nrm(ks[12], (DEPTH, D_MODEL), 0.02)
    w_up = nrm(ks[13], (DEPTH, D_MODEL, 2 * D_FF), D_MODEL ** -0.5)
    ffn_conv_w = nrm(ks[14], (DEPTH, FFN_CONV, 2 * D_FF), FFN_CONV ** -0.5)
    ffn_conv_b = nrm(ks[15], (DEPTH, 2 * D_FF), 0.02)
    w_down = nrm(ks[16], (DEPTH, D_FF, D_MODEL), D_FF ** -0.5)
    return {"x": x, "norm1_w": norm1_w, "w_in": w_in, "q_norm_w": q_norm_w, "k_norm_w": k_norm_w,
            "ssm_conv_w": ssm_conv_w, "ssm_conv_b": ssm_conv_b, "dt_bias": dt_bias, "a_log": a_log,
            "d_skip": d_skip, "ssm_norm_w": ssm_norm_w, "w_out": w_out, "norm2_w": norm2_w,
            "w_up": w_up, "ffn_conv_w": ffn_conv_w, "ffn_conv_b": ffn_conv_b, "w_down": w_down}

def second_block(x, norm1_w, w_in, q_norm_w, k_norm_w, ssm_conv_w, ssm_conv_b, dt_bias, a_log,
              d_skip, ssm_norm_w, w_out, norm2_w, w_up, ffn_conv_w, ffn_conv_b, w_down):
    for i in range(DEPTH):
        x = hybrid_layer(x, norm1_w[i], w_in[i], q_norm_w[i], k_norm_w[i], ssm_conv_w[i],
                         ssm_conv_b[i], dt_bias[i], a_log[i], d_skip[i], ssm_norm_w[i], w_out[i],
                         norm2_w[i], w_up[i], ffn_conv_w[i], ffn_conv_b[i], w_down[i])
    return x


def setup_inputs(seed=0):
    out = dict(first_inputs(seed))
    for name, value in second_inputs(seed + 1).items():
        if name != "x":
            out[name + "_2"] = value
    return out


def reference(
    x, attn_norm, w_in, cmp_pos_k, cmp_w1_k, cmp_w2_k, cmp_pos_v, cmp_w1_v, cmp_w2_v, sinks,
    w_out, ffn_norm, peer_wq, peer_subkeys, peer_u, peer_v, rel_bias, final_norm, norm1_w_2,
    w_in_2, q_norm_w_2, k_norm_w_2, ssm_conv_w_2, ssm_conv_b_2, dt_bias_2, a_log_2, d_skip_2,
    ssm_norm_w_2, w_out_2, norm2_w_2, w_up_2, ffn_conv_w_2, ffn_conv_b_2, w_down_2,
):
    x = first_block(
        x, attn_norm, w_in, cmp_pos_k, cmp_w1_k, cmp_w2_k, cmp_pos_v, cmp_w1_v, cmp_w2_v, sinks,
        w_out, ffn_norm, peer_wq, peer_subkeys, peer_u, peer_v, rel_bias, final_norm,
    )
    return second_block(
        x, norm1_w_2, w_in_2, q_norm_w_2, k_norm_w_2, ssm_conv_w_2, ssm_conv_b_2, dt_bias_2,
        a_log_2, d_skip_2, ssm_norm_w_2, w_out_2, norm2_w_2, w_up_2, ffn_conv_w_2, ffn_conv_b_2,
        w_down_2,
    )


_drawn_inputs = setup_inputs


def setup_inputs(seed=0):
    import zlib

    import numpy as np

    out = dict(_drawn_inputs(seed))
    spreads = {}
    factors = {'attn_norm': 5.153,
     'cmp_pos_k': 8.0,
     'sinks': 4.802,
     'ffn_norm': 6.681,
     'norm1_w_2': 2.882,
     'q_norm_w_2': 8.0,
     'k_norm_w_2': 8.0,
     'ssm_conv_b_2': 3.158,
     'ssm_norm_w_2': 4.712,
     'norm2_w_2': 4.253,
     'ffn_conv_b_2': 4.591,
     'd_skip_2': 29.767}
    for name, (base, spread) in spreads.items():
        noise = np.random.default_rng([zlib.crc32(name.encode()), seed]).standard_normal(out[name].shape)
        drawn = base * np.exp(spread * noise) if base else spread * noise
        out[name] = jnp.asarray(drawn.astype(out[name].dtype))
    for name, factor in factors.items():
        out[name] = (out[name] * factor).astype(out[name].dtype)
    return out
```

```python
import math
from contextlib import ExitStack

import numpy as np

import concourse.bass as bass
from concourse import mybir

P = 128
T = 256
TT = T // P
D = 2048
KT = D // P
TILE = 2048
WEIGHT_SLOTS = 4
N = 512
EPS = 1e-6
NEG = -1e30
LOWEST = -3.0e38

HEADS = 16
DH = 64
GROUP_HEADS = 8
CMP_LEN, CMP_STRIDE, CMP_HIDDEN = 32, 16, 128
N_CMP = T // CMP_STRIDE - 1
CMP_PAD = 16
BUCKETS, EXACT, MAX_DIST = 32, 16, 2048
SWA_WINDOW = 128
CMP_FIRST = -(CMP_PAD * CMP_STRIDE - CMP_STRIDE + CMP_LEN - 1) - 1
GATES = 3 * HEADS
PEER_HEADS, PEER_KEYS, TOPK = 8, 128, 16
EXPERT_TILES = PEER_KEYS

HEADS2, DH2 = 8, 128
SSM_HEADS, SSM_DH, SSM_GROUPS = 16, 64, 2
SSM_W = SSM_HEADS * SSM_DH
XBC_TILES = 12
SSM_TAPS = 4
FF_TILES = 44
FF_GROUPS = 22

UNITS = 3 * HEADS

STREAM = [("w_in_t", 24, 6), ("w_out_t", 16, 4), ("peer_wq_t", 16, 4), ("experts_t", 256, 0),
          ("w_in_2_t", 44, 11), ("w_out_2_t", 16, 4), ("w_up_2_t", 88, 22), ("w_down_2_t", 44, 4)]

F32 = mybir.dt.float32
U32 = mybir.dt.uint32
ALU = mybir.AluOpType
ACT = mybir.ActivationFunctionType
AX = mybir.AxisListType



def build(nc, ins, out):
    ctx = ExitStack()
    with ctx:
        def sb(name, shape, dt=F32):
            return ctx.enter_context(nc.sbuf_tensor(name, shape, dt))

        def sem(name):
            return ctx.enter_context(nc.semaphore(name))

        slot = [sb(f"weight_slot{s}", [P, TILE]) for s in range(WEIGHT_SLOTS)]
        resid = sb("resid", [P, TT, D])
        act_t = sb("act_t", [P, KT, T])
        big = sb("big", [P, EXPERT_TILES * T])
        bank = ctx.enter_context(nc.psum_tensor("bank", [P, 8, N], F32))

        ident = sb("ident", [P, P])
        ones = sb("ones", [P, P])
        iota = sb("iota", [P, P])
        triu = sb("triu", [P, P])
        low_mask = sb("low_mask", [P, P])
        gains = sb("gains", [P, 7, KT])
        conv1 = sb("conv1", [P, XBC_TILES, SSM_TAPS + 1])
        conv2 = sb("conv2", [P, FF_GROUPS, 16])
        rows = sb("rows", [P, 4, SSM_HEADS])
        stat = sb("stat", [P, 64])
        picked_t = sb("picked_t", [P, 3, T])
        scratch = sb("scratch", [P, 1536])

        class Region:

            def __init__(self, at=0):
                self.at = at

            def take(self, floats, pattern=None, dt=F32, **sizes):
                ap = big[:, self.at:self.at + floats]
                self.at += floats
                assert self.at <= EXPERT_TILES * T, self.at
                if dt is not F32:
                    ap = ap.bitcast(dt)
                return ap.rearrange(pattern, **sizes) if pattern else ap

        r1 = Region()
        o1 = r1.take(TT * D, "p (i d) -> p i d", i=TT)
        q1 = r1.take(16 * T, "p (c t) -> p c t", c=16)
        k1 = r1.take(5 * T, "p (c t) -> p c t", c=5)
        v1 = r1.take(TT * 384, "p (i c) -> p i c", i=TT)
        gate1 = r1.take(TT * GATES, "p (i h b) -> p i h b", i=TT, b=3)
        bias1 = r1.take(2 * HEADS * T, "p (h y) -> p h y", y=T)
        cbias = r1.take(TT * HEADS * CMP_PAD, "p (i h c) -> p i h c", i=TT, c=CMP_PAD)
        cmp_w1_at = r1.at
        cmp_w1 = r1.take(2 * CMP_LEN * P, "p (v l n) -> p v l n", v=2, n=P)
        cmp_w2 = r1.take(2 * DH, "p (v n) -> p v n", v=2)
        cmp_pos = r1.take(2 * CMP_LEN, "p (v l) -> p v l", v=2)
        cmp_in = r1.take(2 * CMP_LEN * CMP_PAD, "p (v l c) -> p v l c", v=2, c=CMP_PAD)
        cmp_hid = r1.take(2 * 2 * CMP_PAD, "p (g v c) -> p g v c", g=2, v=2)
        cmp_k = r1.take(CMP_PAD)
        block_of = r1.take(GROUP_HEADS)
        valid_c = r1.take(TT * CMP_PAD, "p (i c) -> p i c", i=TT)
        gate_w = r1.take(KT * GATES, "p (k n) -> p k n", k=KT)
        buckets = r1.take(P)

        def attention_buffers(region):
            return (region.take(2 * 386, "p (b n) -> p b n", b=2), region.take(2 * 384, "p (b n) -> p b n", b=2),
                    region.take(N), region.take(2 * UNITS), region.take(2 * UNITS))

        r1_tables = Region(r1.at)
        onehot_rev = r1_tables.take(3 * P)
        onehot_cmp = r1_tables.take(T - CMP_FIRST)
        by_distance = r1_tables.take(3 * P)
        logits1, probs_t1, share1, negmax1, expsum1 = attention_buffers(r1)
        r1_cmp = Region(cmp_w1_at)
        cmp_hid8 = [r1_cmp.take(GROUP_HEADS * CMP_PAD, "p (h c) -> p h c", c=CMP_PAD) for _ in range(2)]
        cmp_v = r1_cmp.take(2 * N, "p (g n) -> p g n", g=2)
        cmp_logits = r1_cmp.take(2 * TT * GROUP_HEADS * CMP_PAD, "p (g i h c) -> p g i h c", g=2, i=TT, c=CMP_PAD)
        cmp_probs_t = r1_cmp.take(4 * P, "p (n q) -> p n q", q=P)
        cmp_stat = r1_cmp.take(4 * 32, "p (k n) -> p k n", k=4)

        r2 = Region()
        peer_q = r2.take(16 * T, "p (c t) -> p c t", c=16)
        subkeys = r2.take(2 * P, "p (s n) -> p s n", s=2)
        scores = r2.take(TT * 16 * P, "p (r n) -> p r n", n=P)
        scores_left = r2.take(TT * 16 * P, "p (r n) -> p r n", n=P)
        top = r2.take(TT * 16 * TOPK, "p (r k) -> p r k", k=TOPK)
        top_at = r2.take(TT * 16 * TOPK, "p (r k) -> p r k", dt=U32, k=TOPK)
        top_key = r2.take(TT * 16 * TOPK, "p (r k) -> p r k", k=TOPK)
        pairs = r2.take(TT * PEER_HEADS * TOPK * TOPK, "p (r n) -> p r n", n=TOPK * TOPK)
        pairs_left = r2.take(TT * PEER_HEADS * TOPK * TOPK, "p (r n) -> p r n", n=TOPK * TOPK)
        best = r2.take(TT * PEER_HEADS * TOPK, "p (r k) -> p r k", k=TOPK)
        best_at = r2.take(TT * PEER_HEADS * TOPK, "p (r k) -> p r k", dt=U32, k=TOPK)
        part_at = r2.take(2 * TT * PEER_HEADS * TOPK, "p (s r) -> p s r", dt=U32, s=2)
        part = r2.take(2 * TT * PEER_HEADS * TOPK, "p (s r) -> p s r", s=2)
        is_part = r2.take(TT * PEER_HEADS * TOPK * TOPK, "p (r a) -> p r a", a=TOPK)
        picked = r2.take(3 * TT * P, "p (s i k) -> p s i k", s=3, k=P)
        best_sum = r2.take(2 * TT * PEER_HEADS, "p (s r) -> p s r", s=2)

        gates = big[:, :].rearrange("p (e t) -> p e t", t=T)
        onehots = scratch[:, 0:2 * 2 * P].rearrange("p (b s n) -> p b s n", b=2, s=2)
        hidden = scratch[:, 0:2 * T].rearrange("p (b t) -> p b t", b=2)
        weighed = scratch[:, 2 * T:4 * T].rearrange("p (b t) -> p b t", b=2)
        final_gain = big[:, 0:D]

        r4 = Region(D)
        qkvz_at = r4.at
        qk2 = r4.take(TT * D, "p (i c) -> p i c", i=TT)
        qk_t = r4.take(16 * T, "p (c t) -> p c t", c=16)
        vz2 = r4.take(TT * D, "p (i c) -> p i c", i=TT)
        qkvz_half = [qk2, vz2]
        xbc_raw_at = r4.at
        xbc_raw = r4.take(XBC_TILES * T, "p (c t) -> p c t", c=XBC_TILES)
        xbc = r4.take(XBC_TILES * T, "p (c t) -> p c t", c=XBC_TILES)
        o2 = r4.take(TT * D, "p (i d) -> p i d", i=TT)
        dt_w = r4.take(KT * SSM_HEADS, "p (k n) -> p k n", k=KT)
        causal = r4.take(T)
        logits2, probs_t2, share2, negmax2, expsum2 = attention_buffers(r4)
        dt_ = r4.take(4 * TT * SSM_HEADS, "p (k n) -> p k n", k=4)
        dt_tmp = r4.take(3 * TT * SSM_HEADS, "p (k n) -> p k n", k=3)
        x_tok = r4.take(TT * SSM_W, "p (i c) -> p i c", i=TT)
        la_triu = r4.take(SSM_HEADS * P)
        r4_scan = Region(xbc_raw_at)
        x_dt = r4_scan.take(TT * SSM_W, "p (i c) -> p i c", i=TT)
        cb = r4_scan.take(SSM_GROUPS * 3 * P, "p (g n) -> p g n", g=SSM_GROUPS)
        decay = Region(qkvz_at).take(3 * SSM_HEADS * P, "p (b h l) -> p b h l", b=3, h=SSM_HEADS)
        squares = big[:, 0:D]
        norm2_rows, norm3_rows, norm4_rows = o1, o2, o2

        r5 = Region()
        ff_hidden = r5.take(FF_TILES * T, "p (c t) -> p c t", c=FF_TILES)
        taps = r5.take(2 * 4 * T, "p (b q t) -> p b q t", b=2, q=4)
        TURN0 = [8 * n for n in range(8)]
        BIAS_ROW = 2 * HEADS * 3 * P
        bias_dram = nc.dram_tensor("bias_by_distance", [BIAS_ROW], F32)
        bias_copies = nc.dram_tensor("bias_by_distance_copies", [P, BIAS_ROW], F32)

        CONSTS = [(ident, "c_ident"), (gains, "gains"), (ones, "c_ones"), (iota, "c_iota"), (triu, "c_triu"),
                  (low_mask, "c_low_mask"), (conv1, "conv1"), (conv2, "conv2"), (rows, "rows")]
        STAGE1 = [(buckets[0:BUCKETS + 2, 0:2 * HEADS], "bias_rows"), (onehot_rev[0:BUCKETS + 2, :], "c_onehot_rev"),
                  (onehot_cmp[0:BUCKETS + 2, :], "c_onehot_cmp"), (gate_w, "gate_w"), (cmp_w1, "cmp_w1"),
                  (cmp_w2, "cmp_w2"), (cmp_pos, "cmp_pos"), (block_of, "c_block_of"), (valid_c, "c_valid")]
        STAGE4 = [(dt_w, "dt_w"), (causal, "c_causal")]
        CONST_DMAS, STAGE1_DMAS, STAGE4_DMAS = 16 * len(CONSTS), 16 * len(STAGE1), 16 * len(STAGE4)

        x_landed = sem("x_landed")
        consts_landed = sem("consts_landed")
        stage1_landed = sem("stage1_landed")
        bias_stored = sem("bias_stored")
        bias_spread = sem("bias_spread")
        bias_landed = sem("bias_landed")
        subkeys_landed = sem("subkeys_landed")
        final_gain_landed = sem("final_gain_landed")
        stage4_landed = sem("stage4_landed")
        out_stored = sem("out_stored")
        tile_landed = [sem(f"tile_landed{s}") for s in range(WEIGHT_SLOTS)]
        tile_used = [sem(f"tile_used{s}") for s in range(WEIGHT_SLOTS)]
        pair_copied = [sem(f"pair_copied{b}") for b in range(2)]
        squared = sem("squared")
        scaled = sem("scaled")
        turned = sem("turned")
        turned_copied = sem("turned_copied")
        tables_done = sem("tables_done")
        tables_copied = sem("tables_copied")
        small_done = sem("small_done")
        small_copied = sem("small_copied")
        cmp_pe = sem("cmp_pe")
        cmp_dve = sem("cmp_dve")
        cmp_act = sem("cmp_act")
        cmp_shifted = sem("cmp_shifted")
        scores_done = sem("scores_done")
        logits_written = sem("logits_written")
        logits_ready = sem("logits_ready")
        probs_ready = sem("probs_ready")
        probs_turned = sem("probs_turned")
        probs_copied = sem("probs_copied")
        mixed = sem("mixed")
        set_copied = sem("set_copied")
        subkey_scores_done = sem("subkey_scores_done")
        subkey_scores_copied = sem("subkey_scores_copied")
        best_ready = sem("best_ready")
        best_exp = sem("best_exp")
        picked_ready = sem("picked_ready")
        picked_turned = sem("picked_turned")
        picked_copied = sem("picked_copied")
        onehot1_ready = sem("onehot1_ready")
        onehot2_ready = sem("onehot2_ready")
        gates_done = [sem(f"gates_done{b}") for b in range(2)]
        gates_copied = [sem(f"gates_copied{b}") for b in range(2)]
        gelu_done = [sem(f"gelu_done{e}") for e in range(2)]
        weighed_ready = [sem(f"weighed_ready{e}") for e in range(2)]
        shares_done = sem("shares_done")
        share_added = [sem(f"share_added{b}") for b in range(4)]
        normed = sem("normed")
        scan_pe = sem("scan_pe")
        scan_dve = sem("scan_dve")
        scan_act = sem("scan_act")
        tap_done = [sem(f"tap_done{b}") for b in range(2)]
        conv_done = [sem(f"conv_done{b}") for b in range(2)]
        silu_done = [sem(f"silu_done{b}") for b in range(2)]
        hidden_ready = [sem(f"hidden_ready{b}") for b in range(2)]
        conv_step = [sem(f"conv_step{b}") for b in range(2)]
        root_wanted = sem("root_wanted")
        root_done = sem("root_done")
        dve_step = sem("dve_step")
        act_step = sem("act_step")

        PRIMED = 1

        def prime(eng, semaphores):
            for semaphore in semaphores:
                eng.sem_inc(semaphore, PRIMED)

        ROOTS = [0, 1, 2, 3, "heads 0", "heads 1", "scan", 5]
        loads, uses, groups = {}, {}, {}
        n_loads, n_uses, n_groups = 0, [0] * WEIGHT_SLOTS, 0
        for name, tiles, n in STREAM:
            loads[name], uses[name], groups[name] = n_loads, list(n_uses), n_groups
            n_loads += tiles // WEIGHT_SLOTS
            for s in range(WEIGHT_SLOTS):
                n_uses[s] += 0 if name == "experts_t" and s >= 2 else tiles // WEIGHT_SLOTS
            n_groups += n

        def pair(name, g):
            return (groups[name] + g) % 2, (groups[name] + g) // 2

        EXPERT_STEPS = EXPERT_TILES // 2
        DOWN_CHUNKS = FF_TILES // 4
        DOWN_USES = [3, 3, 3, 2]

        def wait_pairs(eng, name):
            n = next(n for which, _, n in STREAM if which == name)
            for g in (n - 2, n - 1):
                b, used = pair(name, g)
                eng.wait_ge(pair_copied[b], 2 * (used + 1) + PRIMED)

        def row(ap, n):
            return ap.unsqueeze(len(ap.shape)).to_broadcast([*ap.shape, n])

        def copies(ap, n, at=1):
            shape = list(ap.shape)
            return ap.unsqueeze(at).to_broadcast([*shape[:at], n, *shape[at:]])

        class Steps:

            def __init__(self, eng, semaphore):
                self.eng, self.semaphore, self.n = eng, semaphore, 0

            def note(self, instruction):
                instruction.then_inc(self.semaphore, 1)
                self.n += 1

            def settle(self):
                self.eng.wait_ge(self.semaphore, self.n)

            def link(self, instruction):
                self.note(instruction)
                self.settle()

        units1 = []
        for branch in range(3):
            for h in range(HEADS):
                g, c = h // GROUP_HEADS, h % GROUP_HEADS
                part_of = slice(DH * g, DH * g + DH)
                units1.append(dict(
                    q=q1[part_of, c + (8 if branch == 2 else 0), :], k=k1[part_of, branch, :],
                    v=[v1[:, i, P * branch + DH * g:P * branch + DH * g + DH] for i in range(TT)],
                    bias=bias1[:, h + (HEADS if branch == 2 else 0), :], scale=DH ** -0.5,
                    sink=rows[:, 0, h:h + 1] if branch == 2 else None, width=DH,
                    set=2 * branch + g, at=DH * c))
        units2 = [dict(q=qk_t[:, h, :], k=qk_t[:, HEADS2 + h, :],
                       v=[qkvz_half[1][:, i, DH2 * h:DH2 * h + DH2] for i in range(TT)],
                       bias=causal, scale=DH2 ** -0.5, sink=None, width=DH2, set=6 + h // 4, at=DH2 * (h % 4))
                  for h in range(HEADS2)]
        attention1 = dict(units=units1, first=0, logits=logits1, probs_t=probs_t1, negmax=negmax1, expsum=expsum1)
        attention2 = dict(units=units2, first=UNITS, logits=logits2, probs_t=probs_t2, negmax=negmax2, expsum=expsum2)

        block = ctx.enter_context(nc.Block())

        @block.sync
        def _(sp):
            for i in range(TT):
                sp.dma_start(resid[:, i, :], ins["x"][0, i * P:(i + 1) * P, :]).then_inc(x_landed, 16)
            for name, tiles, _ in STREAM[:3]:
                with sp.Fori(0, tiles // WEIGHT_SLOTS) as n:
                    for s in range(WEIGHT_SLOTS):
                        sp.wait_ge(tile_used[s], n + uses[name][s] + PRIMED)
                        sp.dma_start(slot[s][:, :], ins[name][bass.ds(n * WEIGHT_SLOTS + s, 1)].rearrange(
                            "a p n -> p (a n)")).then_inc(tile_landed[s], 16)
            for s in (2, 3):
                sp.wait_ge(tile_used[s], uses["experts_t"][s] + PRIMED)
            with sp.Fori(0, EXPERT_STEPS) as n:
                for s in range(WEIGHT_SLOTS):
                    if s < 2:
                        sp.wait_ge(tile_used[s], n + uses["experts_t"][s] + PRIMED)
                    else:
                        sp.wait_ge(shares_done, 8 * n + PRIMED)
                    sp.dma_start(slot[s][:, :], ins["experts_t"][bass.ds(n * WEIGHT_SLOTS + s, 1)].rearrange(
                        "a p n -> p (a n)")).then_inc(tile_landed[s], 16)
            sp.wait_ge(shares_done, 8 * EXPERT_STEPS + PRIMED)
            for name, tiles, _ in STREAM[4:7]:
                with sp.Fori(0, tiles // WEIGHT_SLOTS) as n:
                    for s in range(WEIGHT_SLOTS):
                        sp.wait_ge(tile_used[s], n + uses[name][s] + PRIMED)
                        sp.dma_start(slot[s][:, :], ins[name][bass.ds(n * WEIGHT_SLOTS + s, 1)].rearrange(
                            "a p n -> p (a n)")).then_inc(tile_landed[s], 16)
            name = "w_down_2_t"
            with sp.Fori(0, 4) as g:
                for c in range(DOWN_CHUNKS):
                    s = c % WEIGHT_SLOTS
                    sp.wait_ge(tile_used[s], g * DOWN_USES[s] + uses[name][s] + c // WEIGHT_SLOTS + PRIMED)
                    sp.dma_start(slot[s][:, :], ins[name][bass.ds(g * DOWN_CHUNKS + c, 1)].rearrange(
                        "a p n -> p (a n)")).then_inc(tile_landed[s], 16)
            for g in range(4):
                b, used = pair(name, g)
                sp.wait_ge(pair_copied[b], 2 * (used + 1) + PRIMED)
                sp.dma_start(out[0].rearrange("(i p) d -> p i d", p=P)[:, :, N * g:N * (g + 1)],
                             resid[:, :, N * g:N * (g + 1)]).then_inc(out_stored, 16)
            sp.wait_ge(out_stored, 16 * 4)

        @block.tensor
        def _(pe):
            prime(pe, [*tile_used, *gates_done, shares_done])

            def mm(out_, lhs_t, rhs, start=True, stop=True):
                return pe.matmul(out_, lhs_t, rhs, start=start, stop=stop, skip_group_check=True)

            def product(name, g, i=0, chunks=4, lhs=act_t, stationary_weights=4):
                b, used = pair(name, g)
                per_group = [1] * 4 if chunks == 4 else DOWN_USES
                pe.wait_ge(pair_copied[b], i * 2 + 2 * used + PRIMED)
                for c in range(chunks):
                    s = c % WEIGHT_SLOTS
                    w = slot[s][:, :].rearrange("p (k n) -> p k n", k=4)
                    load = loads[name] + g * per_group[s] + c // WEIGHT_SLOTS + 1
                    pe.wait_ge(tile_landed[s], i * (32 * per_group[s]) + 16 * load)
                    for k in range(4):
                        kt, first, last = 4 * c + k, c == 0 and k == 0, c == chunks - 1 and k == 3
                        if stationary_weights:
                            for n in range(stationary_weights):
                                m = mm(bank[:, 2 * b + n // 2, T * (n % 2):T * (n % 2) + T], w[:, k, P * n:P * n + P],
                                       lhs[:, kt, :], start=first and n % 2 == 0, stop=last)
                        else:
                            for t in range(TT):
                                m = mm(bank[:, 2 * b + t, :], lhs[:, kt, P * t:P * t + P], w[:, k, :],
                                       start=first, stop=last)
                    m.then_inc(tile_used[s], 1)

            def product_loop(name, steps, **how):
                with pe.Fori(0, steps) as i:
                    for j in range(2):
                        product(name, j, i=i, **how)

            def turn(n, src):
                for b in range(8):
                    i, quarter = b // 4, b % 4
                    if b % 4 == 0:
                        pe.wait_ge(scaled, TT * n + i + 1)
                    if TURN0[n] + b >= 4:
                        pe.wait_ge(turned_copied, TURN0[n] + b - 3)
                    for j in range(4):
                        c = 4 * quarter + j
                        m = pe.transpose(bank[:, 4 + b % 4, P * j:P * j + P], src[:, i, P * c:P * c + P], ident[:, :])
                    m.then_inc(turned, 1)

            def attention(a):
                units, first = a["units"], a["first"]

                def scores(n):
                    u, b = units[n], (first + n) % 2
                    if first + n >= 2:
                        pe.wait_ge(logits_ready, 2 * (first + n - 1))
                    mm(bank[:, b, 0:T], u["q"][:, P:T], u["k"][:, 0:T])
                    mm(bank[:, b, T:T + P], u["q"][:, 0:P], u["k"][:, 0:P]).then_inc(scores_done, 1)

                def turn_probs(n):
                    b = (first + n) % 2
                    pe.wait_ge(probs_ready, 2 * (first + n + 1))
                    if first + n >= 2:
                        pe.wait_ge(probs_copied, first + n - 1)
                    for k, at in enumerate((0, P, T + 1)):
                        m = pe.transpose(bank[:, 2 + b, P * k:P * k + P], a["logits"][:, b, at:at + P], ident[:, :])
                    m.then_inc(probs_turned, 1)

                def mix(n):
                    u, b = units[n], (first + n) % 2
                    o, w, at = 4 + 2 * (u["set"] % 2), u["width"], u["at"]
                    pt = a["probs_t"][:, b, :]
                    pe.wait_ge(probs_copied, first + n + 1)
                    if at == 0 and u["set"] >= 2:
                        pe.wait_ge(set_copied, 2 * (u["set"] - 1))
                    mm(bank[:, o + 1, at:at + w], pt[:, 0:P], u["v"][0], stop=False)
                    mm(bank[:, o + 1, at:at + w], pt[:, P:T], u["v"][1], start=False)
                    mm(bank[:, o, at:at + w], pt[:, T:T + P], u["v"][0]).then_inc(mixed, 1)

                scores(0)
                for n in range(len(units) + 1):
                    if n + 1 < len(units):
                        scores(n + 1)
                    if n < len(units):
                        turn_probs(n)
                    if n >= 1:
                        mix(n - 1)

            pe.wait_ge(stage1_landed, STAGE1_DMAS)
            mm(bank[0:2 * HEADS, 0, 0:3 * P], buckets[0:BUCKETS + 2, 0:2 * HEADS], onehot_rev[0:BUCKETS + 2, :])
            for i in range(TT):
                for c in range(CMP_PAD):
                    at = P * i - CMP_STRIDE * c - CMP_LEN + 1 - CMP_FIRST
                    m = mm(bank[:, 1, HEADS * (CMP_PAD * i + c):HEADS * (CMP_PAD * i + c + 1)],
                           onehot_cmp[0:BUCKETS + 2, at:at + P], buckets[0:BUCKETS + 2, 0:HEADS])
            m.then_inc(tables_done, 1)

            pe.wait_ge(x_landed, 16 * TT)
            pe.wait_ge(consts_landed, CONST_DMAS)
            turn(0, o1)
            pe.wait_ge(turned_copied, TURN0[1])
            pe.wait_ge(tables_copied, 2)
            product_loop("w_in_t", 2)
            product("w_in_t", 4)
            b, used = pair("w_in_t", 5)
            pe.wait_ge(pair_copied[b], 2 * used + PRIMED)
            pe.wait_ge(turned_copied, TURN0[1])
            for c in range(4):
                w = slot[c][:, :].rearrange("p (k n) -> p k n", k=4)
                pe.wait_ge(tile_landed[c], 16 * (loads["w_in_t"] + 6))
                for k in range(4):
                    kt, first, last = 4 * c + k, c == 0 and k == 0, c == 3 and k == 3
                    mm(bank[:, 4, 0:T], w[:, k, 0:P], act_t[:, kt, :], start=first, stop=last)
                    for t in range(TT):
                        m = mm(bank[:, 2 * b + t, 0:3 * P], act_t[:, kt, P * t:P * t + P], w[:, k, P:N],
                               start=first, stop=last)
                m.then_inc(tile_used[c], 1)
            for t in range(TT):
                for kt in range(KT):
                    m = mm(bank[:, 5 + t, 0:GATES], act_t[:, kt, P * t:P * t + P], gate_w[:, kt, :],
                           start=kt == 0, stop=kt == KT - 1)
            m.then_inc(small_done, 1)

            pe.wait_ge(small_copied, 1)
            pe.wait_ge(cmp_dve, 2)
            for g in range(2):
                part_of = slice(DH * g, DH * g + DH)
                for v in range(2):
                    for l in range(CMP_LEN):
                        m = mm(bank[:, 6 + g, CMP_PAD * v:CMP_PAD * v + N_CMP], cmp_w1[part_of, v, l, :],
                               cmp_in[part_of, v, l, 0:N_CMP], start=l == 0, stop=l == CMP_LEN - 1)
            m.then_inc(cmp_pe, 1)
            pe.wait_ge(cmp_act, 1)
            for g in range(2):
                m = mm(bank[DH * g:DH * g + DH, 4, 0:CMP_PAD], cmp_w2[:, 0, :], cmp_hid[:, g, 0, :])
            m.then_inc(cmp_pe, 1)
            for g in range(2):
                pe.wait_ge(cmp_dve, 3 + g)
                m = mm(bank[:, 5, DH * g:DH * g + DH], cmp_hid8[g][:, :, :].rearrange("p h c -> p (h c)"), cmp_w2[:, 1, :])
            m.then_inc(cmp_pe, 1)
            pe.wait_ge(cmp_dve, 5)
            for g in range(2):
                part_of = slice(DH * g, DH * g + DH)
                for i in range(TT):
                    for h in range(GROUP_HEADS):
                        at = CMP_PAD * (GROUP_HEADS * i + h)
                        m = mm(bank[:, 6 + g, at:at + CMP_PAD], q1[part_of, h, P * i:P * i + P], cmp_k[part_of, :])
            m.then_inc(cmp_pe, 1)
            pe.wait_ge(cmp_dve, 6)
            for g in range(2):
                for i in range(TT):
                    m = pe.transpose(bank[:, 4, P * (2 * g + i):P * (2 * g + i) + P],
                                     cmp_logits[:, g, i, :, :].rearrange("p h c -> p (h c)"), ident[:, :])
            m.then_inc(cmp_pe, 1)
            pe.wait_ge(cmp_dve, 7)
            for g in range(2):
                for i in range(TT):
                    m = mm(bank[:, 2 * i + g, :], cmp_probs_t[:, 2 * g + i, :], cmp_v[:, g, :])
            m.then_inc(cmp_pe, 1)

            pe.wait_ge(cmp_dve, 8)
            attention(attention1)
            turn(1, o1)
            pe.wait_ge(turned_copied, TURN0[2])
            product_loop("w_out_t", 2, stationary_weights=0)

            turn(2, norm2_rows)
            pe.wait_ge(turned_copied, TURN0[3])
            product_loop("peer_wq_t", 2)
            pe.wait_ge(subkeys_landed, 16)
            wait_pairs(pe, "peer_wq_t")
            for n in range(8):
                if n >= 4:
                    pe.wait_ge(subkey_scores_copied, n - 3)
                for j in range(4):
                    r = 4 * n + j
                    i, c = r // 16, r % 16
                    m = mm(bank[:, 4 + n % 4, P * j:P * j + P], peer_q[:, c, P * i:P * i + P], subkeys[:, c % 2, :])
                m.then_inc(subkey_scores_done, 1)
            pe.wait_ge(picked_ready, 1)
            pe.wait_ge(subkey_scores_copied, 8)
            for s in range(3):
                for i in range(TT):
                    n = 2 * s + i
                    m = pe.transpose(bank[:, 4 + n // 4, P * (n % 4):P * (n % 4) + P], picked[:, s, i, :], ident[:, :])
            m.then_inc(picked_turned, 1)
            with pe.Fori(0, T // 8) as n:
                for j in range(8):
                    if j % 4 == 0:
                        pe.wait_ge(gates_copied[j // 4], n + PRIMED)
                    pe.wait_ge(onehot1_ready, 8 * n + j + 1)
                    pe.wait_ge(onehot2_ready, 8 * n + j + 1)
                    mm(bank[:, 6 + j // 4, P * (j % 4):P * (j % 4) + P], onehots[:, j % 2, 1, :],
                       onehots[:, j % 2, 0, :]).then_inc(gates_done[j % 2], 1)

            base = loads["experts_t"]
            with pe.Fori(0, EXPERT_STEPS) as n:
                for e in range(2):
                    pe.wait_ge(tile_landed[e], 16 * n + 16 * (base + 1))
                    pe.wait_ge(gelu_done[e], n + PRIMED)
                    for kt in range(KT):
                        m = mm(bank[:, e, 0:T], slot[e][:, P * kt:P * kt + P], act_t[:, kt, :],
                               start=kt == 0, stop=kt == KT - 1)
                    m.then_inc(tile_used[e], 1)
                for half in range(2):
                    for e in range(2):
                        if half == 0:
                            pe.wait_ge(tile_landed[2 + e], 16 * n + 16 * (base + 1))
                            pe.wait_ge(weighed_ready[e], n + 1 + PRIMED)
                        for c in range(4):
                            if e == 0:
                                pe.wait_ge(share_added[c], 2 * n + half + PRIMED)
                            m = mm(bank[:, 2 + c, :], weighed[:, e, P * half:P * half + P],
                                   slot[2 + e][:, N * c:N * c + N], start=e == 0, stop=e == 1)
                            if e == 1:
                                m.then_inc(shares_done, 1)

            turn(3, norm3_rows)
            pe.wait_ge(turned_copied, TURN0[4])
            product_loop("w_in_2_t", 4, stationary_weights=0)
            for g in range(8, 11):
                product("w_in_2_t", g)
            pe.wait_ge(stage4_landed, STAGE4_DMAS)
            for t in range(TT):
                for kt in range(KT):
                    m = mm(bank[:, 6 + t, 0:SSM_HEADS], act_t[:, kt, P * t:P * t + P], dt_w[:, kt, :],
                           start=kt == 0, stop=kt == KT - 1)
            m.then_inc(small_done, 1)
            pe.wait_ge(small_copied, 2)
            turn(4, qkvz_half[0])
            pe.wait_ge(turned_copied, TURN0[5])
            attention(attention2)

            pe.wait_ge(scan_act, 1)
            pe.wait_ge(set_copied, 2 * 8)
            for n in range(4):
                i = n // 2
                for j in range(4):
                    m = pe.transpose(bank[:, 4 + n, P * j:P * j + P], xbc[:, 4 * (n % 2) + j, P * i:P * i + P], ident[:, :])
            m.then_inc(scan_pe, 1)
            for g in range(SSM_GROUPS):
                mm(bank[:, g, 0:T], xbc[:, 8 + g, 0:P], xbc[:, 10 + g, :])
                m = mm(bank[:, g, T:T + P], xbc[:, 8 + g, P:T], xbc[:, 10 + g, P:T])
            m.then_inc(scan_pe, 1)
            pe.wait_ge(scan_dve, 1)
            mm(bank[:, 2, 0:TT * SSM_HEADS], triu[:, :], dt_[:, 1, :])
            mm(bank[:, 3, 0:SSM_HEADS], ones[:, :], dt_[:, 1, 0:SSM_HEADS]).then_inc(scan_pe, 1)
            for i in range(TT):
                pe.wait_ge(scan_dve, 2 + i)
                for c in range(4):
                    m = mm(bank[:, 4 + c, :], ones[:, :], la_triu[:, N * c:N * c + N])
                m.then_inc(scan_pe, 1)
            pe.wait_ge(scan_dve, 4)
            for g in range(SSM_GROUPS):
                for j in range(GROUP_HEADS):
                    h = GROUP_HEADS * g + j
                    cols = slice(SSM_DH * j, SSM_DH * j + SSM_DH)
                    xs = [x_dt[:, i, SSM_DH * h:SSM_DH * h + SSM_DH] for i in range(TT)]
                    mm(bank[:, g, cols], decay[:, 0, h, :], xs[0])
                    mm(bank[:, 2 + g, cols], decay[:, 2, h, :], xs[0], stop=False)
                    m = mm(bank[:, 2 + g, cols], decay[:, 1, h, :], xs[1], start=False)
            m.then_inc(scan_pe, 1)
            turn(5, o2)
            pe.wait_ge(turned_copied, TURN0[6])
            product_loop("w_out_2_t", 2, stationary_weights=0)

            turn(6, norm4_rows)
            pe.wait_ge(turned_copied, TURN0[7])
            product_loop("w_up_2_t", FF_GROUPS // 2)
            for j in range(2):
                pe.wait_ge(hidden_ready[j], FF_GROUPS // 2 + PRIMED)
            product_loop("w_down_2_t", 2, chunks=DOWN_CHUNKS, lhs=ff_hidden, stationary_weights=0)

        @block.vector
        def _(dve):
            prime(dve, [*pair_copied, *share_added, *weighed_ready, *hidden_ready])
            steps = Steps(dve, dve_step)
            link, note, settle = steps.link, steps.note, steps.settle

            def rms_scale(e, n_features):
                at = stat[:, 4 * e + 2:4 * e + 4]
                link(dve.tensor_scalar(at, stat[:, 4 * e:4 * e + 2], 1.0 / n_features, EPS, ALU.mult, ALU.add))
                dve.reciprocal(at, at).then_inc(root_wanted, 1)
                dve.wait_ge(root_done, ROOTS.index(e) + 1)

            def scale_rows(e, dst):
                dve.wait_ge(squared, TT * (e + 1))
                rms_scale(e, D)
                for i in range(TT):
                    dve.tensor_scalar(dst[:, i, :], resid[:, i, :], stat[:, 4 * e + 2 + i:4 * e + 3 + i], None,
                                      ALU.mult).then_inc(scaled, 1)

            def copy_turned(n, dst):
                for b in range(8):
                    i, c = b // 4, 4 * (b % 4)
                    dve.wait_ge(turned, TURN0[n] + b + 1)
                    dve.tensor_tensor(dst[:, c:c + 4, P * i:P * i + P],
                                      bank[:, 4 + b % 4, :].rearrange("p (c t) -> p c t", c=4),
                                      row(gains[:, n, c:c + 4], P), ALU.mult).then_inc(turned_copied, 1)

            def copy_groups(name, g0, steps_, dst_of):
                with dve.Fori(0, steps_) as i:
                    for j in range(2):
                        b, used = pair(name, g0 + j)
                        dve.wait_ge(tile_used[3], 2 * i + uses[name][3] + g0 + j + 1 + PRIMED)
                        for k in range(2):
                            dve.tensor_copy(dst_of(i, j, k), bank[:, 2 * b + k, :]).then_inc(pair_copied[b], 1)

            def add_groups(name):
                with dve.Fori(0, 2) as i:
                    for j in range(2):
                        b, used = pair(name, j)
                        dve.wait_ge(tile_used[3], 2 * i + uses[name][3] + j + 1 + PRIMED)
                        for t in range(TT):
                            part_ = resid[:, t, bass.ds(i * 2 * N + j * N, N)]
                            dve.tensor_tensor(part_, bank[:, 2 * b + t, :], part_, ALU.add).then_inc(pair_copied[b], 1)

            def attention(a, set_done):
                units, first, logits = a["units"], a["first"], a["logits"]
                for n, u in enumerate(units):
                    g, b = first + n, (first + n) % 2
                    dve.wait_ge(scores_done, g + 1)
                    if g >= 2:
                        dve.wait_ge(probs_turned, g - 1)
                    at = logits[:, b, :]
                    dve.scalar_tensor_tensor(at[:, 0:T], bank[:, b, 0:T], u["scale"], u["bias"][:, 0:T],
                                             ALU.mult, ALU.add)
                    last = dve.scalar_tensor_tensor(at[:, T + 1:T + 1 + P], bank[:, b, T:T + P], u["scale"],
                                                    u["bias"][:, P:T], ALU.mult, ALU.add)
                    if u["sink"] is not None:
                        last = dve.tensor_copy(at[:, T:T + P + 2:P + 1], u["sink"].to_broadcast([P, 2]))
                    last.then_inc(logits_written, 1)
                    dve.wait_ge(logits_written, g + 1)
                    s = 0 if u["sink"] is None else 1
                    dve.tensor_reduce(a["negmax"][:, UNITS + n:UNITS + n + 1], at[:, 0:T + s], AX.X, ALU.max,
                                      negate=True).then_inc(logits_ready, 1)
                    dve.tensor_reduce(a["negmax"][:, n:n + 1], at[:, T + 1:T + 1 + P + s], AX.X, ALU.max,
                                      negate=True).then_inc(logits_ready, 1)
                    if n >= 2 and units[n - 2]["set"] != units[n - 1]["set"]:
                        set_done(n - 2)
                set_done(len(units) - 1)

            dve.memset(cmp_hid[:, :, :, :], 0.0).then_inc(cmp_dve, 1)
            dve.wait_ge(tables_done, 1)
            dve.tensor_copy(by_distance[0:2 * HEADS, :], bank[0:2 * HEADS, 0, 0:3 * P]).then_inc(tables_copied, 1)
            dve.tensor_copy(cbias[:, :, :, :], bank[:, 1, :].rearrange("p (i c h) -> p i h c", i=TT, c=CMP_PAD)
                            ).then_inc(tables_copied, 1)

            dve.wait_ge(x_landed, 16 * TT)
            dve.wait_ge(consts_landed, CONST_DMAS)
            scale_rows(0, o1)
            copy_turned(0, act_t)
            copy_groups("w_in_t", 0, 2, lambda i, j, k: q1[:, bass.ds(i * 8 + (4 * j + 2 * k), 2), :].rearrange("p c t -> p (c t)"))
            b, used = pair("w_in_t", 4)
            dve.wait_ge(tile_used[3], uses["w_in_t"][3] + 5 + PRIMED)
            for k in range(2):
                dve.tensor_copy(k1[:, 2 * k:2 * k + 2, :].rearrange("p c t -> p (c t)"), bank[:, 2 * b + k, :]).then_inc(pair_copied[b], 1)
            b, used = pair("w_in_t", 5)
            dve.wait_ge(tile_used[3], uses["w_in_t"][3] + 6 + PRIMED)
            for t in range(TT):
                dve.tensor_copy(v1[:, t, :], bank[:, 2 * b + t, 0:3 * P]).then_inc(pair_copied[b], 1)
            link(dve.tensor_copy(k1[:, 4, :], bank[:, 4, 0:T]))

            dve.wait_ge(stage1_landed, STAGE1_DMAS)
            for v in range(2):
                src = k1[:, 3 + v, :]
                blocks = bass.AP(tensor=src.tensor, offset=src.offset,
                                 ap=[list(src.ap[0]), [1, CMP_LEN], [CMP_STRIDE, N_CMP]])
                m = dve.tensor_tensor(cmp_in[:, v, :, 0:N_CMP], blocks, row(cmp_pos[:, v, :], N_CMP), ALU.add)
            m.then_inc(cmp_dve, 1)
            dve.wait_ge(cmp_act, 1)
            for g in range(2):
                dve.tensor_copy(cmp_hid8[g][:, :, :], copies(cmp_hid[:, g, 1, :], GROUP_HEADS)).then_inc(cmp_dve, 1)
            dve.wait_ge(cmp_pe, 3)
            for g in range(2):
                dve.tensor_tensor(cmp_v[:, g, :].rearrange("p (h d) -> p h d", h=GROUP_HEADS),
                                  copies(bank[:, 5, DH * g:DH * g + DH], GROUP_HEADS), row(block_of, DH), ALU.mult)
            dve.tensor_copy(cmp_k, bank[:, 4, 0:CMP_PAD]).then_inc(cmp_dve, 1)
            dve.wait_ge(cmp_pe, 4)
            rows_c = cmp_logits[:, :, :, :, :].rearrange("p g i h c -> p (g i h) c")
            for g in range(2):
                note(dve.scalar_tensor_tensor(
                    cmp_logits[:, g, :, :, :].rearrange("p i h c -> p i (h c)"),
                    bank[:, 6 + g, 0:T].rearrange("p (i n) -> p i n", i=TT), DH ** -0.5,
                    cbias[:, :, GROUP_HEADS * g:GROUP_HEADS * (g + 1), :].rearrange("p i h c -> p i (h c)"),
                    ALU.mult, ALU.add))
            settle()
            link(dve.tensor_reduce(cmp_stat[:, 0, :], rows_c, AX.X, ALU.max))
            dve.tensor_tensor(rows_c, rows_c, row(cmp_stat[:, 0, :], CMP_PAD), ALU.subtract).then_inc(cmp_shifted, 1)
            dve.wait_ge(cmp_act, 2)
            link(dve.tensor_reduce(cmp_stat[:, 1, :], rows_c, AX.X, ALU.add))
            link(dve.reciprocal(cmp_stat[:, 2, :], cmp_stat[:, 1, :]))
            dve.wait_ge(small_copied, 1)
            for g in range(2):
                note(dve.tensor_tensor(
                    cmp_stat[:, 3, 16 * g:16 * g + 16].rearrange("p (i h) -> p i h", i=TT),
                    cmp_stat[:, 2, 16 * g:16 * g + 16].rearrange("p (i h) -> p i h", i=TT),
                    gate1[:, :, GROUP_HEADS * g:GROUP_HEADS * (g + 1), 0], ALU.mult))
            for g in range(2):
                m = dve.tensor_tensor(cmp_logits[:, g, :, :, :], cmp_logits[:, g, :, :, :],
                                      copies(valid_c, GROUP_HEADS, at=2), ALU.mult)
            m.then_inc(cmp_dve, 1)
            dve.wait_ge(cmp_pe, 5)
            dve.tensor_copy(cmp_probs_t[:, :, :].rearrange("p n q -> p (n q)"), bank[:, 4, :]).then_inc(cmp_dve, 1)
            dve.wait_ge(cmp_pe, 6)
            settle()
            for g in range(2):
                for i in range(TT):
                    at = 16 * g + 8 * i
                    m = dve.tensor_tensor(o1[:, i, N * g:N * g + N].rearrange("p (h d) -> p h d", d=DH),
                                          bank[:, 2 * i + g, :].rearrange("p (h d) -> p h d", d=DH),
                                          row(cmp_stat[:, 3, at:at + 8], DH), ALU.mult)
            m.then_inc(cmp_dve, 1)

            dve.wait_ge(bias_landed, 16)

            def set_done1(n):
                u = units1[n]
                s, n0 = u["set"], n - GROUP_HEADS + 1
                branch, g = s // 2, s % 2
                dve.wait_ge(mixed, n + 1)
                dve.wait_ge(probs_ready, 2 * (n + 1))
                sums = expsum1.rearrange("p (i n) -> p i n", i=TT)[:, :, n0:n0 + GROUP_HEADS]
                dve.wait_ge(cmp_dve, 8)
                link(dve.reciprocal(sums, sums))
                if branch < 2:
                    link(dve.tensor_tensor(sums, sums, gate1[:, :, GROUP_HEADS * g:GROUP_HEADS * (g + 1), 1 + branch],
                                           ALU.mult))
                for i in range(TT):
                    at = N * (s - 2 if branch == 2 else g)
                    part_ = o1[:, i, at:at + N]
                    dst = part_ if branch == 2 else share1
                    dve.tensor_tensor(dst.rearrange("p (h d) -> p h d", d=DH),
                                      bank[:, 4 + 2 * (s % 2) + i, :].rearrange("p (h d) -> p h d", d=DH),
                                      row(sums[:, i, :], DH), ALU.mult).then_inc(set_copied, 1)
                    if branch < 2:
                        dve.wait_ge(set_copied, 2 * s + i + 1)
                        link(dve.tensor_tensor(part_, part_, share1, ALU.add))

            attention(attention1, set_done1)
            dve.wait_ge(set_copied, 2 * 6)
            for i in range(TT):
                dve.tensor_copy(stat[:, 60 + i:61 + i], o1[:, i, D - 1:D]).then_inc(scaled, 1)
            copy_turned(1, act_t)
            add_groups("w_out_t")

            scale_rows(1, norm2_rows)
            copy_turned(2, act_t)
            copy_groups("peer_wq_t", 0, 2, lambda i, j, k: peer_q[:, bass.ds(i * 8 + (4 * j + 2 * k), 2), :].rearrange("p c t -> p (c t)"))
            for n in range(8):
                dve.wait_ge(subkey_scores_done, n + 1)
                dve.tensor_copy(scores[:, 4 * n:4 * n + 4, :].rearrange("p r n -> p (r n)"), bank[:, 4 + n % 4, :]
                                ).then_inc(subkey_scores_copied, 1)
            dve.wait_ge(subkey_scores_copied, 8)

            def top16(n, src, left, values, at):
                for r in range(n):
                    note(dve.max(values[:, r, 0:8], src[:, r, :]))
                settle()
                for r in range(n):
                    note(dve.match_replace(left[:, r, :], values[:, r, 0:8], src[:, r, :], LOWEST))
                    note(dve.max_index(at[:, r, 0:8], values[:, r, 0:8], src[:, r, :]))
                settle()
                for r in range(n):
                    note(dve.max(values[:, r, 8:16], left[:, r, :]))
                settle()
                for r in range(n):
                    note(dve.max_index(at[:, r, 8:16], values[:, r, 8:16], left[:, r, :]))
                settle()

            top16(TT * 16, scores, scores_left, top, top_at)
            note(dve.tensor_copy(top_key.rearrange("p r k -> p (r k)"), top_at.rearrange("p r k -> p (r k)")))
            top_side = top.rearrange("p (r s) k -> p r s k", s=2)
            link(dve.tensor_tensor(pairs.rearrange("p r (a b) -> p r a b", a=TOPK), row(top_side[:, :, 0, :], TOPK),
                                   copies(top_side[:, :, 1, :], TOPK, at=2), ALU.add))
            top16(TT * PEER_HEADS, pairs, pairs_left, best, best_at)
            sub = picked[:, 2, :, :].rearrange("p i (h k) -> p (i h) k", k=TOPK)
            dve.tensor_tensor(sub, best, row(best[:, :, 0], TOPK), ALU.subtract).then_inc(best_ready, 1)
            flat_at = best_at.rearrange("p r k -> p (r k)")
            note(dve.tensor_scalar(part_at[:, 0, :], flat_at, 4, None, ALU.logical_shift_right))
            link(dve.tensor_scalar(part_at[:, 1, :], flat_at, TOPK - 1, None, ALU.bitwise_and))
            link(dve.tensor_copy(part.rearrange("p s r -> p (s r)"), part_at.rearrange("p s r -> p (s r)")))
            keys = top_key.rearrange("p (r s) k -> p r s k", s=2)
            for s in range(2):
                link(dve.tensor_tensor(is_part, row(part[:, s, :], TOPK), copies(iota[:, 0:TOPK], TT * P), ALU.is_equal))
                four = is_part.rearrange("p (r j) a -> p r j a", j=TOPK)
                link(dve.tensor_tensor(four, four, copies(keys[:, :, s, :], TOPK, at=2), ALU.mult))
                link(dve.tensor_reduce(picked[:, s, :, :].rearrange("p i k -> p (i k)"), is_part, AX.X, ALU.add))
            dve.wait_ge(best_exp, 1)
            link(dve.tensor_reduce(best_sum[:, 0, :], sub, AX.X, ALU.add))
            link(dve.reciprocal(best_sum[:, 1, :], best_sum[:, 0, :]))
            dve.tensor_tensor(sub, sub, row(best_sum[:, 1, :], TOPK), ALU.mult).then_inc(picked_ready, 1)
            dve.wait_ge(picked_turned, 1)
            dve.tensor_copy(picked_t[:, 0:2, :].rearrange("p s t -> p (s t)"), bank[:, 4, :]).then_inc(picked_copied, 1)
            dve.tensor_copy(picked_t[:, 2, :], bank[:, 5, 0:T]).then_inc(picked_copied, 1)
            dve.wait_ge(picked_copied, 2)
            with dve.Fori(0, T // 8) as n:
                for j in range(8):
                    dve.wait_ge(gates_done[j % 2], 4 * n + j // 2 + PRIMED)
                    dve.tensor_scalar(onehots[:, j % 2, 0, :], iota[:, :], picked_t[:, 0, bass.ds(8 * n + j, 1)],
                                      picked_t[:, 2, bass.ds(8 * n + j, 1)], ALU.is_equal, ALU.mult
                                      ).then_inc(onehot1_ready, 1)
                    dve.tensor_scalar(onehots[:, j % 2, 1, :], iota[:, :], picked_t[:, 1, bass.ds(8 * n + j, 1)], None,
                                      ALU.is_equal).then_inc(onehot2_ready, 1)

            for b in range(2):
                dve.wait_ge(gates_copied[b], T // 8 + PRIMED)
            with dve.Fori(0, EXPERT_STEPS) as n:
                for e in range(2):
                    dve.wait_ge(gelu_done[e], n + 1 + PRIMED)
                    dve.wait_ge(shares_done, 8 * n + PRIMED)
                    dve.tensor_tensor(weighed[:, e, :], hidden[:, e, :],
                                      gates[:, bass.ds(2 * n + e, 1), :].rearrange("p a t -> p (a t)"), ALU.mult
                                      ).then_inc(weighed_ready[e], 1)
                for half in range(2):
                    for c in range(4):
                        dve.wait_ge(shares_done, 8 * n + 4 * half + c + 1 + PRIMED)
                        dve.wait_ge(share_added[c], 2 * n + half + PRIMED)
                        part_ = resid[:, half, N * c:N * c + N]
                        dve.tensor_tensor(part_, bank[:, 2 + c, :], part_, ALU.add).then_inc(share_added[c], 1)

            dve.wait_ge(final_gain_landed, 16)
            dve.wait_ge(squared, TT * 3)
            rms_scale(2, D)
            for i in range(TT):
                dve.scalar_tensor_tensor(resid[:, i, :], resid[:, i, :], stat[:, 10 + i:11 + i], final_gain,
                                         ALU.mult, ALU.mult).then_inc(normed, 1)
            dve.wait_ge(normed, TT)
            scale_rows(3, norm3_rows)
            copy_turned(3, act_t)
            for half in range(2):
                copy_groups("w_in_2_t", 4 * half, 2, lambda i, j, k: qkvz_half[half][:, k, bass.ds(i * 2 * N + j * N, N)])
            for g in range(8, 11):
                b, used = pair("w_in_2_t", g)
                dve.wait_ge(tile_used[3], uses["w_in_2_t"][3] + g + 1 + PRIMED)
                for k in range(2):
                    c = 4 * (g - 8) + 2 * k
                    dve.tensor_copy(xbc_raw[:, c:c + 2, :].rearrange("p c t -> p (c t)"), bank[:, 2 * b + k, :]).then_inc(pair_copied[b], 1)
            dve.wait_ge(small_done, 2)
            for t in range(TT):
                cols = slice(SSM_HEADS * t, SSM_HEADS * (t + 1))
                m = dve.tensor_tensor(dt_tmp[:, 0, cols], bank[:, 6 + t, 0:SSM_HEADS], rows[:, 1, :], ALU.add)
            m.then_inc(small_copied, 1)

            for i in range(TT):
                dve.wait_ge(squared, TT * 4 + i + 1)
                heads = qk2[:, i, :].rearrange("p (h d) -> p h d", d=DH2)
                link(dve.tensor_reduce(stat[:, 24:40], squares.rearrange("p (h d) -> p h d", d=DH2), AX.X, ALU.add))
                link(dve.tensor_scalar(stat[:, 40:56], stat[:, 24:40], 1.0 / DH2, EPS, ALU.mult, ALU.add))
                dve.reciprocal(stat[:, 40:56], stat[:, 40:56]).then_inc(root_wanted, 1)
                dve.wait_ge(root_done, ROOTS.index(f"heads {i}") + 1)
                dve.tensor_tensor(heads, heads, row(stat[:, 40:56], DH2), ALU.mult).then_inc(scaled, 1)
            copy_turned(4, qk_t)

            def set_done2(n):
                u = units2[n]
                s, n0 = u["set"], n - 3
                dve.wait_ge(mixed, UNITS + n + 1)
                dve.wait_ge(probs_ready, 2 * (UNITS + n + 1))
                sums = expsum2.rearrange("p (i n) -> p i n", i=TT)[:, :, n0:n0 + 4]
                link(dve.reciprocal(sums, sums))
                for i in range(TT):
                    dve.tensor_tensor(o2[:, i, N * (s - 6):N * (s - 5)].rearrange("p (h d) -> p h d", d=DH2),
                                      bank[:, 4 + 2 * (s % 2) + i, :].rearrange("p (h d) -> p h d", d=DH2),
                                      row(sums[:, i, :], DH2), ALU.mult).then_inc(set_copied, 1)

            attention(attention2, set_done2)

            for tap in range(SSM_TAPS):
                for c in range(XBC_TILES):
                    if tap == 0:
                        note(dve.tensor_scalar(xbc[:, c, :], xbc_raw[:, c, :], conv1[:, c, 3:4], conv1[:, c, 4:5],
                                               ALU.mult, ALU.add))
                    else:
                        m = dve.scalar_tensor_tensor(xbc[:, c, tap:T], xbc_raw[:, c, 0:T - tap],
                                                     conv1[:, c, 3 - tap:4 - tap], xbc[:, c, tap:T], ALU.mult, ALU.add)
                        if tap == 3 and c == XBC_TILES - 1:
                            m.then_inc(normed, 1)
                        else:
                            note(m)
                if tap < 3:
                    settle()
            dve.wait_ge(small_copied, 2)
            dve.scalar_tensor_tensor(dt_tmp[:, 1, :], dt_tmp[:, 0, :], -1.0, dt_tmp[:, 0, :], ALU.mult, ALU.max).then_inc(normed, 1)
            dve.wait_ge(scan_act, 2)
            link(dve.scalar_tensor_tensor(dt_[:, 0, :], dt_tmp[:, 0, :], 0.0, dt_tmp[:, 1, :], ALU.max, ALU.add))
            la = dt_[:, 1, :]
            dve.scalar_tensor_tensor(la.rearrange("p (i h) -> p i h", i=TT), dt_[:, 0, :].rearrange("p (i h) -> p i h", i=TT),
                                     -1.0, copies(dt_tmp[:, 2, 0:SSM_HEADS], TT), ALU.mult, ALU.mult).then_inc(scan_dve, 1)
            dve.wait_ge(scan_dve, 1)
            triangle = la_triu.rearrange("p (h l) -> p h l", l=P)
            note(dve.tensor_tensor(triangle, row(la[:, 0:SSM_HEADS], P), copies(triu[:, :], SSM_HEADS), ALU.mult))
            dve.wait_ge(scan_pe, 1)
            for n in range(4):
                m = dve.tensor_copy(x_tok[:, n // 2, N * (n % 2):N * (n % 2) + N], bank[:, 4 + n, :])
            m.then_inc(scan_dve, 1)
            dve.wait_ge(scan_pe, 3)
            for g in range(SSM_GROUPS):
                note(dve.tensor_copy(cb[:, g, :], bank[:, g, 0:3 * P]))
            link(dve.tensor_copy(dt_[:, 2, :], bank[:, 2, 0:TT * SSM_HEADS]))
            link(dve.tensor_tensor(dt_[:, 3, 0:SSM_HEADS], bank[:, 3, 0:SSM_HEADS], dt_[:, 2, 0:SSM_HEADS], ALU.subtract))
            for i in range(TT):
                dve.wait_ge(scan_pe, 4 + i)
                for blk, per_key, op in ([(0, dt_[:, 2, 0:SSM_HEADS], ALU.subtract)] if i == 0 else
                                         [(1, dt_[:, 2, SSM_HEADS:], ALU.subtract), (2, dt_[:, 3, 0:SSM_HEADS], ALU.add)]):
                    for c in range(4):
                        m = dve.tensor_tensor(decay[:, blk, 4 * c:4 * c + 4, :],
                                              bank[:, 4 + c, :].rearrange("p (h l) -> p h l", l=P),
                                              row(per_key[:, 4 * c:4 * c + 4], P), op)
                        note(m)
                if i == 0:
                    dve.tensor_tensor(triangle, row(la[:, SSM_HEADS:], P), copies(triu[:, :], SSM_HEADS),
                                      ALU.mult).then_inc(scan_dve, 1)
                settle()
                dve.tensor_tensor(decay[:, i, :, :], decay[:, i, :, :], copies(low_mask[:, :], SSM_HEADS), ALU.add
                                  ).then_inc(normed, 1)
            link(dve.tensor_tensor(x_dt.rearrange("p i (h d) -> p (i h) d", d=SSM_DH),
                                   x_tok.rearrange("p i (h d) -> p (i h) d", d=SSM_DH), row(dt_[:, 0, :], SSM_DH), ALU.mult))
            dve.wait_ge(scan_act, 3)
            for blk, at in ((0, 0), (1, 2), (2, 1)):
                for g in range(SSM_GROUPS):
                    part_ = decay[:, blk, GROUP_HEADS * g:GROUP_HEADS * (g + 1), :]
                    m = dve.tensor_tensor(part_, part_, copies(cb[:, g, P * at:P * at + P], GROUP_HEADS), ALU.mult)
            m.then_inc(scan_dve, 1)
            for i in range(TT):
                heads = x_tok[:, i, :].rearrange("p (h d) -> p h d", d=SSM_DH)
                note(dve.tensor_tensor(heads, heads, row(rows[:, 3, :], SSM_DH), ALU.mult))
            settle()
            dve.wait_ge(scan_pe, 6)
            for i in range(TT):
                for g in range(SSM_GROUPS):
                    note(dve.tensor_tensor(o2[:, i, SSM_W + N * g:SSM_W + N * (g + 1)], bank[:, 2 * i + g, :],
                                           x_tok[:, i, N * g:N * (g + 1)], ALU.add))
            settle()
            dve.wait_ge(scan_act, 4)
            y = o2[:, :, SSM_W:]
            link(dve.tensor_tensor(y, y, vz2[:, :, SSM_W:], ALU.mult))
            link(dve.tensor_tensor(squares.rearrange("p (i d) -> p i d", i=TT), y, y, ALU.mult))
            link(dve.tensor_reduce(stat[:, 24:28], squares.rearrange("p (n d) -> p n d", d=N), AX.X, ALU.add))
            link(dve.tensor_scalar(stat[:, 28:32], stat[:, 24:28], 1.0 / N, EPS, ALU.mult, ALU.add))
            dve.reciprocal(stat[:, 28:32], stat[:, 28:32]).then_inc(root_wanted, 1)
            dve.wait_ge(root_done, ROOTS.index("scan") + 1)
            for i in range(TT):
                part_ = y[:, i, :].rearrange("p (g d) -> p g d", d=N)
                dve.tensor_tensor(part_, part_, row(stat[:, 28 + 2 * i:30 + 2 * i], N), ALU.mult).then_inc(scaled, 1)
            copy_turned(5, act_t)
            add_groups("w_out_2_t")

            scale_rows(5, norm4_rows)
            copy_turned(6, act_t)
            with dve.Fori(0, FF_GROUPS // 2) as i:
                for j in range(2):
                    b, used = pair("w_up_2_t", j)
                    w = conv2[:, bass.ds(2 * i + j, 1), :].rearrange("p a n -> p (a n)")
                    dve.wait_ge(tap_done[j], i + 1)
                    for tap in (1, 2):
                        for q in range(4):
                            raw = bank[:, 2 * b + q // 2, T * (q % 2):T * (q % 2) + T - tap]
                            m = dve.scalar_tensor_tensor(taps[:, j, q, tap:T], raw, w[:, 4 * q + 2 - tap:4 * q + 3 - tap],
                                                         taps[:, j, q, tap:T], ALU.mult, ALU.add)
                            m.then_inc(conv_step[j] if tap == 1 else conv_done[j] if q < 2 else pair_copied[b], 1)
                        if tap == 1:
                            dve.wait_ge(conv_step[j], 4 * i + 4)
                    dve.wait_ge(silu_done[j], i + 1)
                    dve.wait_ge(pair_copied[b], 2 * i + 2 * (used + 1) + PRIMED)
                    dve.tensor_tensor(ff_hidden[:, bass.ds(4 * i + 2 * j, 2), :], taps[:, j, 0:2, :], taps[:, j, 2:4, :],
                                      ALU.mult).then_inc(hidden_ready[j], 1)
            for g in range(4):
                b, used = pair("w_down_2_t", g)
                dve.wait_ge(tile_used[2], uses["w_down_2_t"][2] + DOWN_USES[2] * (g + 1) + PRIMED)
                for t in range(TT):
                    part_ = resid[:, t, N * g:N * g + N]
                    dve.tensor_tensor(part_, bank[:, 2 * b + t, :], part_, ALU.add).then_inc(pair_copied[b], 1)

        @block.scalar
        def _(act):
            prime(act, [*gates_copied, *gelu_done])
            for dst, name in STAGE1[:3]:
                act.dma_start(dst, ins[name]).then_inc(stage1_landed, 16)
            for dst, name in CONSTS:
                act.dma_start(dst[:], ins[name]).then_inc(consts_landed, 16)
            for dst, name in STAGE1[3:]:
                act.dma_start(dst, ins[name]).then_inc(stage1_landed, 16)

            def root(which, at):
                act.wait_ge(root_wanted, ROOTS.index(which) + 1)
                act.activation(at, at, ACT.Sqrt).then_inc(root_done, 1)

            def square_rows(e, dst):
                for i in range(TT):
                    act.activation(dst[:, i, :], resid[:, i, :], ACT.Square, accum_out=stat[:, 4 * e + i:4 * e + i + 1]
                                   ).then_inc(squared, 1)
                root(e, stat[:, 4 * e + 2:4 * e + 4])

            def attention(a):
                units, first, logits = a["units"], a["first"], a["logits"]

                def exps(n):
                    g, b = first + n, (first + n) % 2
                    s = 0 if units[n]["sink"] is None else 1
                    act.wait_ge(logits_ready, 2 * (g + 1))
                    for at, width, col in ((0, T + s, UNITS + n), (T + 1, P + s, n)):
                        part_ = logits[:, b, at:at + width]
                        act.activation(part_, part_, ACT.Exp, bias=a["negmax"][:, col:col + 1],
                                       accum_out=a["expsum"][:, col:col + 1]).then_inc(probs_ready, 1)

                def copy_probs(n):
                    g, b = first + n, (first + n) % 2
                    act.wait_ge(probs_turned, g + 1)
                    if g >= 2:
                        act.wait_ge(mixed, g - 1)
                    act.activation(a["probs_t"][:, b, :], bank[:, 2 + b, 0:3 * P], ACT.Copy).then_inc(probs_copied, 1)

                for n in range(len(units) + 1):
                    if n < len(units):
                        exps(n)
                    if n >= 1:
                        copy_probs(n - 1)

            act.wait_ge(tables_copied, 1)
            act.dma_start(bias_dram[:].rearrange("(h j) -> h j", j=3 * P), by_distance[0:2 * HEADS, :]).then_inc(bias_stored, 16)
            act.wait_ge(x_landed, 16 * TT)
            square_rows(0, o1)
            act.wait_ge(bias_stored, 16)
            act.dma_start(bias_copies[:, :], bias_dram[:].partition_broadcast(P)).then_inc(bias_spread, 16)
            act.wait_ge(bias_spread, 16)
            act.dma_start(bias1, bass.AP(tensor=bias_copies, offset=P - 1, ap=[[BIAS_ROW - 1, P], [3 * P, 2 * HEADS], [1, T]])
                          ).then_inc(bias_landed, 16)
            act.wait_ge(small_done, 1)
            for t in range(TT):
                m = act.activation(gate1[:, t, :, :].rearrange("p h b -> p (h b)"), bank[:, 5 + t, 0:GATES], ACT.Sigmoid)
            m.then_inc(small_copied, 1)
            act.wait_ge(cmp_dve, 1)
            act.wait_ge(cmp_pe, 1)
            for g in range(2):
                m = act.activation(cmp_hid[:, g, :, 0:N_CMP],
                                   bank[:, 6 + g, 0:2 * CMP_PAD].rearrange("p (v c) -> p v c", v=2)[:, :, 0:N_CMP],
                                   ACT.Gelu_apprx_tanh)
            m.then_inc(cmp_act, 1)
            act.wait_ge(cmp_shifted, 1)
            flat = cmp_logits[:, :, :, :, :].rearrange("p g i h c -> p (g i h c)")
            act.activation(flat, flat, ACT.Exp).then_inc(cmp_act, 1)
            attention(attention1)

            wait_pairs(act, "w_out_t")
            square_rows(1, norm2_rows)
            act.wait_ge(best_ready, 1)
            flat = picked[:, 2, :, :].rearrange("p i k -> p (i k)")
            act.activation(flat, flat, ACT.Exp).then_inc(best_exp, 1)
            with act.Fori(0, T // 8) as n:
                for b in range(2):
                    act.wait_ge(gates_done[1], 4 * n + 2 * b + 2 + PRIMED)
                    act.activation(gates[:, :, bass.ds(8 * n + 4 * b, 4)], bank[:, 6 + b, :].rearrange("p (t e) -> p e t", t=4),
                                   ACT.Copy).then_inc(gates_copied[b], 1)
            with act.Fori(0, EXPERT_STEPS) as n:
                for e in range(2):
                    act.wait_ge(tile_used[e], n + uses["experts_t"][e] + 1 + PRIMED)
                    act.wait_ge(weighed_ready[e], n + PRIMED)
                    act.activation(hidden[:, e, :], bank[:, e, 0:T], ACT.Gelu_apprx_tanh).then_inc(gelu_done[e], 1)

            for c in range(4):
                act.wait_ge(share_added[c], 2 * EXPERT_STEPS + PRIMED)
            square_rows(2, o2)
            act.wait_ge(normed, TT)
            square_rows(3, norm3_rows)
            wait_pairs(act, "w_in_2_t")
            for i in range(TT):
                if i:
                    act.wait_ge(scaled, TT * 4 + i)
                act.activation(squares, qk2[:, i, :], ACT.Square).then_inc(squared, 1)
                root(f"heads {i}", stat[:, 40:56])
            attention(attention2)
            act.wait_ge(normed, TT + 1)
            flat = xbc.rearrange("p c t -> p (c t)")
            act.activation(flat, flat, ACT.Silu).then_inc(scan_act, 1)
            act.wait_ge(normed, TT + 2)
            act.activation(dt_tmp[:, 1, :], dt_tmp[:, 1, :], ACT.Exp, scale=-1.0).then_inc(act_step, 1)
            act.wait_ge(act_step, 1)
            act.activation(dt_tmp[:, 2, 0:SSM_HEADS], rows[:, 2, :], ACT.Exp)
            act.activation(dt_tmp[:, 1, :], dt_tmp[:, 1, :], ACT.Ln, bias=1.0).then_inc(scan_act, 1)
            act.wait_ge(normed, TT + 4)
            for blk in range(3):
                flat = decay[:, blk, :, :].rearrange("p h l -> p (h l)")
                m = act.activation(flat, flat, ACT.Exp)
            m.then_inc(scan_act, 1)
            z = vz2[:, :, SSM_W:]
            act.activation(z, z, ACT.Silu).then_inc(scan_act, 1)
            root("scan", stat[:, 28:32])
            wait_pairs(act, "w_out_2_t")
            square_rows(5, norm4_rows)
            with act.Fori(0, FF_GROUPS // 2) as i:
                for j in range(2):
                    b, used = pair("w_up_2_t", j)
                    w = conv2[:, bass.ds(2 * i + j, 1), :].rearrange("p a n -> p (a n)")
                    act.wait_ge(tile_used[3], 2 * i + uses["w_up_2_t"][3] + j + 1 + PRIMED)
                    act.wait_ge(hidden_ready[j], i + PRIMED)
                    for q in range(4):
                        m = act.activation(taps[:, j, q, :], bank[:, 2 * b + q // 2, T * (q % 2):T * (q % 2) + T],
                                           ACT.Identity, scale=w[:, 4 * q + 2:4 * q + 3], bias=w[:, 4 * q + 3:4 * q + 4])
                    m.then_inc(tap_done[j], 1)
                    act.wait_ge(conv_done[j], 2 * i + 2)
                    gate_taps = taps[:, j, 0:2, :].rearrange("p q t -> p (q t)")
                    act.activation(gate_taps, gate_taps, ACT.Silu).then_inc(silu_done[j], 1)

        @block.gpsimd
        def _(pool):
            wait_pairs(pool, "w_out_t")
            pool.dma_start(subkeys, ins["subkeys"]).then_inc(subkeys_landed, 16)
            pool.wait_ge(weighed_ready[1], D // T + PRIMED)
            pool.dma_start(final_gain, ins["final_norm"].partition_broadcast(P)).then_inc(final_gain_landed, 16)
            pool.wait_ge(weighed_ready[1], EXPERT_STEPS + PRIMED)
            for dst, name in STAGE4:
                pool.dma_start(dst, ins[name]).then_inc(stage4_landed, 16)


def bucket_of(distance):
    d = np.maximum(distance, 0)
    large = EXACT + (np.log(np.maximum(d, 1).astype(np.float32) / np.float32(EXACT))
                     / np.float32(math.log(MAX_DIST / EXACT)) * (BUCKETS - EXACT)).astype(np.int32)
    return np.where(d < EXACT, d, np.minimum(large, BUCKETS - 1))


def one_hot(distances):
    distances = np.asarray(distances)
    table = np.zeros((BUCKETS + 2, distances.size), np.float32)
    ok = distances >= 0
    table[bucket_of(distances[ok]), np.nonzero(ok)[0]] = 1.0
    table[BUCKETS, ~ok] = 1.0
    table[BUCKETS + 1, distances >= SWA_WINDOW] = 1.0
    return table


def constants():
    p = np.arange(P)
    c = np.arange(CMP_PAD)
    t = np.arange(T).reshape(TT, P).T
    valid = (t[:, :, None] >= CMP_STRIDE * c + CMP_LEN - 1) & (c < N_CMP)
    upper = p[:, None] <= p[None, :]
    return {
        "c_ident": np.eye(P), "c_ones": np.ones((P, P)), "c_iota": np.tile(p, (P, 1)), "c_triu": upper,
        "c_low_mask": np.where(upper, 0.0, NEG),
        "c_causal": np.where(p[:, None] + P >= np.arange(T)[None, :], 0.0, NEG),
        "c_onehot_rev": one_hot(T - 1 - np.arange(3 * P)), "c_onehot_cmp": one_hot(np.arange(CMP_FIRST, T)),
        "c_block_of": p[:, None] // CMP_PAD == np.arange(GROUP_HEADS)[None, :], "c_valid": valid,
    }


def tiles_of(w, n):
    k, columns = w.shape
    w = w.reshape(k // 512, 4, P, columns // n, n).transpose(3, 0, 2, 1, 4)
    return np.ascontiguousarray(w).reshape(-1, P, 4 * n)


def laid_out(a):
    def column(v):
        return v.reshape(-1, P).T

    def in_rows(v):
        return np.broadcast_to(v, (P, v.size))

    w_in = a["w_in"][0]
    at = np.cumsum([0, HEADS * DH, P, P, P, P, P, P, GATES, HEADS * DH, P, P])
    q_a, kc, vc, ks, vs, kw, vw, gate, q_b, k_b, v_b = (w_in[:, x:y] for x, y in zip(at[:-1], at[1:]))

    def by_pairs(q):
        return q.reshape(D, 2, GROUP_HEADS, DH).transpose(0, 2, 1, 3).reshape(D, HEADS * DH)

    w_in = np.concatenate([by_pairs(q_a), by_pairs(q_b), ks, kw, k_b, kc, vc, vs, vw, v_b], axis=1)
    w_in_2 = a["w_in_2"][0]
    w_up = a["w_up_2"][0].reshape(D, 2, FF_GROUPS, 2 * P).transpose(0, 2, 1, 3).reshape(D, -1)
    u = a["peer_u"][0].reshape(EXPERT_STEPS_, 2, P, KT, P).transpose(0, 1, 4, 3, 2).reshape(EXPERT_STEPS_, 2, P, TILE)
    v = a["peer_v"][0].reshape(EXPERT_STEPS_, 2, P, TILE)
    rel = np.concatenate([a["rel_bias"], np.full((1, 2 * HEADS), NEG, np.float32),
                          np.concatenate([np.zeros((1, HEADS), np.float32), np.full((1, HEADS), NEG, np.float32)], axis=1)])

    def w1(w):
        return np.tile(w[0].reshape(CMP_LEN, DH, CMP_HIDDEN).transpose(1, 0, 2), (2, 1, 1))

    ones = np.ones((P, KT), np.float32)
    conv2 = np.concatenate([a["ffn_conv_w_2"][0], a["ffn_conv_b_2"]], axis=0)
    out = {
        "x": a["x"], "w_in_t": tiles_of(w_in, N), "w_out_t": tiles_of(a["w_out"][0], N),
        "peer_wq_t": tiles_of(a["peer_wq"][0], N), "experts_t": np.concatenate([u, v], axis=1).reshape(-1, P, TILE),
        "w_in_2_t": tiles_of(w_in_2[:, :-SSM_HEADS], N), "w_out_2_t": tiles_of(a["w_out_2"][0], N),
        "w_up_2_t": tiles_of(w_up, N), "w_down_2_t": tiles_of(a["w_down_2"][0], N),
        "gate_w": gate.reshape(KT, P, GATES).transpose(1, 0, 2),
        "dt_w": w_in_2[:, -SSM_HEADS:].reshape(KT, P, SSM_HEADS).transpose(1, 0, 2),
        "gains": np.stack([column(a["attn_norm"]), ones, column(a["ffn_norm"]), column(a["norm1_w_2"]),
                           np.concatenate([np.repeat(a["q_norm_w_2"].T, 8, 1), np.repeat(a["k_norm_w_2"].T, 8, 1)], axis=1),
                           np.concatenate([ones[:, :8], column(a["ssm_norm_w_2"])], axis=1), column(a["norm2_w_2"])], axis=1),
        "conv1": np.concatenate([a["ssm_conv_w_2"][0], a["ssm_conv_b_2"]], axis=0).reshape(5, XBC_TILES, P).transpose(2, 1, 0),
        "conv2": conv2.reshape(4, 2, FF_GROUPS, 2, P).transpose(4, 2, 1, 3, 0).reshape(P, FF_GROUPS, 16),
        "rows": np.stack([in_rows(a[n]) for n in ("sinks", "dt_bias_2", "a_log_2", "d_skip_2")], axis=1),
        "bias_rows": rel, "cmp_w1": np.stack([w1(a["cmp_w1_k"]), w1(a["cmp_w1_v"])], axis=1),
        "cmp_w2": np.stack([a["cmp_w2_k"][0], a["cmp_w2_v"][0]], axis=1),
        "cmp_pos": np.stack([np.tile(a["cmp_pos_k"][0].T, (2, 1)), np.tile(a["cmp_pos_v"][0].T, (2, 1))], axis=1),
        "subkeys": a["peer_subkeys"][0].transpose(2, 0, 1), "final_norm": a["final_norm"],
        **constants(),
    }
    return {k: np.ascontiguousarray(v, dtype=np.float32) for k, v in out.items()}


EXPERT_STEPS_ = EXPERT_TILES // 2


def kernel(**inputs):
    import concourse.bacc as bacc
    from concourse.bass_utils import run_bass_kernel_spmd as run

    nc = bacc.Bacc("TRN2", target_bir_lowering=False, num_devices=1)
    arrays = laid_out({k: np.asarray(v) for k, v in inputs.items()})
    ins = {k: nc.dram_tensor("in_" + k, list(v.shape), F32, kind="ExternalInput").ap() for k, v in arrays.items()}
    out = nc.dram_tensor("out", [1, T, D], F32, kind="ExternalOutput").ap()
    build(nc, ins, out)
    return run(nc, [{"in_" + k: v for k, v in arrays.items()}], core_ids=[0]).results[0]["out"]
```

```python
import math
from contextlib import ExitStack

import numpy as np

import concourse.bass as bass
from concourse import mybir

P = 128
T = 256
TT = T // P
D = 2048
KT = D // P
TILE = 2048
RAW = 2
HALF = TILE // 2
SPLIT = 4
LOOKAHEAD = 3
QUAD = 8
N = 512
EPS = 1e-6
NEG = -1e30
LOWEST = -3.0e38

HEADS = 16
DH = 64
GROUP_HEADS = 8
CMP_LEN, CMP_STRIDE, CMP_HIDDEN = 32, 16, 128
N_CMP = T // CMP_STRIDE - 1
CMP_PAD = 16
BUCKETS, EXACT, MAX_DIST = 32, 16, 2048
SWA_WINDOW = 128
CMP_FIRST = -(CMP_PAD * CMP_STRIDE - CMP_STRIDE + CMP_LEN - 1) - 1
GATES = 3 * HEADS
PEER_HEADS, PEER_KEYS, TOPK = 8, 128, 16
QUARTER = 64
EXPERT_TILES = PEER_KEYS

HEADS2, DH2 = 8, 128
SSM_HEADS, SSM_DH, SSM_GROUPS = 16, 64, 2
SSM_W = SSM_HEADS * SSM_DH
XBC_TILES = 12
SSM_TAPS = 4
BIG = 23552
FF_TILES = 44
FF_GROUPS = 22

UNITS = 3 * HEADS

STREAM = [("w_in_t", 24, 6), ("w_out_t", 16, 4), ("peer_wq_t", 16, 4), ("experts_t", 256, 0),
          ("w_in_2_t", 44, 11), ("w_out_2_t", 16, 4), ("w_up_2_t", 88, 22), ("w_down_2_t", 44, 4)]

F32 = mybir.dt.float32
F32R = mybir.dt.float32r
U32 = mybir.dt.uint32
ALU = mybir.AluOpType
ACT = mybir.ActivationFunctionType
AX = mybir.AxisListType



def build(nc, ins, out):
    ctx = ExitStack()
    with ctx:
        def sb(name, shape, dt=F32):
            return ctx.enter_context(nc.sbuf_tensor(name, shape, dt))

        def sem(name):
            return ctx.enter_context(nc.semaphore(name))

        raw = [sb(f"raw{r}", [P, TILE]) for r in range(RAW)]
        high = [sb(f"high{b}", [P, HALF], F32R) for b in range(SPLIT)]
        low = [sb(f"low{b}", [P, HALF], F32R) for b in range(SPLIT)]
        resid = sb("resid", [P, TT, D])
        act_at = nc.sbuf_base
        act_high = sb("act_high", [P, KT, T], F32R)
        act_low = sb("act_low", [P, KT, T], F32R)
        act_place = nc.alloc_sbuf_tensor_at("act_place", [P, 2 * KT * T], F32, offset=act_at)
        big_at = nc.sbuf_base
        big = sb("big", [P, BIG])
        ff_high = nc.alloc_sbuf_tensor_at("ff_high", [P, FF_TILES, T], F32R, offset=big_at)
        ff_low = nc.alloc_sbuf_tensor_at("ff_low", [P, FF_TILES, T], F32R, offset=big_at + 4 * FF_TILES * T)
        bank = ctx.enter_context(nc.psum_tensor("bank", [P, 8, N], F32))

        ident = sb("ident", [P, P])
        ones = sb("ones", [P, P])
        iota = sb("iota", [P, P])
        triu = sb("triu", [P, P])
        low_mask = sb("low_mask", [P, P])
        gains = sb("gains", [P, 7, KT])
        conv1 = sb("conv1", [P, XBC_TILES, SSM_TAPS + 1])
        conv2 = sb("conv2", [P, FF_GROUPS, 16])
        rows = sb("rows", [P, 4, SSM_HEADS])
        stat = sb("stat", [P, 64])
        picked_place = sb("taps", [P, 2, 4, T])
        picked_low = picked_place[:, 1, 0, :]
        picked_t = picked_place[:, 0, 0:3, :]
        small_at = nc.sbuf_base
        narrow_w = [sb(f"narrow_w{n}", [P, KT * GATES], F32R) for n in range(2)]
        onehot_r = nc.alloc_sbuf_tensor_at("onehot_r", [P, 2, 3, P], F32R, offset=small_at)
        gate_high_r = nc.alloc_sbuf_tensor_at("gate_high_r", [P, T], F32R, offset=small_at + 4 * 6 * P)
        weighed_high = nc.alloc_sbuf_tensor_at("weighed_high", [P, 2, T], F32R, offset=small_at)
        weighed_low = nc.alloc_sbuf_tensor_at("weighed_low", [P, 2, T], F32R, offset=small_at + 4 * 2 * T)

        class Region:

            def __init__(self, at=0, within=None):
                self.at, self.within = at, big if within is None else within
                self.size = self.within.shape[1]

            def take(self, floats, pattern=None, dt=F32, **sizes):
                ap = self.within[:, self.at:self.at + floats]
                self.at += floats
                assert self.at <= self.size, self.at
                if dt is not F32:
                    ap = ap.bitcast(dt)
                return ap.rearrange(pattern, **sizes) if pattern else ap

        r1 = Region()
        o1 = r1.take(TT * D, "p (i d) -> p i d", i=TT)
        q1 = r1.take(16 * T, "p (c t) -> p c t", c=16)
        k1 = r1.take(5 * T, "p (c t) -> p c t", c=5)
        v1 = r1.take(TT * 384, "p (i c) -> p i c", i=TT)
        gate1 = r1.take(TT * GATES, "p (i h b) -> p i h b", i=TT, b=3)
        bias1 = Region(within=act_place).take(2 * HEADS * T, "p (h y) -> p h y", y=T)
        cbias = r1.take(TT * HEADS * CMP_PAD, "p (i h c) -> p i h c", i=TT, c=CMP_PAD)
        cmp_w1_at = r1.at
        cmp_w1 = r1.take(2 * CMP_LEN * P, "p (v l n) -> p v l n", v=2, n=P)
        cmp_w2 = r1.take(2 * DH, "p (v n) -> p v n", v=2)
        cmp_pos = r1.take(2 * CMP_LEN, "p (v l) -> p v l", v=2)
        cmp_in = r1.take(2 * CMP_LEN * CMP_PAD, "p (v l c) -> p v l c", v=2, c=CMP_PAD)
        cmp_hid = r1.take(2 * 2 * CMP_PAD, "p (g v c) -> p g v c", g=2, v=2)
        cmp_k = r1.take(CMP_PAD)
        block_of = r1.take(GROUP_HEADS)
        valid_c = r1.take(TT * CMP_PAD, "p (i c) -> p i c", i=TT)
        gate_w = r1.take(KT * GATES, "p (k n) -> p k n", k=KT)
        buckets = r1.take(P)

        def attention_buffers(region):
            return (region.take(2 * 386, "p (b n) -> p b n", b=2), region.take(2 * 384, "p (b n) -> p b n", b=2),
                    region.take(N), region.take(2 * UNITS), region.take(2 * UNITS))

        r1_tables = Region(r1.at)
        onehot_rev = r1_tables.take(3 * P)
        onehot_cmp = r1_tables.take(T - CMP_FIRST)
        by_distance = r1_tables.take(3 * P)
        logits1, probs_t1, share1, negmax1, expsum1 = attention_buffers(r1)
        r1_cmp = Region(cmp_w1_at)
        cmp_hid8 = [r1_cmp.take(GROUP_HEADS * CMP_PAD, "p (h c) -> p h c", c=CMP_PAD) for _ in range(2)]
        cmp_v = r1_cmp.take(2 * N, "p (g n) -> p g n", g=2)
        cmp_logits = r1_cmp.take(2 * TT * GROUP_HEADS * CMP_PAD, "p (g i h c) -> p g i h c", g=2, i=TT, c=CMP_PAD)
        cmp_probs_t = r1_cmp.take(4 * P, "p (n q) -> p n q", q=P)
        cmp_stat = r1_cmp.take(4 * 32, "p (k n) -> p k n", k=4)

        r2 = Region()
        peer_q = r2.take(16 * T, "p (c t) -> p c t", c=16)
        subkeys = r2.take(2 * P, "p (s n) -> p s n", s=2)
        scores = r2.take(TT * 16 * P, "p (r n) -> p r n", n=P)
        scores_left = r2.take(TT * 16 * P, "p (r n) -> p r n", n=P)
        top = r2.take(TT * 16 * TOPK, "p (r k) -> p r k", k=TOPK)
        top_at = r2.take(TT * 16 * TOPK, "p (r k) -> p r k", dt=U32, k=TOPK)
        top_key = r2.take(TT * 16 * TOPK, "p (r k) -> p r k", k=TOPK)
        pairs = r2.take(TT * PEER_HEADS * TOPK * TOPK, "p (r n) -> p r n", n=TOPK * TOPK)
        pairs_left = scores.rearrange("p r n -> p (r n)").rearrange("p (r n) -> p r n", n=TOPK * TOPK)
        best = r2.take(TT * PEER_HEADS * TOPK, "p (r k) -> p r k", k=TOPK)
        best_at = r2.take(TT * PEER_HEADS * TOPK, "p (r k) -> p r k", dt=U32, k=TOPK)
        part_at = r2.take(2 * TT * PEER_HEADS * TOPK, "p (s r) -> p s r", dt=U32, s=2)
        part = r2.take(2 * TT * PEER_HEADS * TOPK, "p (s r) -> p s r", s=2)
        is_part = scores_left.rearrange("p r n -> p (r n)").rearrange("p (r a) -> p r a", a=TOPK)
        picked = r2.take(3 * TT * P, "p (s i k) -> p s i k", s=3, k=P)
        best_sum = r2.take(2 * TT * PEER_HEADS, "p (s r) -> p s r", s=2)

        r3 = Region()
        gates_out = r3.take(2 * EXPERT_TILES * QUARTER, "p (b e t) -> p b e t", b=2, t=QUARTER)
        gates_in = r3.take(2 * T, "p (q e t) -> p q e t", q=T // QUARTER, e=2)
        hidden = r3.take(2 * T, "p (b t) -> p b t", b=2)
        weighed = r3.take(2 * T, "p (b t) -> p b t", b=2)
        onehots = [[onehot_r[:, b, s, :] for s in range(3)] for b in range(2)]
        final_gain = big[:, 0:D]
        gates_dram = nc.dram_tensor("gates_dram", [T // QUARTER, P, EXPERT_TILES, QUARTER], F32)

        r4 = Region(D)
        qk2 = r4.take(TT * D, "p (i c) -> p i c", i=TT)
        o2 = qk2
        x_tok_at = r4.at
        qk_t = r4.take(16 * T, "p (c t) -> p c t", c=16)
        vz2 = r4.take(TT * D, "p (i c) -> p i c", i=TT)
        qkvz_half = [qk2, vz2]
        xbc_raw_at = r4.at
        xbc_raw = r4.take(XBC_TILES * T, "p (c t) -> p c t", c=XBC_TILES)
        xbc = r4.take(XBC_TILES * T, "p (c t) -> p c t", c=XBC_TILES)
        dt_w = r4.take(KT * SSM_HEADS, "p (k n) -> p k n", k=KT)
        causal = r4.take(T)
        logits2, probs_t2, share2, negmax2, expsum2 = attention_buffers(r4)
        dt_ = r4.take(4 * TT * SSM_HEADS, "p (k n) -> p k n", k=4)
        dt_tmp = r4.take(3 * TT * SSM_HEADS, "p (k n) -> p k n", k=3)
        x_tok = Region(x_tok_at).take(TT * SSM_W, "p (i c) -> p i c", i=TT)
        r4_scan = Region(xbc_raw_at)
        x_dt = r4_scan.take(TT * SSM_W, "p (i c) -> p i c", i=TT)
        cb = r4_scan.take(SSM_GROUPS * 3 * P, "p (g n) -> p g n", g=SSM_GROUPS)
        r4_act = Region(within=act_place)
        decay = r4_act.take(3 * SSM_HEADS * P, "p (b h l) -> p b h l", b=3, h=SSM_HEADS)
        la_triu = r4_act.take(SSM_HEADS * P)
        squares = big[:, 0:D]
        norm2_rows, norm3_rows, norm4_rows = o1, o2, o2

        taps = picked_place
        TURN0 = [8 * n for n in range(8)]
        BIAS_ROW = 2 * HEADS * 3 * P
        bias_dram = nc.dram_tensor("bias_by_distance", [BIAS_ROW], F32)
        bias_copies = nc.dram_tensor("bias_by_distance_copies", [P, BIAS_ROW], F32)

        CONSTS = [(ident, "c_ident"), (gains, "gains"), (ones, "c_ones"), (iota, "c_iota"), (triu, "c_triu"),
                  (low_mask, "c_low_mask"), (conv1, "conv1"), (conv2, "conv2"), (rows, "rows")]
        STAGE1 = [(buckets[0:BUCKETS + 2, 0:2 * HEADS], "bias_rows"), (onehot_rev[0:BUCKETS + 2, :], "c_onehot_rev"),
                  (onehot_cmp[0:BUCKETS + 2, :], "c_onehot_cmp"), (gate_w, "gate_w"), (cmp_w1, "cmp_w1"),
                  (cmp_w2, "cmp_w2"), (cmp_pos, "cmp_pos"), (block_of, "c_block_of"), (valid_c, "c_valid")]
        STAGE4 = [(dt_w, "dt_w"), (causal, "c_causal")]
        CONST_DMAS, STAGE1_DMAS, STAGE4_DMAS = 16 * len(CONSTS), 16 * len(STAGE1), 16 * len(STAGE4)

        x_landed = sem("x_landed")
        consts_landed = sem("consts_landed")
        stage1_landed = sem("stage1_landed")
        bias_stored = sem("bias_stored")
        bias_spread = sem("bias_spread")
        bias_landed = sem("bias_landed")
        subkeys_landed = sem("subkeys_landed")
        final_gain_landed = sem("final_gain_landed")
        stage4_landed = sem("stage4_landed")
        out_stored = sem("out_stored")
        raw_landed = [sem(f"raw_landed{r}") for r in range(RAW)]
        high_ready = [sem(f"high_ready{b}") for b in range(SPLIT)]
        low_ready = [sem(f"low_ready{b}") for b in range(SPLIT)]
        half_used = [sem(f"half_used{b}") for b in range(SPLIT)]
        pair_copied = [sem(f"pair_copied{b}") for b in range(2)]
        squared = sem("squared")
        scaled = sem("scaled")
        turned = sem("turned")
        turned_copied = sem("turned_copied")
        tables_done = sem("tables_done")
        tables_copied = sem("tables_copied")
        narrow_split = sem("narrow_split")
        small_done = sem("small_done")
        small_copied = sem("small_copied")
        cmp_pe = sem("cmp_pe")
        cmp_dve = sem("cmp_dve")
        cmp_act = sem("cmp_act")
        cmp_shifted = sem("cmp_shifted")
        scores_done = sem("scores_done")
        logits_written = sem("logits_written")
        logits_ready = sem("logits_ready")
        probs_ready = sem("probs_ready")
        probs_turned = sem("probs_turned")
        probs_copied = sem("probs_copied")
        mixed = sem("mixed")
        set_copied = sem("set_copied")
        subkey_scores_done = sem("subkey_scores_done")
        subkey_scores_copied = sem("subkey_scores_copied")
        best_ready = sem("best_ready")
        best_exp = sem("best_exp")
        picked_ready = sem("picked_ready")
        picked_turned = sem("picked_turned")
        picked_copied = sem("picked_copied")
        onehots_ready = sem("onehots_ready")
        gates_done = [sem(f"gates_done{b}") for b in range(2)]
        gates_copied = [sem(f"gates_copied{b}") for b in range(2)]
        gates_stored = [sem(f"gates_stored{b}") for b in range(2)]
        gates_loaded = sem("gates_loaded")
        weighed_high_ready = [sem(f"weighed_high_ready{e}") for e in range(2)]
        weighed_low_ready = [sem(f"weighed_low_ready{e}") for e in range(2)]
        ff_high_ready = [sem(f"ff_high_ready{b}") for b in range(2)]
        ff_product_ready = [sem(f"ff_product_ready{b}") for b in range(2)]
        gelu_done = [sem(f"gelu_done{e}") for e in range(2)]
        weighed_ready = [sem(f"weighed_ready{e}") for e in range(2)]
        shares_done = sem("shares_done")
        share_added = [sem(f"share_added{o}") for o in range(8)]
        normed = sem("normed")
        scan_pe = sem("scan_pe")
        scan_dve = sem("scan_dve")
        scan_act = sem("scan_act")
        tap_done = [sem(f"tap_done{b}") for b in range(2)]
        conv_done = [sem(f"conv_done{b}") for b in range(2)]
        silu_done = [sem(f"silu_done{b}") for b in range(2)]
        hidden_ready = [sem(f"hidden_ready{b}") for b in range(2)]
        conv_step = [sem(f"conv_step{b}") for b in range(2)]
        root_wanted = sem("root_wanted")
        root_done = sem("root_done")
        dve_step = sem("dve_step")
        act_step = sem("act_step")

        PRIMED = 1

        def prime(eng, semaphores):
            for semaphore in semaphores:
                eng.sem_inc(semaphore, PRIMED)

        ROOTS = [0, 1, 2, 3, "heads 0", "heads 1", "scan", 5]
        quads, groups = {}, {}
        n_quads, n_groups = 0, 0
        for name, tiles, n in STREAM:
            quads[name], groups[name] = n_quads, n_groups
            n_quads += tiles // 4
            n_groups += n

        def half(name, p, quad=0):
            q, p = quad + (quads[name] + p // QUAD), p % QUAD
            return p % SPLIT, p // 2 % RAW, p % 2, 2 * q + p // 4

        def down_half(p, g=0):
            g, p = g + p // DOWN_HALVES, p % DOWN_HALVES
            b, r, used = p % SPLIT, p // 2 % RAW, 2 * quads["w_down_2_t"]
            return b, r, p % 2, used + g * DOWN_USES[b] + p // 4

        def pair(name, g):
            return (groups[name] + g) % 2, (groups[name] + g) // 2

        EXPERT_STEPS = EXPERT_TILES // 2
        DOWN_TILES = FF_TILES // 4
        DOWN_HALVES = 2 * DOWN_TILES
        DOWN_USES = [6, 6, 5, 5]
        DOWN_LOADS = [6, 5]

        def wait_pairs(eng, name):
            n = next(n for which, _, n in STREAM if which == name)
            for g in (n - 2, n - 1):
                b, used = pair(name, g)
                eng.wait_ge(pair_copied[b], 2 * (used + 1) + PRIMED)

        def row(ap, n):
            return ap.unsqueeze(len(ap.shape)).to_broadcast([*ap.shape, n])

        def copies(ap, n, at=1):
            shape = list(ap.shape)
            return ap.unsqueeze(at).to_broadcast([*shape[:at], n, *shape[at:]])

        class Steps:

            def __init__(self, eng, semaphore):
                self.eng, self.semaphore, self.n = eng, semaphore, 0

            def note(self, instruction):
                instruction.then_inc(self.semaphore, 1)
                self.n += 1

            def settle(self):
                self.eng.wait_ge(self.semaphore, self.n)

            def link(self, instruction):
                self.note(instruction)
                self.settle()

        units1 = []
        for branch in range(3):
            for h in range(HEADS):
                g, c = h // GROUP_HEADS, h % GROUP_HEADS
                part_of = slice(DH * g, DH * g + DH)
                units1.append(dict(
                    q=q1[part_of, c + (8 if branch == 2 else 0), :], k=k1[part_of, branch, :],
                    v=[v1[:, i, P * branch + DH * g:P * branch + DH * g + DH] for i in range(TT)],
                    bias=bias1[:, h + (HEADS if branch == 2 else 0), :], scale=DH ** -0.5,
                    sink=rows[:, 0, h:h + 1] if branch == 2 else None, width=DH,
                    set=2 * branch + g, at=DH * c))
        units2 = [dict(q=qk_t[:, h, :], k=qk_t[:, HEADS2 + h, :],
                       v=[qkvz_half[1][:, i, DH2 * h:DH2 * h + DH2] for i in range(TT)],
                       bias=causal, scale=DH2 ** -0.5, sink=None, width=DH2, set=6 + h // 4, at=DH2 * (h % 4))
                  for h in range(HEADS2)]
        attention1 = dict(units=units1, first=0, logits=logits1, probs_t=probs_t1, negmax=negmax1, expsum=expsum1)
        attention2 = dict(units=units2, first=UNITS, logits=logits2, probs_t=probs_t2, negmax=negmax2, expsum=expsum2)

        block = ctx.enter_context(nc.Block())

        @block.sync
        def _(sp):
            def load(name, tile, r, used):
                sp.wait_ge(low_ready[2 * r + 1], used + PRIMED)
                sp.dma_start(raw[r][:, :], ins[name][bass.ds(tile, 1)].rearrange("a p n -> p (a n)")
                             ).then_inc(raw_landed[r], 16)

            for i in range(TT):
                sp.dma_start(resid[:, i, :], ins["x"][0, i * P:(i + 1) * P, :]).then_inc(x_landed, 16)
            for name, tiles, _ in STREAM[:-1]:
                with sp.Fori(0, tiles // 4) as n:
                    for t in range(4):
                        if name == "experts_t" and t == 2:
                            sp.wait_ge(weighed_ready[1], n + PRIMED)
                            sp.wait_ge(gates_stored[0], 16 * 2)
                            sp.wait_ge(gates_stored[1], 16 * 2)
                            sp.dma_start(gates_in, gates_dram[:, :, bass.ds(2 * n, 2), :].rearrange(
                                "q p e t -> p q e t")).then_inc(gates_loaded, 16)
                        load(name, n * 4 + t, t % RAW, n * 2 + (2 * quads[name] + t // 2))
            name = "w_down_2_t"
            with sp.Fori(0, 4) as g:
                for t in range(DOWN_TILES):
                    r = t % RAW
                    load(name, g * DOWN_TILES + t, r, g * DOWN_LOADS[r] + (2 * quads[name] + t // 2))
            for g in range(4):
                b, used = pair(name, g)
                sp.wait_ge(pair_copied[b], 2 * (used + 1) + PRIMED)
                sp.dma_start(out[0].rearrange("(i p) d -> p i d", p=P)[:, :, N * g:N * (g + 1)],
                             resid[:, :, N * g:N * (g + 1)]).then_inc(out_stored, 16)
            sp.wait_ge(out_stored, 16 * 4)

        @block.tensor
        def _(pe):
            prime(pe, [*half_used, *gates_done, shares_done])

            def mm(out_, lhs_t, rhs, start=True, stop=True):
                return pe.matmul(out_, lhs_t, rhs, start=start, stop=stop, skip_group_check=True)

            def mm3(out_, lhs_t, rhs, start, stop):
                mm(out_, lhs_t[0], rhs[0], start=start, stop=False)
                mm(out_, lhs_t[0], rhs[1], start=False, stop=False)
                return mm(out_, lhs_t[1], rhs[0], start=False, stop=stop)

            def parts(pair_, *at):
                return [ap[at] for ap in pair_]

            def take(h):
                b, _, _, used = h
                pe.wait_ge(low_ready[b], used + 1 + PRIMED)
                return [ap[:, :].rearrange("p (k n) -> p k n", k=2) for ap in (high[b], low[b])]

            def product(b, halves, lhs, stationary_weights):
                every = slice(None)
                for p, h in enumerate(halves):
                    w = take(h)
                    for k in range(2):
                        kt = 2 * p + k
                        first, last = kt == 0, kt == 2 * len(halves) - 1
                        if stationary_weights:
                            for n in range(stationary_weights):
                                m = mm3(bank[:, 2 * b + n // 2, T * (n % 2):T * (n % 2) + T],
                                        parts(w, every, k, slice(P * n, P * n + P)), parts(lhs, every, kt, every),
                                        start=first and n % 2 == 0, stop=last)
                        else:
                            for t in range(TT):
                                m = mm3(bank[:, 2 * b + t, :], parts(lhs, every, kt, slice(P * t, P * t + P)),
                                        parts(w, every, k, every), start=first, stop=last)
                    m.then_inc(half_used[h[0]], 1)

            def product_group(name, g, i=0, stationary_weights=4):
                b, used = pair(name, g)
                pe.wait_ge(pair_copied[b], i * 2 + 2 * used + PRIMED)
                product(b, [half(name, p, i * 2 + g) for p in range(QUAD)], (act_high, act_low), stationary_weights)

            def product_loop(name, steps, stationary_weights=4):
                with pe.Fori(0, steps) as i:
                    for j in range(2):
                        product_group(name, j, i, stationary_weights)

            def turn(n, src):
                for b in range(8):
                    i, quarter = b // 4, b % 4
                    if b % 4 == 0:
                        pe.wait_ge(scaled, TT * n + i + 1)
                    if TURN0[n] + b >= 4:
                        pe.wait_ge(turned_copied, TURN0[n] + b - 3)
                    for j in range(4):
                        c = 4 * quarter + j
                        m = pe.transpose(bank[:, 4 + b % 4, P * j:P * j + P], src[:, i, P * c:P * c + P], ident[:, :])
                    m.then_inc(turned, 1)

            def attention(a):
                units, first = a["units"], a["first"]

                def scores(n):
                    u, b = units[n], (first + n) % 2
                    if first + n >= 2:
                        pe.wait_ge(logits_ready, 2 * (first + n - 1))
                    mm(bank[:, b, 0:T], u["q"][:, P:T], u["k"][:, 0:T])
                    mm(bank[:, b, T:T + P], u["q"][:, 0:P], u["k"][:, 0:P]).then_inc(scores_done, 1)

                def turn_probs(n):
                    b = (first + n) % 2
                    pe.wait_ge(probs_ready, 2 * (first + n + 1))
                    if first + n >= 2:
                        pe.wait_ge(probs_copied, first + n - 1)
                    for k, at in enumerate((0, P, T + 1)):
                        m = pe.transpose(bank[:, 2 + b, P * k:P * k + P], a["logits"][:, b, at:at + P], ident[:, :])
                    m.then_inc(probs_turned, 1)

                def mix(n):
                    u, b = units[n], (first + n) % 2
                    o, w, at = 4 + 2 * (u["set"] % 2), u["width"], u["at"]
                    pt = a["probs_t"][:, b, :]
                    pe.wait_ge(probs_copied, first + n + 1)
                    if at == 0 and u["set"] >= 2:
                        pe.wait_ge(set_copied, 2 * (u["set"] - 1))
                    mm(bank[:, o + 1, at:at + w], pt[:, 0:P], u["v"][0], stop=False)
                    mm(bank[:, o + 1, at:at + w], pt[:, P:T], u["v"][1], start=False)
                    mm(bank[:, o, at:at + w], pt[:, T:T + P], u["v"][0]).then_inc(mixed, 1)

                scores(0)
                for n in range(len(units) + 1):
                    if n + 1 < len(units):
                        scores(n + 1)
                    if n < len(units):
                        turn_probs(n)
                    if n >= 1:
                        mix(n - 1)

            pe.wait_ge(stage1_landed, STAGE1_DMAS)
            mm(bank[0:2 * HEADS, 0, 0:3 * P], buckets[0:BUCKETS + 2, 0:2 * HEADS], onehot_rev[0:BUCKETS + 2, :])
            for i in range(TT):
                for c in range(CMP_PAD):
                    at = P * i - CMP_STRIDE * c - CMP_LEN + 1 - CMP_FIRST
                    m = mm(bank[:, 1, HEADS * (CMP_PAD * i + c):HEADS * (CMP_PAD * i + c + 1)],
                           onehot_cmp[0:BUCKETS + 2, at:at + P], buckets[0:BUCKETS + 2, 0:HEADS])
            m.then_inc(tables_done, 1)

            pe.wait_ge(x_landed, 16 * TT)
            pe.wait_ge(consts_landed, CONST_DMAS)
            turn(0, o1)
            pe.wait_ge(turned_copied, TURN0[1])
            pe.wait_ge(tables_copied, 2)
            product_loop("w_in_t", 2)
            product_group("w_in_t", 4)
            b, used = pair("w_in_t", 5)
            pe.wait_ge(pair_copied[b], 2 * used + PRIMED)
            pe.wait_ge(turned_copied, TURN0[1])
            every = slice(None)
            acts = (act_high, act_low)
            for p in range(QUAD):
                h = half("w_in_t", p, 5)
                w = take(h)
                for k in range(2):
                    kt, first, last = 2 * p + k, p == 0 and k == 0, p == QUAD - 1 and k == 1
                    mm3(bank[:, 4, 0:T], parts(w, every, k, slice(0, P)), parts(acts, every, kt, every), first, last)
                    for t in range(TT):
                        m = mm3(bank[:, 2 * b + t, 0:3 * P], parts(acts, every, kt, slice(P * t, P * t + P)),
                                parts(w, every, k, slice(P, N)), first, last)
                m.then_inc(half_used[h[0]], 1)
            pe.wait_ge(narrow_split, 2)
            for t in range(TT):
                for kt in range(KT):
                    m = mm3(bank[:, 5 + t, 0:GATES], parts(acts, every, kt, slice(P * t, P * t + P)),
                            parts(narrow_w, every, slice(GATES * kt, GATES * kt + GATES)), kt == 0, kt == KT - 1)
            m.then_inc(small_done, 1)

            pe.wait_ge(small_copied, 1)
            pe.wait_ge(cmp_dve, 2)
            for g in range(2):
                part_of = slice(DH * g, DH * g + DH)
                for v in range(2):
                    for l in range(CMP_LEN):
                        m = mm(bank[:, 6 + g, CMP_PAD * v:CMP_PAD * v + N_CMP], cmp_w1[part_of, v, l, :],
                               cmp_in[part_of, v, l, 0:N_CMP], start=l == 0, stop=l == CMP_LEN - 1)
            m.then_inc(cmp_pe, 1)
            pe.wait_ge(cmp_act, 1)
            for g in range(2):
                m = mm(bank[DH * g:DH * g + DH, 4, 0:CMP_PAD], cmp_w2[:, 0, :], cmp_hid[:, g, 0, :])
            m.then_inc(cmp_pe, 1)
            for g in range(2):
                pe.wait_ge(cmp_dve, 3 + g)
                m = mm(bank[:, 5, DH * g:DH * g + DH], cmp_hid8[g][:, :, :].rearrange("p h c -> p (h c)"), cmp_w2[:, 1, :])
            m.then_inc(cmp_pe, 1)
            pe.wait_ge(cmp_dve, 5)
            for g in range(2):
                part_of = slice(DH * g, DH * g + DH)
                for i in range(TT):
                    for h in range(GROUP_HEADS):
                        at = CMP_PAD * (GROUP_HEADS * i + h)
                        m = mm(bank[:, 6 + g, at:at + CMP_PAD], q1[part_of, h, P * i:P * i + P], cmp_k[part_of, :])
            m.then_inc(cmp_pe, 1)
            pe.wait_ge(cmp_dve, 6)
            for g in range(2):
                for i in range(TT):
                    m = pe.transpose(bank[:, 4, P * (2 * g + i):P * (2 * g + i) + P],
                                     cmp_logits[:, g, i, :, :].rearrange("p h c -> p (h c)"), ident[:, :])
            m.then_inc(cmp_pe, 1)
            pe.wait_ge(cmp_dve, 7)
            for g in range(2):
                for i in range(TT):
                    m = mm(bank[:, 2 * i + g, :], cmp_probs_t[:, 2 * g + i, :], cmp_v[:, g, :])
            m.then_inc(cmp_pe, 1)

            pe.wait_ge(cmp_dve, 8)
            attention(attention1)
            turn(1, o1)
            pe.wait_ge(turned_copied, TURN0[2])
            product_loop("w_out_t", 2, stationary_weights=0)

            turn(2, norm2_rows)
            pe.wait_ge(turned_copied, TURN0[3])
            product_loop("peer_wq_t", 2)
            pe.wait_ge(subkeys_landed, 16)
            wait_pairs(pe, "peer_wq_t")
            for n in range(8):
                if n >= 4:
                    pe.wait_ge(subkey_scores_copied, n - 3)
                for j in range(4):
                    r = 4 * n + j
                    i, c = r // 16, r % 16
                    m = mm(bank[:, 4 + n % 4, P * j:P * j + P], peer_q[:, c, P * i:P * i + P], subkeys[:, c % 2, :])
                m.then_inc(subkey_scores_done, 1)
            pe.wait_ge(picked_ready, 1)
            pe.wait_ge(subkey_scores_copied, 8)
            for s in range(3):
                for i in range(TT):
                    n = 2 * s + i
                    m = pe.transpose(bank[:, 4 + n // 4, P * (n % 4):P * (n % 4) + P], picked[:, s, i, :], ident[:, :])
            m.then_inc(picked_turned, 1)
            with pe.Fori(0, T // 8) as n:
                for j in range(8):
                    if j % 4 == 0:
                        pe.wait_ge(gates_copied[j // 4], n + PRIMED)
                    pe.wait_ge(onehots_ready, 8 * n + j + 1)
                    second, first_high, first_low = onehots[j % 2]
                    mm(bank[:, 6 + j // 4, P * (j % 4):P * (j % 4) + P], second, first_high, stop=False)
                    mm(bank[:, 6 + j // 4, P * (j % 4):P * (j % 4) + P], second, first_low, start=False
                       ).then_inc(gates_done[j % 2], 1)

            for b in range(2):
                pe.wait_ge(gates_copied[b], T // 8 + PRIMED)
            with pe.Fori(0, EXPERT_STEPS) as n:
                for e in range(2):
                    pe.wait_ge(gelu_done[e], n + PRIMED)
                    for p in (2 * e, 2 * e + 1):
                        h = half("experts_t", p, n)
                        b = h[0]
                        pe.wait_ge(low_ready[b], h[3] + 1 + PRIMED)
                        for k in range(KT // 2):
                            kt = KT // 2 * (p % 2) + k
                            m = mm3(bank[:, e, 0:T], parts((high[b], low[b]), every, slice(P * k, P * k + P)),
                                    parts(acts, every, kt, every), kt == 0, kt == KT - 1)
                        m.then_inc(half_used[b], 1)
                for columns in range(2):
                    for e in range(2):
                        h = half("experts_t", 4 + 2 * columns + e, n)
                        b = h[0]
                        if columns == 0:
                            pe.wait_ge(weighed_low_ready[e], n + 1)
                        pe.wait_ge(low_ready[b], h[3] + 1 + PRIMED)
                        for c in range(4):
                            o = 4 * columns + c
                            t, at = c // 2, N * (c % 2)
                            if e == 0:
                                before = {0: 6, 1: 7, 6: 0, 7: 1}.get(o, o)
                                pe.wait_ge(share_added[before], n + (1 if o >= 6 else 0) + PRIMED)
                            m = mm3(bank[:, 2 + o % 6, :], parts((weighed_high, weighed_low), every, e, slice(P * t, P * t + P)),
                                    parts((high[b], low[b]), every, slice(at, at + N)), e == 0, e == 1)
                            if e == 1 and c < 3:
                                m.then_inc(shares_done, 1)
                        m.then_inc(half_used[b], 1)

            turn(3, norm3_rows)
            pe.wait_ge(turned_copied, TURN0[4])
            product_loop("w_in_2_t", 4, stationary_weights=0)
            for g in range(8, 11):
                product_group("w_in_2_t", g)
            pe.wait_ge(narrow_split, 4)
            for t in range(TT):
                for kt in range(KT):
                    m = mm3(bank[:, 6 + t, 0:SSM_HEADS], parts(acts, every, kt, slice(P * t, P * t + P)),
                            parts(narrow_w, every, slice(SSM_HEADS * kt, SSM_HEADS * (kt + 1))), kt == 0, kt == KT - 1)
            m.then_inc(small_done, 1)
            pe.wait_ge(small_copied, 2)
            turn(4, qkvz_half[0])
            pe.wait_ge(turned_copied, TURN0[5])
            attention(attention2)

            pe.wait_ge(scan_act, 1)
            pe.wait_ge(set_copied, 2 * 8)
            for n in range(4):
                i = n // 2
                for j in range(4):
                    m = pe.transpose(bank[:, 4 + n, P * j:P * j + P], xbc[:, 4 * (n % 2) + j, P * i:P * i + P], ident[:, :])
            m.then_inc(scan_pe, 1)
            for g in range(SSM_GROUPS):
                mm(bank[:, g, 0:T], xbc[:, 8 + g, 0:P], xbc[:, 10 + g, :])
                m = mm(bank[:, g, T:T + P], xbc[:, 8 + g, P:T], xbc[:, 10 + g, P:T])
            m.then_inc(scan_pe, 1)
            pe.wait_ge(scan_dve, 1)
            mm(bank[:, 2, 0:TT * SSM_HEADS], triu[:, :], dt_[:, 1, :])
            mm(bank[:, 3, 0:SSM_HEADS], ones[:, :], dt_[:, 1, 0:SSM_HEADS]).then_inc(scan_pe, 1)
            for i in range(TT):
                pe.wait_ge(scan_dve, 2 + i)
                for c in range(4):
                    m = mm(bank[:, 4 + c, :], ones[:, :], la_triu[:, N * c:N * c + N])
                m.then_inc(scan_pe, 1)
            pe.wait_ge(scan_dve, 4)
            for g in range(SSM_GROUPS):
                for j in range(GROUP_HEADS):
                    h = GROUP_HEADS * g + j
                    cols = slice(SSM_DH * j, SSM_DH * j + SSM_DH)
                    xs = [x_dt[:, i, SSM_DH * h:SSM_DH * h + SSM_DH] for i in range(TT)]
                    mm(bank[:, g, cols], decay[:, 0, h, :], xs[0])
                    mm(bank[:, 2 + g, cols], decay[:, 2, h, :], xs[0], stop=False)
                    m = mm(bank[:, 2 + g, cols], decay[:, 1, h, :], xs[1], start=False)
            m.then_inc(scan_pe, 1)
            turn(5, o2)
            pe.wait_ge(turned_copied, TURN0[6])
            product_loop("w_out_2_t", 2, stationary_weights=0)

            turn(6, norm4_rows)
            pe.wait_ge(turned_copied, TURN0[7])
            product_loop("w_up_2_t", FF_GROUPS // 2)
            for j in range(2):
                pe.wait_ge(hidden_ready[j], FF_GROUPS // 2 + PRIMED)
            with pe.Fori(0, 2) as i:
                for j in range(2):
                    b, used = pair("w_down_2_t", j)
                    pe.wait_ge(pair_copied[b], i * 2 + 2 * used + PRIMED)
                    product(b, [down_half(p, i * 2 + j) for p in range(DOWN_HALVES)], (ff_high, ff_low), 0)

        @block.vector
        def _(dve):
            prime(dve, [*low_ready, *pair_copied, *share_added, *weighed_ready, *hidden_ready])
            steps = Steps(dve, dve_step)
            link, note, settle = steps.link, steps.note, steps.settle

            def rms_scale(e, n_features):
                at = stat[:, 4 * e + 2:4 * e + 4]
                link(dve.tensor_scalar(at, stat[:, 4 * e:4 * e + 2], 1.0 / n_features, EPS, ALU.mult, ALU.add))
                dve.reciprocal(at, at).then_inc(root_wanted, 1)
                dve.wait_ge(root_done, ROOTS.index(e) + 1)

            def scale_rows(e, dst):
                dve.wait_ge(squared, TT * (e + 1))
                rms_scale(e, D)
                for i in range(TT):
                    dve.tensor_scalar(dst[:, i, :], resid[:, i, :], stat[:, 4 * e + 2 + i:4 * e + 3 + i], None,
                                      ALU.mult).then_inc(scaled, 1)

            def as_f32(ap):
                return ap.bitcast(F32)

            def split_low(h):
                b, r, which, used = h
                dve.wait_ge(high_ready[b], used + 1)
                dve.tensor_tensor(low[b][:, :], raw[r][:, HALF * which:HALF * (which + 1)], as_f32(high[b][:, :]),
                                  ALU.subtract).then_inc(low_ready[b], 1)

            def split_turned(n):
                for b in range(8):
                    i, c = b // 4, 4 * (b % 4)
                    dve.wait_ge(turned, TURN0[n] + b + 1)
                    blocks = bank[:, 4 + b % 4, :].rearrange("p (c t) -> p c t", c=4)
                    to = act_high[:, c:c + 4, P * i:P * i + P]
                    link(dve.tensor_tensor(to, blocks, row(gains[:, n, c:c + 4], P), ALU.mult))
                    for k in range(4):
                        m = dve.scalar_tensor_tensor(act_low[:, c + k, P * i:P * i + P], blocks[:, k, :], gains[:, n, c + k:c + k + 1],
                                                     as_f32(act_high[:, c + k, P * i:P * i + P]), ALU.mult, ALU.subtract)
                    m.then_inc(turned_copied, 1)

            def copy_turned(n, dst):
                for b in range(8):
                    i, c = b // 4, 4 * (b % 4)
                    dve.wait_ge(turned, TURN0[n] + b + 1)
                    dve.tensor_tensor(dst[:, c:c + 4, P * i:P * i + P],
                                      bank[:, 4 + b % 4, :].rearrange("p (c t) -> p c t", c=4),
                                      row(gains[:, n, c:c + 4], P), ALU.mult).then_inc(turned_copied, 1)

            def group_done(name, g, i=0):
                for p in range(QUAD):
                    split_low(half(name, p + LOOKAHEAD, i * 2 + g))
                b, _, _, used = half(name, QUAD - 1, i * 2 + g)
                dve.wait_ge(half_used[b], used + 1 + PRIMED)
                return pair(name, g)[0]

            def copy_groups(name, g0, steps_, dst_of):
                with dve.Fori(0, steps_) as i:
                    for j in range(2):
                        b = group_done(name, g0 + j, i)
                        for k in range(2):
                            dve.tensor_copy(dst_of(i, j, k), bank[:, 2 * b + k, :]).then_inc(pair_copied[b], 1)

            def add_groups(name):
                with dve.Fori(0, 2) as i:
                    for j in range(2):
                        b = group_done(name, j, i)
                        for t in range(TT):
                            part_ = resid[:, t, bass.ds(i * 2 * N + j * N, N)]
                            dve.tensor_tensor(part_, bank[:, 2 * b + t, :], part_, ALU.add).then_inc(pair_copied[b], 1)

            def attention(a, set_done):
                units, first, logits = a["units"], a["first"], a["logits"]
                for n, u in enumerate(units):
                    g, b = first + n, (first + n) % 2
                    dve.wait_ge(scores_done, g + 1)
                    if g >= 2:
                        dve.wait_ge(probs_turned, g - 1)
                    at = logits[:, b, :]
                    dve.scalar_tensor_tensor(at[:, 0:T], bank[:, b, 0:T], u["scale"], u["bias"][:, 0:T],
                                             ALU.mult, ALU.add)
                    last = dve.scalar_tensor_tensor(at[:, T + 1:T + 1 + P], bank[:, b, T:T + P], u["scale"],
                                                    u["bias"][:, P:T], ALU.mult, ALU.add)
                    if u["sink"] is not None:
                        last = dve.tensor_copy(at[:, T:T + P + 2:P + 1], u["sink"].to_broadcast([P, 2]))
                    last.then_inc(logits_written, 1)
                    dve.wait_ge(logits_written, g + 1)
                    s = 0 if u["sink"] is None else 1
                    dve.tensor_reduce(a["negmax"][:, UNITS + n:UNITS + n + 1], at[:, 0:T + s], AX.X, ALU.max,
                                      negate=True).then_inc(logits_ready, 1)
                    dve.tensor_reduce(a["negmax"][:, n:n + 1], at[:, T + 1:T + 1 + P + s], AX.X, ALU.max,
                                      negate=True).then_inc(logits_ready, 1)
                    if n >= 2 and units[n - 2]["set"] != units[n - 1]["set"]:
                        set_done(n - 2)
                set_done(len(units) - 1)

            for p in range(LOOKAHEAD):
                split_low(half("w_in_t", p))
            dve.memset(cmp_hid[:, :, :, :], 0.0).then_inc(cmp_dve, 1)
            dve.wait_ge(tables_done, 1)
            dve.tensor_copy(by_distance[0:2 * HEADS, :], bank[0:2 * HEADS, 0, 0:3 * P]).then_inc(tables_copied, 1)
            dve.tensor_copy(cbias[:, :, :, :], bank[:, 1, :].rearrange("p (i c h) -> p i h c", i=TT, c=CMP_PAD)
                            ).then_inc(tables_copied, 1)

            dve.wait_ge(x_landed, 16 * TT)
            dve.wait_ge(consts_landed, CONST_DMAS)
            scale_rows(0, o1)
            split_turned(0)
            copy_groups("w_in_t", 0, 2, lambda i, j, k: q1[:, bass.ds(i * 8 + (4 * j + 2 * k), 2), :].rearrange("p c t -> p (c t)"))
            b = group_done("w_in_t", 4)
            for k in range(2):
                dve.tensor_copy(k1[:, 2 * k:2 * k + 2, :].rearrange("p c t -> p (c t)"), bank[:, 2 * b + k, :]).then_inc(pair_copied[b], 1)
            dve.wait_ge(narrow_split, 1)
            dve.tensor_tensor(narrow_w[1][:, :], gate_w.rearrange("p k n -> p (k n)"), as_f32(narrow_w[0][:, :]),
                              ALU.subtract).then_inc(narrow_split, 1)
            b = group_done("w_in_t", 5)
            for t in range(TT):
                dve.tensor_copy(v1[:, t, :], bank[:, 2 * b + t, 0:3 * P]).then_inc(pair_copied[b], 1)
            link(dve.tensor_copy(k1[:, 4, :], bank[:, 4, 0:T]))

            dve.wait_ge(stage1_landed, STAGE1_DMAS)
            for v in range(2):
                src = k1[:, 3 + v, :]
                blocks = bass.AP(tensor=src.tensor, offset=src.offset,
                                 ap=[list(src.ap[0]), [1, CMP_LEN], [CMP_STRIDE, N_CMP]])
                m = dve.tensor_tensor(cmp_in[:, v, :, 0:N_CMP], blocks, row(cmp_pos[:, v, :], N_CMP), ALU.add)
            m.then_inc(cmp_dve, 1)
            dve.wait_ge(cmp_act, 1)
            for g in range(2):
                dve.tensor_copy(cmp_hid8[g][:, :, :], copies(cmp_hid[:, g, 1, :], GROUP_HEADS)).then_inc(cmp_dve, 1)
            dve.wait_ge(cmp_pe, 3)
            for g in range(2):
                dve.tensor_tensor(cmp_v[:, g, :].rearrange("p (h d) -> p h d", h=GROUP_HEADS),
                                  copies(bank[:, 5, DH * g:DH * g + DH], GROUP_HEADS), row(block_of, DH), ALU.mult)
            dve.tensor_copy(cmp_k, bank[:, 4, 0:CMP_PAD]).then_inc(cmp_dve, 1)
            dve.wait_ge(cmp_pe, 4)
            rows_c = cmp_logits[:, :, :, :, :].rearrange("p g i h c -> p (g i h) c")
            for g in range(2):
                note(dve.scalar_tensor_tensor(
                    cmp_logits[:, g, :, :, :].rearrange("p i h c -> p i (h c)"),
                    bank[:, 6 + g, 0:T].rearrange("p (i n) -> p i n", i=TT), DH ** -0.5,
                    cbias[:, :, GROUP_HEADS * g:GROUP_HEADS * (g + 1), :].rearrange("p i h c -> p i (h c)"),
                    ALU.mult, ALU.add))
            settle()
            link(dve.tensor_reduce(cmp_stat[:, 0, :], rows_c, AX.X, ALU.max))
            dve.tensor_tensor(rows_c, rows_c, row(cmp_stat[:, 0, :], CMP_PAD), ALU.subtract).then_inc(cmp_shifted, 1)
            dve.wait_ge(cmp_act, 2)
            link(dve.tensor_reduce(cmp_stat[:, 1, :], rows_c, AX.X, ALU.add))
            link(dve.reciprocal(cmp_stat[:, 2, :], cmp_stat[:, 1, :]))
            dve.wait_ge(small_copied, 1)
            for g in range(2):
                note(dve.tensor_tensor(
                    cmp_stat[:, 3, 16 * g:16 * g + 16].rearrange("p (i h) -> p i h", i=TT),
                    cmp_stat[:, 2, 16 * g:16 * g + 16].rearrange("p (i h) -> p i h", i=TT),
                    gate1[:, :, GROUP_HEADS * g:GROUP_HEADS * (g + 1), 0], ALU.mult))
            for g in range(2):
                m = dve.tensor_tensor(cmp_logits[:, g, :, :, :], cmp_logits[:, g, :, :, :],
                                      copies(valid_c, GROUP_HEADS, at=2), ALU.mult)
            m.then_inc(cmp_dve, 1)
            dve.wait_ge(cmp_pe, 5)
            dve.tensor_copy(cmp_probs_t[:, :, :].rearrange("p n q -> p (n q)"), bank[:, 4, :]).then_inc(cmp_dve, 1)
            dve.wait_ge(cmp_pe, 6)
            settle()
            for g in range(2):
                for i in range(TT):
                    at = 16 * g + 8 * i
                    m = dve.tensor_tensor(o1[:, i, N * g:N * g + N].rearrange("p (h d) -> p h d", d=DH),
                                          bank[:, 2 * i + g, :].rearrange("p (h d) -> p h d", d=DH),
                                          row(cmp_stat[:, 3, at:at + 8], DH), ALU.mult)
            m.then_inc(cmp_dve, 1)

            dve.wait_ge(bias_landed, 16)

            def set_done1(n):
                u = units1[n]
                s, n0 = u["set"], n - GROUP_HEADS + 1
                branch, g = s // 2, s % 2
                dve.wait_ge(mixed, n + 1)
                dve.wait_ge(probs_ready, 2 * (n + 1))
                sums = expsum1.rearrange("p (i n) -> p i n", i=TT)[:, :, n0:n0 + GROUP_HEADS]
                dve.wait_ge(cmp_dve, 8)
                link(dve.reciprocal(sums, sums))
                if branch < 2:
                    link(dve.tensor_tensor(sums, sums, gate1[:, :, GROUP_HEADS * g:GROUP_HEADS * (g + 1), 1 + branch],
                                           ALU.mult))
                for i in range(TT):
                    at = N * (s - 2 if branch == 2 else g)
                    part_ = o1[:, i, at:at + N]
                    dst = part_ if branch == 2 else share1
                    dve.tensor_tensor(dst.rearrange("p (h d) -> p h d", d=DH),
                                      bank[:, 4 + 2 * (s % 2) + i, :].rearrange("p (h d) -> p h d", d=DH),
                                      row(sums[:, i, :], DH), ALU.mult).then_inc(set_copied, 1)
                    if branch < 2:
                        dve.wait_ge(set_copied, 2 * s + i + 1)
                        link(dve.tensor_tensor(part_, part_, share1, ALU.add))

            attention(attention1, set_done1)
            dve.wait_ge(set_copied, 2 * 6)
            for i in range(TT):
                dve.tensor_copy(stat[:, 60 + i:61 + i], o1[:, i, D - 1:D]).then_inc(scaled, 1)
            split_turned(1)
            add_groups("w_out_t")

            scale_rows(1, norm2_rows)
            split_turned(2)
            copy_groups("peer_wq_t", 0, 2, lambda i, j, k: peer_q[:, bass.ds(i * 8 + (4 * j + 2 * k), 2), :].rearrange("p c t -> p (c t)"))
            for n in range(8):
                dve.wait_ge(subkey_scores_done, n + 1)
                dve.tensor_copy(scores[:, 4 * n:4 * n + 4, :].rearrange("p r n -> p (r n)"), bank[:, 4 + n % 4, :]
                                ).then_inc(subkey_scores_copied, 1)
            dve.wait_ge(subkey_scores_copied, 8)

            def top16(n, src, left, values, at):
                for r in range(n):
                    note(dve.max(values[:, r, 0:8], src[:, r, :]))
                settle()
                for r in range(n):
                    note(dve.match_replace(left[:, r, :], values[:, r, 0:8], src[:, r, :], LOWEST))
                    note(dve.max_index(at[:, r, 0:8], values[:, r, 0:8], src[:, r, :]))
                settle()
                for r in range(n):
                    note(dve.max(values[:, r, 8:16], left[:, r, :]))
                settle()
                for r in range(n):
                    note(dve.max_index(at[:, r, 8:16], values[:, r, 8:16], left[:, r, :]))
                settle()

            top16(TT * 16, scores, scores_left, top, top_at)
            note(dve.tensor_copy(top_key.rearrange("p r k -> p (r k)"), top_at.rearrange("p r k -> p (r k)")))
            top_side = top.rearrange("p (r s) k -> p r s k", s=2)
            link(dve.tensor_tensor(pairs.rearrange("p r (a b) -> p r a b", a=TOPK), row(top_side[:, :, 0, :], TOPK),
                                   copies(top_side[:, :, 1, :], TOPK, at=2), ALU.add))
            top16(TT * PEER_HEADS, pairs, pairs_left, best, best_at)
            sub = picked[:, 2, :, :].rearrange("p i (h k) -> p (i h) k", k=TOPK)
            dve.tensor_tensor(sub, best, row(best[:, :, 0], TOPK), ALU.subtract).then_inc(best_ready, 1)
            flat_at = best_at.rearrange("p r k -> p (r k)")
            note(dve.tensor_scalar(part_at[:, 0, :], flat_at, 4, None, ALU.logical_shift_right))
            link(dve.tensor_scalar(part_at[:, 1, :], flat_at, TOPK - 1, None, ALU.bitwise_and))
            link(dve.tensor_copy(part.rearrange("p s r -> p (s r)"), part_at.rearrange("p s r -> p (s r)")))
            keys = top_key.rearrange("p (r s) k -> p r s k", s=2)
            for s in range(2):
                link(dve.tensor_tensor(is_part, row(part[:, s, :], TOPK), copies(iota[:, 0:TOPK], TT * P), ALU.is_equal))
                four = is_part.rearrange("p (r j) a -> p r j a", j=TOPK)
                link(dve.tensor_tensor(four, four, copies(keys[:, :, s, :], TOPK, at=2), ALU.mult))
                link(dve.tensor_reduce(picked[:, s, :, :].rearrange("p i k -> p (i k)"), is_part, AX.X, ALU.add))
            dve.wait_ge(best_exp, 1)
            link(dve.tensor_reduce(best_sum[:, 0, :], sub, AX.X, ALU.add))
            link(dve.reciprocal(best_sum[:, 1, :], best_sum[:, 0, :]))
            dve.tensor_tensor(sub, sub, row(best_sum[:, 1, :], TOPK), ALU.mult).then_inc(picked_ready, 1)
            dve.wait_ge(picked_turned, 1)
            dve.tensor_copy(picked_t[:, 0:2, :].rearrange("p s t -> p (s t)"), bank[:, 4, :]).then_inc(picked_copied, 1)
            dve.tensor_copy(picked_t[:, 2, :], bank[:, 5, 0:T]).then_inc(picked_copied, 1)
            dve.wait_ge(picked_copied, 2)
            link(dve.tensor_copy(gate_high_r[:, :], picked_t[:, 2, :]))
            link(dve.tensor_tensor(picked_low, picked_t[:, 2, :], as_f32(gate_high_r[:, :]), ALU.subtract))
            link(dve.tensor_copy(picked_t[:, 2, :], as_f32(gate_high_r[:, :])))
            with dve.Fori(0, T // 8) as n:
                for j in range(8):
                    dve.wait_ge(gates_done[j % 2], 4 * n + j // 2 + PRIMED)
                    second, first_high, first_low = onehots[j % 2]
                    first, gate = picked_t[:, 0, bass.ds(8 * n + j, 1)], picked_t[:, 2, bass.ds(8 * n + j, 1)]
                    dve.tensor_scalar(second, iota[:, :], picked_t[:, 1, bass.ds(8 * n + j, 1)], None, ALU.is_equal)
                    dve.tensor_scalar(first_high, iota[:, :], first, gate, ALU.is_equal, ALU.mult)
                    dve.tensor_scalar(first_low, iota[:, :], first, picked_low[:, bass.ds(8 * n + j, 1)], ALU.is_equal, ALU.mult
                                      ).then_inc(onehots_ready, 1)

            def weigh(n, e):
                dve.wait_ge(gelu_done[e], n + 1 + PRIMED)
                if e == 0:
                    dve.wait_ge(gates_loaded, 16 * n + 16)
                    b, _, _, used = half("experts_t", QUAD - 1, n)
                    dve.wait_ge(half_used[b], used + -1 + PRIMED)
                q = T // QUARTER
                dve.tensor_tensor(weighed[:, e, :].rearrange("p (q t) -> p q t", q=q), hidden[:, e, :].rearrange("p (q t) -> p q t", q=q),
                                  gates_in[:, :, e, :], ALU.mult).then_inc(weighed_ready[e], 1)
                dve.wait_ge(weighed_high_ready[e], n + 1)
                dve.tensor_tensor(weighed_low[:, e, :], weighed[:, e, :], as_f32(weighed_high[:, e, :]), ALU.subtract
                                  ).then_inc(weighed_low_ready[e], 1)

            def add_share(n, o):
                if o % 4 == 3:
                    b, _, _, used = half("experts_t", 4 + o // 2, n)
                    dve.wait_ge(half_used[b], used + 1 + PRIMED)
                else:
                    dve.wait_ge(shares_done, 6 * n + (3 * (o // 4) + o % 4 + 1 + PRIMED))
                dve.wait_ge(share_added[o], n + PRIMED)
                t, at = o % 4 // 2, N * (2 * (o // 4) + o % 2)
                part_ = resid[:, t, at:at + N]
                dve.tensor_tensor(part_, bank[:, 2 + o % 6, :], part_, ALU.add).then_inc(share_added[o], 1)

            with dve.Fori(0, EXPERT_STEPS) as n:
                for p in range(QUAD):
                    split_low(half("experts_t", p + LOOKAHEAD, n))
                    if p == 2:
                        weigh(n, 0)
                    if p == 4:
                        weigh(n, 1)
                    if p in (5, 6):
                        for o in (0, 1) if p == 5 else (2, 3):
                            add_share(n, o)
                for o in range(4, 8):
                    add_share(n, o)

            dve.wait_ge(final_gain_landed, 16)
            dve.wait_ge(squared, TT * 3)
            rms_scale(2, D)
            for i in range(TT):
                dve.scalar_tensor_tensor(resid[:, i, :], resid[:, i, :], stat[:, 10 + i:11 + i], final_gain,
                                         ALU.mult, ALU.mult).then_inc(normed, 1)
            dve.wait_ge(normed, TT)
            scale_rows(3, norm3_rows)
            split_turned(3)
            for side in range(2):
                copy_groups("w_in_2_t", 4 * side, 2, lambda i, j, k: qkvz_half[side][:, k, bass.ds(i * 2 * N + j * N, N)])
            for g in range(8, 11):
                b = group_done("w_in_2_t", g)
                for k in range(2):
                    c = 4 * (g - 8) + 2 * k
                    dve.tensor_copy(xbc_raw[:, c:c + 2, :].rearrange("p c t -> p (c t)"), bank[:, 2 * b + k, :]).then_inc(pair_copied[b], 1)
            dve.wait_ge(narrow_split, 3)
            dve.tensor_tensor(narrow_w[1][:, 0:KT * SSM_HEADS], dt_w.rearrange("p k n -> p (k n)"),
                              as_f32(narrow_w[0][:, 0:KT * SSM_HEADS]), ALU.subtract).then_inc(narrow_split, 1)
            dve.wait_ge(small_done, 2)
            for t in range(TT):
                cols = slice(SSM_HEADS * t, SSM_HEADS * (t + 1))
                m = dve.tensor_tensor(dt_tmp[:, 0, cols], bank[:, 6 + t, 0:SSM_HEADS], rows[:, 1, :], ALU.add)
            m.then_inc(small_copied, 1)

            for i in range(TT):
                dve.wait_ge(squared, TT * 4 + i + 1)
                heads = qk2[:, i, :].rearrange("p (h d) -> p h d", d=DH2)
                link(dve.tensor_reduce(stat[:, 24:40], squares.rearrange("p (h d) -> p h d", d=DH2), AX.X, ALU.add))
                link(dve.tensor_scalar(stat[:, 40:56], stat[:, 24:40], 1.0 / DH2, EPS, ALU.mult, ALU.add))
                dve.reciprocal(stat[:, 40:56], stat[:, 40:56]).then_inc(root_wanted, 1)
                dve.wait_ge(root_done, ROOTS.index(f"heads {i}") + 1)
                dve.tensor_tensor(heads, heads, row(stat[:, 40:56], DH2), ALU.mult).then_inc(scaled, 1)
            copy_turned(4, qk_t)

            def set_done2(n):
                u = units2[n]
                s, n0 = u["set"], n - 3
                dve.wait_ge(mixed, UNITS + n + 1)
                dve.wait_ge(probs_ready, 2 * (UNITS + n + 1))
                sums = expsum2.rearrange("p (i n) -> p i n", i=TT)[:, :, n0:n0 + 4]
                link(dve.reciprocal(sums, sums))
                for i in range(TT):
                    dve.tensor_tensor(o2[:, i, N * (s - 6):N * (s - 5)].rearrange("p (h d) -> p h d", d=DH2),
                                      bank[:, 4 + 2 * (s % 2) + i, :].rearrange("p (h d) -> p h d", d=DH2),
                                      row(sums[:, i, :], DH2), ALU.mult).then_inc(set_copied, 1)

            attention(attention2, set_done2)

            for tap in range(SSM_TAPS):
                for c in range(XBC_TILES):
                    if tap == 0:
                        note(dve.tensor_scalar(xbc[:, c, :], xbc_raw[:, c, :], conv1[:, c, 3:4], conv1[:, c, 4:5],
                                               ALU.mult, ALU.add))
                    else:
                        m = dve.scalar_tensor_tensor(xbc[:, c, tap:T], xbc_raw[:, c, 0:T - tap],
                                                     conv1[:, c, 3 - tap:4 - tap], xbc[:, c, tap:T], ALU.mult, ALU.add)
                        if tap == 3 and c == XBC_TILES - 1:
                            m.then_inc(normed, 1)
                        else:
                            note(m)
                if tap < 3:
                    settle()
            dve.wait_ge(small_copied, 2)
            dve.scalar_tensor_tensor(dt_tmp[:, 1, :], dt_tmp[:, 0, :], -1.0, dt_tmp[:, 0, :], ALU.mult, ALU.max).then_inc(normed, 1)
            dve.wait_ge(scan_act, 2)
            link(dve.scalar_tensor_tensor(dt_[:, 0, :], dt_tmp[:, 0, :], 0.0, dt_tmp[:, 1, :], ALU.max, ALU.add))
            la = dt_[:, 1, :]
            dve.scalar_tensor_tensor(la.rearrange("p (i h) -> p i h", i=TT), dt_[:, 0, :].rearrange("p (i h) -> p i h", i=TT),
                                     -1.0, copies(dt_tmp[:, 2, 0:SSM_HEADS], TT), ALU.mult, ALU.mult).then_inc(scan_dve, 1)
            dve.wait_ge(scan_dve, 1)
            triangle = la_triu.rearrange("p (h l) -> p h l", l=P)
            note(dve.tensor_tensor(triangle, row(la[:, 0:SSM_HEADS], P), copies(triu[:, :], SSM_HEADS), ALU.mult))
            dve.wait_ge(scan_pe, 1)
            for n in range(4):
                m = dve.tensor_copy(x_tok[:, n // 2, N * (n % 2):N * (n % 2) + N], bank[:, 4 + n, :])
            m.then_inc(scan_dve, 1)
            dve.wait_ge(scan_pe, 3)
            for g in range(SSM_GROUPS):
                note(dve.tensor_copy(cb[:, g, :], bank[:, g, 0:3 * P]))
            link(dve.tensor_copy(dt_[:, 2, :], bank[:, 2, 0:TT * SSM_HEADS]))
            link(dve.tensor_tensor(dt_[:, 3, 0:SSM_HEADS], bank[:, 3, 0:SSM_HEADS], dt_[:, 2, 0:SSM_HEADS], ALU.subtract))
            for i in range(TT):
                dve.wait_ge(scan_pe, 4 + i)
                for blk, per_key, op in ([(0, dt_[:, 2, 0:SSM_HEADS], ALU.subtract)] if i == 0 else
                                         [(1, dt_[:, 2, SSM_HEADS:], ALU.subtract), (2, dt_[:, 3, 0:SSM_HEADS], ALU.add)]):
                    for c in range(4):
                        m = dve.tensor_tensor(decay[:, blk, 4 * c:4 * c + 4, :],
                                              bank[:, 4 + c, :].rearrange("p (h l) -> p h l", l=P),
                                              row(per_key[:, 4 * c:4 * c + 4], P), op)
                        note(m)
                if i == 0:
                    dve.tensor_tensor(triangle, row(la[:, SSM_HEADS:], P), copies(triu[:, :], SSM_HEADS),
                                      ALU.mult).then_inc(scan_dve, 1)
                settle()
                dve.tensor_tensor(decay[:, i, :, :], decay[:, i, :, :], copies(low_mask[:, :], SSM_HEADS), ALU.add
                                  ).then_inc(normed, 1)
            link(dve.tensor_tensor(x_dt.rearrange("p i (h d) -> p (i h) d", d=SSM_DH),
                                   x_tok.rearrange("p i (h d) -> p (i h) d", d=SSM_DH), row(dt_[:, 0, :], SSM_DH), ALU.mult))
            dve.wait_ge(scan_act, 3)
            for blk, at in ((0, 0), (1, 2), (2, 1)):
                for g in range(SSM_GROUPS):
                    part_ = decay[:, blk, GROUP_HEADS * g:GROUP_HEADS * (g + 1), :]
                    m = dve.tensor_tensor(part_, part_, copies(cb[:, g, P * at:P * at + P], GROUP_HEADS), ALU.mult)
            m.then_inc(scan_dve, 1)
            for i in range(TT):
                heads = x_tok[:, i, :].rearrange("p (h d) -> p h d", d=SSM_DH)
                note(dve.tensor_tensor(heads, heads, row(rows[:, 3, :], SSM_DH), ALU.mult))
            settle()
            dve.wait_ge(scan_pe, 6)
            for i in range(TT):
                for g in range(SSM_GROUPS):
                    note(dve.tensor_tensor(o2[:, i, SSM_W + N * g:SSM_W + N * (g + 1)], bank[:, 2 * i + g, :],
                                           x_tok[:, i, N * g:N * (g + 1)], ALU.add))
            settle()
            dve.wait_ge(scan_act, 4)
            y = o2[:, :, SSM_W:]
            link(dve.tensor_tensor(y, y, vz2[:, :, SSM_W:], ALU.mult))
            link(dve.tensor_tensor(squares.rearrange("p (i d) -> p i d", i=TT), y, y, ALU.mult))
            link(dve.tensor_reduce(stat[:, 24:28], squares.rearrange("p (n d) -> p n d", d=N), AX.X, ALU.add))
            link(dve.tensor_scalar(stat[:, 28:32], stat[:, 24:28], 1.0 / N, EPS, ALU.mult, ALU.add))
            dve.reciprocal(stat[:, 28:32], stat[:, 28:32]).then_inc(root_wanted, 1)
            dve.wait_ge(root_done, ROOTS.index("scan") + 1)
            for i in range(TT):
                part_ = y[:, i, :].rearrange("p (g d) -> p g d", d=N)
                dve.tensor_tensor(part_, part_, row(stat[:, 28 + 2 * i:30 + 2 * i], N), ALU.mult).then_inc(scaled, 1)
            split_turned(5)
            add_groups("w_out_2_t")

            scale_rows(5, norm4_rows)
            split_turned(6)
            with dve.Fori(0, FF_GROUPS // 2) as i:
                for j in range(2):
                    b, used = pair("w_up_2_t", j)
                    w = conv2[:, bass.ds(2 * i + j, 1), :].rearrange("p a n -> p (a n)")
                    for p in range(QUAD):
                        split_low(half("w_up_2_t", p + LOOKAHEAD, i * 2 + j))
                    dve.wait_ge(tap_done[j], i + 1)
                    for tap in (1, 2):
                        for q in range(4):
                            plain = bank[:, 2 * b + q // 2, T * (q % 2):T * (q % 2) + T - tap]
                            m = dve.scalar_tensor_tensor(taps[:, j, q, tap:T], plain, w[:, 4 * q + 2 - tap:4 * q + 3 - tap],
                                                         taps[:, j, q, tap:T], ALU.mult, ALU.add)
                            m.then_inc(conv_step[j] if tap == 1 else conv_done[j] if q < 2 else pair_copied[b], 1)
                        if tap == 1:
                            dve.wait_ge(conv_step[j], 4 * i + 4)
                    dve.wait_ge(silu_done[j], i + 1)
                    dve.wait_ge(pair_copied[b], 2 * i + 2 * (used + 1) + PRIMED)
                    dve.tensor_tensor(taps[:, j, 0:2, :], taps[:, j, 0:2, :], taps[:, j, 2:4, :],
                                      ALU.mult).then_inc(ff_product_ready[j], 1)
                    dve.wait_ge(ff_high_ready[j], i + 1)
                    at = bass.ds(4 * i + 2 * j, 2)
                    dve.tensor_tensor(ff_low[:, at, :], taps[:, j, 0:2, :], as_f32(ff_high[:, at, :]), ALU.subtract
                                      ).then_inc(hidden_ready[j], 1)

            def down_group(b, g, column, last=False):
                for p in range(DOWN_HALVES):
                    if not last or p + LOOKAHEAD < DOWN_HALVES:
                        split_low(down_half(p + LOOKAHEAD, g))
                sb_, _, _, used = down_half(DOWN_HALVES - 1, g)
                dve.wait_ge(half_used[sb_], used + 1 + PRIMED)
                for t in range(TT):
                    part_ = resid[:, t, column]
                    dve.tensor_tensor(part_, bank[:, 2 * b + t, :], part_, ALU.add).then_inc(pair_copied[b], 1)

            for g in range(4):
                down_group(pair("w_down_2_t", g)[0], g, slice(N * g, N * g + N), last=g == 3)

        @block.scalar
        def _(act):
            prime(act, [*gates_copied, *gelu_done])
            for dst, name in STAGE1[:3]:
                act.dma_start(dst, ins[name]).then_inc(stage1_landed, 16)
            for dst, name in CONSTS:
                act.dma_start(dst[:], ins[name]).then_inc(consts_landed, 16)
            for dst, name in STAGE1[3:]:
                act.dma_start(dst, ins[name]).then_inc(stage1_landed, 16)

            def split_high(h):
                b, r, which, used = h
                act.wait_ge(raw_landed[r], 16 * used + 16)
                act.wait_ge(half_used[b], used + PRIMED)
                act.activation(high[b][:, :], raw[r][:, HALF * which:HALF * (which + 1)], ACT.Copy
                               ).then_inc(high_ready[b], 1)

            def split_groups(name, groups_, i=0):
                for g in groups_:
                    for p in range(QUAD):
                        split_high(half(name, p + LOOKAHEAD, i * 2 + g))

            def split_loop(name, steps_):
                with act.Fori(0, steps_) as i:
                    split_groups(name, range(2), i)

            for p in range(LOOKAHEAD):
                split_high(half("w_in_t", p))

            def root(which, at):
                act.wait_ge(root_wanted, ROOTS.index(which) + 1)
                act.activation(at, at, ACT.Sqrt).then_inc(root_done, 1)

            def square_rows(e, dst):
                for i in range(TT):
                    act.activation(dst[:, i, :], resid[:, i, :], ACT.Square, accum_out=stat[:, 4 * e + i:4 * e + i + 1]
                                   ).then_inc(squared, 1)
                root(e, stat[:, 4 * e + 2:4 * e + 4])

            def attention(a):
                units, first, logits = a["units"], a["first"], a["logits"]

                def exps(n):
                    g, b = first + n, (first + n) % 2
                    s = 0 if units[n]["sink"] is None else 1
                    act.wait_ge(logits_ready, 2 * (g + 1))
                    for at, width, col in ((0, T + s, UNITS + n), (T + 1, P + s, n)):
                        part_ = logits[:, b, at:at + width]
                        act.activation(part_, part_, ACT.Exp, bias=a["negmax"][:, col:col + 1],
                                       accum_out=a["expsum"][:, col:col + 1]).then_inc(probs_ready, 1)

                def copy_probs(n):
                    g, b = first + n, (first + n) % 2
                    act.wait_ge(probs_turned, g + 1)
                    if g >= 2:
                        act.wait_ge(mixed, g - 1)
                    act.activation(a["probs_t"][:, b, :], bank[:, 2 + b, 0:3 * P], ACT.Copy).then_inc(probs_copied, 1)

                for n in range(len(units) + 1):
                    if n < len(units):
                        exps(n)
                    if n >= 1:
                        copy_probs(n - 1)

            act.wait_ge(tables_copied, 1)
            act.dma_start(bias_dram[:].rearrange("(h j) -> h j", j=3 * P), by_distance[0:2 * HEADS, :]).then_inc(bias_stored, 16)
            act.wait_ge(x_landed, 16 * TT)
            square_rows(0, o1)
            act.wait_ge(stage1_landed, STAGE1_DMAS)
            act.activation(narrow_w[0][:, :], gate_w.rearrange("p k n -> p (k n)"), ACT.Copy).then_inc(narrow_split, 1)
            act.wait_ge(bias_stored, 16)
            act.dma_start(bias_copies[:, :], bias_dram[:].partition_broadcast(P)).then_inc(bias_spread, 16)
            split_loop("w_in_t", 2)
            split_groups("w_in_t", (4, 5))
            act.wait_ge(bias_spread, 16)
            act.wait_ge(small_done, 1)
            act.dma_start(bias1, bass.AP(tensor=bias_copies, offset=P - 1, ap=[[BIAS_ROW - 1, P], [3 * P, 2 * HEADS], [1, T]])
                          ).then_inc(bias_landed, 16)
            act.wait_ge(small_done, 1)
            for t in range(TT):
                m = act.activation(gate1[:, t, :, :].rearrange("p h b -> p (h b)"), bank[:, 5 + t, 0:GATES], ACT.Sigmoid)
            m.then_inc(small_copied, 1)
            act.wait_ge(cmp_dve, 1)
            act.wait_ge(cmp_pe, 1)
            for g in range(2):
                m = act.activation(cmp_hid[:, g, :, 0:N_CMP],
                                   bank[:, 6 + g, 0:2 * CMP_PAD].rearrange("p (v c) -> p v c", v=2)[:, :, 0:N_CMP],
                                   ACT.Gelu_apprx_tanh)
            m.then_inc(cmp_act, 1)
            act.wait_ge(cmp_shifted, 1)
            flat = cmp_logits[:, :, :, :, :].rearrange("p g i h c -> p (g i h c)")
            act.activation(flat, flat, ACT.Exp).then_inc(cmp_act, 1)
            attention(attention1)

            split_loop("w_out_t", 2)
            wait_pairs(act, "w_out_t")
            square_rows(1, norm2_rows)
            split_loop("peer_wq_t", 2)
            act.wait_ge(best_ready, 1)
            flat = picked[:, 2, :, :].rearrange("p i k -> p (i k)")
            act.activation(flat, flat, ACT.Exp).then_inc(best_exp, 1)
            for q in range(T // QUARTER):
                if q >= 2:
                    act.wait_ge(gates_stored[q % 2], 16 * (q // 2))
                with act.Fori(0, QUARTER // 8) as n:
                    for b in range(2):
                        act.wait_ge(gates_done[1], 4 * n + (QUARTER // 2 * q + 2 * b + 2 + PRIMED))
                        act.activation(gates_out[:, q % 2, :, bass.ds(8 * n + 4 * b, 4)],
                                       bank[:, 6 + b, :].rearrange("p (t e) -> p e t", t=4), ACT.Copy).then_inc(gates_copied[b], 1)
                for b in range(2):
                    act.wait_ge(gates_copied[b], QUARTER // 8 * (q + 1) + PRIMED)
                act.dma_start(gates_dram[q], gates_out[:, q % 2, :, :]).then_inc(gates_stored[q % 2], 16)

            def gelu(n, e):
                b, _, _, used = half("experts_t", 2 * e + 1, n)
                act.wait_ge(half_used[b], used + 1 + PRIMED)
                act.wait_ge(weighed_ready[e], n + PRIMED)
                act.activation(hidden[:, e, :], bank[:, e, 0:T], ACT.Gelu_apprx_tanh).then_inc(gelu_done[e], 1)

            def weigh(n, e):
                act.wait_ge(weighed_ready[e], n + 1 + PRIMED)
                act.activation(weighed_high[:, e, :], weighed[:, e, :], ACT.Copy).then_inc(weighed_high_ready[e], 1)

            with act.Fori(0, EXPERT_STEPS) as n:
                for p in range(QUAD):
                    split_high(half("experts_t", p + LOOKAHEAD, n))
                    if p in (2, 4):
                        gelu(n, p // 2 - 1)
                        weigh(n, p // 2 - 1)

            for o in range(8):
                act.wait_ge(share_added[o], EXPERT_STEPS + PRIMED)
            square_rows(2, o2)
            act.wait_ge(normed, TT)
            square_rows(3, norm3_rows)
            split_loop("w_in_2_t", 4)
            split_groups("w_in_2_t", (8, 9, 10))
            act.wait_ge(stage4_landed, STAGE4_DMAS)
            act.activation(narrow_w[0][:, 0:KT * SSM_HEADS], dt_w.rearrange("p k n -> p (k n)"), ACT.Copy).then_inc(narrow_split, 1)
            wait_pairs(act, "w_in_2_t")
            for i in range(TT):
                if i:
                    act.wait_ge(scaled, TT * 4 + i)
                act.activation(squares, qk2[:, i, :], ACT.Square).then_inc(squared, 1)
                root(f"heads {i}", stat[:, 40:56])
            attention(attention2)
            act.wait_ge(normed, TT + 1)
            flat = xbc.rearrange("p c t -> p (c t)")
            act.activation(flat, flat, ACT.Silu).then_inc(scan_act, 1)
            act.wait_ge(normed, TT + 2)
            act.activation(dt_tmp[:, 1, :], dt_tmp[:, 1, :], ACT.Exp, scale=-1.0).then_inc(act_step, 1)
            act.wait_ge(act_step, 1)
            act.activation(dt_tmp[:, 2, 0:SSM_HEADS], rows[:, 2, :], ACT.Exp)
            act.activation(dt_tmp[:, 1, :], dt_tmp[:, 1, :], ACT.Ln, bias=1.0).then_inc(scan_act, 1)
            act.wait_ge(normed, TT + 4)
            for blk in range(3):
                flat = decay[:, blk, :, :].rearrange("p h l -> p (h l)")
                m = act.activation(flat, flat, ACT.Exp)
            m.then_inc(scan_act, 1)
            z = vz2[:, :, SSM_W:]
            act.activation(z, z, ACT.Silu).then_inc(scan_act, 1)
            root("scan", stat[:, 28:32])
            split_loop("w_out_2_t", 2)
            wait_pairs(act, "w_out_2_t")
            square_rows(5, norm4_rows)
            with act.Fori(0, FF_GROUPS // 2) as i:
                for j in range(2):
                    b, used = pair("w_up_2_t", j)
                    w = conv2[:, bass.ds(2 * i + j, 1), :].rearrange("p a n -> p (a n)")
                    split_groups("w_up_2_t", (j,), i)
                    sb_, _, _, used_ = half("w_up_2_t", QUAD - 1, i * 2 + j)
                    act.wait_ge(half_used[sb_], used_ + 1 + PRIMED)
                    act.wait_ge(hidden_ready[j], i + PRIMED)
                    for q in range(4):
                        m = act.activation(taps[:, j, q, :], bank[:, 2 * b + q // 2, T * (q % 2):T * (q % 2) + T],
                                           ACT.Identity, scale=w[:, 4 * q + 2:4 * q + 3], bias=w[:, 4 * q + 3:4 * q + 4])
                    m.then_inc(tap_done[j], 1)
                    act.wait_ge(conv_done[j], 2 * i + 2)
                    gate_taps = taps[:, j, 0:2, :].rearrange("p q t -> p (q t)")
                    act.activation(gate_taps, gate_taps, ACT.Silu).then_inc(silu_done[j], 1)
                    act.wait_ge(ff_product_ready[j], i + 1)
                    act.activation(ff_high[:, bass.ds(4 * i + 2 * j, 2), :], taps[:, j, 0:2, :], ACT.Copy).then_inc(ff_high_ready[j], 1)
            for g in range(4):
                for p in range(DOWN_HALVES):
                    if g < 3 or p + LOOKAHEAD < DOWN_HALVES:
                        split_high(down_half(p + LOOKAHEAD, g))

        @block.gpsimd
        def _(pool):
            wait_pairs(pool, "w_out_t")
            pool.dma_start(subkeys, ins["subkeys"]).then_inc(subkeys_landed, 16)
            pool.wait_ge(gates_stored[0], 16 * 2)
            pool.dma_start(final_gain, ins["final_norm"].partition_broadcast(P)).then_inc(final_gain_landed, 16)
            pool.wait_ge(weighed_ready[1], EXPERT_STEPS + PRIMED)
            for dst, name in STAGE4:
                pool.dma_start(dst, ins[name]).then_inc(stage4_landed, 16)


def bucket_of(distance):
    d = np.maximum(distance, 0)
    large = EXACT + (np.log(np.maximum(d, 1).astype(np.float32) / np.float32(EXACT))
                     / np.float32(math.log(MAX_DIST / EXACT)) * (BUCKETS - EXACT)).astype(np.int32)
    return np.where(d < EXACT, d, np.minimum(large, BUCKETS - 1))


def one_hot(distances):
    distances = np.asarray(distances)
    table = np.zeros((BUCKETS + 2, distances.size), np.float32)
    ok = distances >= 0
    table[bucket_of(distances[ok]), np.nonzero(ok)[0]] = 1.0
    table[BUCKETS, ~ok] = 1.0
    table[BUCKETS + 1, distances >= SWA_WINDOW] = 1.0
    return table


def constants():
    p = np.arange(P)
    c = np.arange(CMP_PAD)
    t = np.arange(T).reshape(TT, P).T
    valid = (t[:, :, None] >= CMP_STRIDE * c + CMP_LEN - 1) & (c < N_CMP)
    upper = p[:, None] <= p[None, :]
    return {
        "c_ident": np.eye(P), "c_ones": np.ones((P, P)), "c_iota": np.tile(p, (P, 1)), "c_triu": upper,
        "c_low_mask": np.where(upper, 0.0, NEG),
        "c_causal": np.where(p[:, None] + P >= np.arange(T)[None, :], 0.0, NEG),
        "c_onehot_rev": one_hot(T - 1 - np.arange(3 * P)), "c_onehot_cmp": one_hot(np.arange(CMP_FIRST, T)),
        "c_block_of": p[:, None] // CMP_PAD == np.arange(GROUP_HEADS)[None, :], "c_valid": valid,
    }


def tiles_of(w, n):
    k, columns = w.shape
    w = w.reshape(k // 512, 4, P, columns // n, n).transpose(3, 0, 2, 1, 4)
    return np.ascontiguousarray(w).reshape(-1, P, 4 * n)


def laid_out(a):
    def column(v):
        return v.reshape(-1, P).T

    def in_rows(v):
        return np.broadcast_to(v, (P, v.size))

    w_in = a["w_in"][0]
    at = np.cumsum([0, HEADS * DH, P, P, P, P, P, P, GATES, HEADS * DH, P, P])
    q_a, kc, vc, ks, vs, kw, vw, gate, q_b, k_b, v_b = (w_in[:, x:y] for x, y in zip(at[:-1], at[1:]))

    def by_pairs(q):
        return q.reshape(D, 2, GROUP_HEADS, DH).transpose(0, 2, 1, 3).reshape(D, HEADS * DH)

    w_in = np.concatenate([by_pairs(q_a), by_pairs(q_b), ks, kw, k_b, kc, vc, vs, vw, v_b], axis=1)
    w_in_2 = a["w_in_2"][0]
    w_up = a["w_up_2"][0].reshape(D, 2, FF_GROUPS, 2 * P).transpose(0, 2, 1, 3).reshape(D, -1)
    u = a["peer_u"][0].reshape(EXPERT_STEPS_, 2, P, KT, P).transpose(0, 1, 4, 3, 2).reshape(EXPERT_STEPS_, 2, P, TILE)
    v = a["peer_v"][0].reshape(EXPERT_STEPS_, 2, P, 2, HALF).transpose(0, 3, 2, 1, 4).reshape(EXPERT_STEPS_, 2, P, TILE)
    rel = np.concatenate([a["rel_bias"], np.full((1, 2 * HEADS), NEG, np.float32),
                          np.concatenate([np.zeros((1, HEADS), np.float32), np.full((1, HEADS), NEG, np.float32)], axis=1)])

    def w1(w):
        return np.tile(w[0].reshape(CMP_LEN, DH, CMP_HIDDEN).transpose(1, 0, 2), (2, 1, 1))

    ones = np.ones((P, KT), np.float32)
    conv2 = np.concatenate([a["ffn_conv_w_2"][0], a["ffn_conv_b_2"]], axis=0)
    out = {
        "x": a["x"], "w_in_t": tiles_of(w_in, N), "w_out_t": tiles_of(a["w_out"][0], N),
        "peer_wq_t": tiles_of(a["peer_wq"][0], N), "experts_t": np.concatenate([u, v], axis=1).reshape(-1, P, TILE),
        "w_in_2_t": tiles_of(w_in_2[:, :-SSM_HEADS], N), "w_out_2_t": tiles_of(a["w_out_2"][0], N),
        "w_up_2_t": tiles_of(w_up, N), "w_down_2_t": tiles_of(a["w_down_2"][0], N),
        "gate_w": gate.reshape(KT, P, GATES).transpose(1, 0, 2),
        "dt_w": w_in_2[:, -SSM_HEADS:].reshape(KT, P, SSM_HEADS).transpose(1, 0, 2),
        "gains": np.stack([column(a["attn_norm"]), ones, column(a["ffn_norm"]), column(a["norm1_w_2"]),
                           np.concatenate([np.repeat(a["q_norm_w_2"].T, 8, 1), np.repeat(a["k_norm_w_2"].T, 8, 1)], axis=1),
                           np.concatenate([ones[:, :8], column(a["ssm_norm_w_2"])], axis=1), column(a["norm2_w_2"])], axis=1),
        "conv1": np.concatenate([a["ssm_conv_w_2"][0], a["ssm_conv_b_2"]], axis=0).reshape(5, XBC_TILES, P).transpose(2, 1, 0),
        "conv2": conv2.reshape(4, 2, FF_GROUPS, 2, P).transpose(4, 2, 1, 3, 0).reshape(P, FF_GROUPS, 16),
        "rows": np.stack([in_rows(a[n]) for n in ("sinks", "dt_bias_2", "a_log_2", "d_skip_2")], axis=1),
        "bias_rows": rel, "cmp_w1": np.stack([w1(a["cmp_w1_k"]), w1(a["cmp_w1_v"])], axis=1),
        "cmp_w2": np.stack([a["cmp_w2_k"][0], a["cmp_w2_v"][0]], axis=1),
        "cmp_pos": np.stack([np.tile(a["cmp_pos_k"][0].T, (2, 1)), np.tile(a["cmp_pos_v"][0].T, (2, 1))], axis=1),
        "subkeys": a["peer_subkeys"][0].transpose(2, 0, 1), "final_norm": a["final_norm"],
        **constants(),
    }
    return {k: np.ascontiguousarray(v, dtype=np.float32) for k, v in out.items()}


EXPERT_STEPS_ = EXPERT_TILES // 2


def kernel(**inputs):
    import concourse.bacc as bacc
    from concourse.bass_utils import run_bass_kernel_spmd as run

    nc = bacc.Bacc("TRN2", target_bir_lowering=False, num_devices=1)
    arrays = laid_out({k: np.asarray(v) for k, v in inputs.items()})
    ins = {k: nc.dram_tensor("in_" + k, list(v.shape), F32, kind="ExternalInput").ap() for k, v in arrays.items()}
    out = nc.dram_tensor("out", [1, T, D], F32, kind="ExternalOutput").ap()
    build(nc, ins, out)
    return run(nc, [{"in_" + k: v for k, v in arrays.items()}], core_ids=[0]).results[0]["out"]
```

```python
import math
from contextlib import ExitStack

import numpy as np

import concourse.bass as bass
from concourse import mybir

P = 128
T = 256
TT = T // P
D = 2048
KT = D // P
TILE = 2048
RAW = 2
HALF = TILE // 2
SPLIT = 4
LOOKAHEAD = 3
QUAD = 8
N = 512
EPS = 1e-6
NEG = -1e30
LOWEST = -3.0e38

HEADS = 16
DH = 64
GROUP_HEADS = 8
CMP_LEN, CMP_STRIDE, CMP_HIDDEN = 32, 16, 128
N_CMP = T // CMP_STRIDE - 1
CMP_PAD = 16
BUCKETS, EXACT, MAX_DIST = 32, 16, 2048
SWA_WINDOW = 128
CMP_FIRST = -(CMP_PAD * CMP_STRIDE - CMP_STRIDE + CMP_LEN - 1) - 1
GATES = 3 * HEADS
PEER_HEADS, PEER_KEYS, TOPK = 8, 128, 16
FOUR = 4
ACT_FIRST = 3
SLOTS = 4
QUARTER = 64
EXPERT_TILES = PEER_KEYS

HEADS2, DH2 = 8, 128
SSM_HEADS, SSM_DH, SSM_GROUPS = 16, 64, 2
SSM_W = SSM_HEADS * SSM_DH
XBC_TILES = 12
SSM_TAPS = 4
BIG = 23552
FF_TILES = 44
FF_GROUPS = 22

UNITS = 3 * HEADS

STREAM = [("w_in_t", 24, 6), ("w_out_t", 16, 4), ("peer_wq_t", 16, 4), ("experts_t", 256, 0),
          ("w_in_2_t", 44, 11), ("w_out_2_t", 16, 4), ("w_up_2_t", 88, 22), ("w_down_2_t", 44, 4)]

F32 = mybir.dt.float32
F32R = mybir.dt.float32r
U32 = mybir.dt.uint32
ALU = mybir.AluOpType
ACT = mybir.ActivationFunctionType
AX = mybir.AxisListType



def build(nc, ins, out):
    ctx = ExitStack()
    with ctx:
        def sb(name, shape, dt=F32):
            return ctx.enter_context(nc.sbuf_tensor(name, shape, dt))

        def sem(name):
            return ctx.enter_context(nc.semaphore(name))

        raw = [sb(f"raw{r}", [P, TILE]) for r in range(RAW)]
        high = [sb(f"high{b}", [P, HALF], F32R) for b in range(SPLIT)]
        low = [sb(f"low{b}", [P, HALF], F32R) for b in range(SPLIT)]
        resid = sb("resid", [P, TT, D])
        act_at = nc.sbuf_base
        act_high = sb("act_high", [P, KT, T], F32R)
        act_low = sb("act_low", [P, KT, T], F32R)
        act_place = nc.alloc_sbuf_tensor_at("act_place", [P, 2 * KT * T], F32, offset=act_at)
        act_whole = act_place[:, KT * T:].rearrange("p (c t) -> p c t", c=KT)
        big_at = nc.sbuf_base
        big = sb("big", [P, BIG])
        ff_high = nc.alloc_sbuf_tensor_at("ff_high", [P, FF_TILES, T], F32R, offset=big_at)
        ff_low = nc.alloc_sbuf_tensor_at("ff_low", [P, FF_TILES, T], F32R, offset=big_at + 4 * FF_TILES * T)
        bank = ctx.enter_context(nc.psum_tensor("bank", [P, 8, N], F32))

        ident = sb("ident", [P, P])
        ones = sb("ones", [P, P])
        iota = sb("iota", [P, P])
        triu = sb("triu", [P, P])
        low_mask = sb("low_mask", [P, P])
        gains = sb("gains", [P, 7, KT])
        conv1 = sb("conv1", [P, XBC_TILES, SSM_TAPS + 1])
        conv2 = sb("conv2", [P, FF_GROUPS, 16])
        rows = sb("rows", [P, 4, SSM_HEADS])
        stat = sb("stat", [P, 64])
        picked_place = sb("taps", [P, 2, 4, T])
        picked_low = picked_place[:, 1, 0, :]
        picked_t = picked_place[:, 0, 0:3, :]
        small_at = nc.sbuf_base
        narrow_w = [sb(f"narrow_w{n}", [P, KT * GATES], F32R) for n in range(2)]
        gate_high_r = nc.alloc_sbuf_tensor_at("gate_high_r", [P, T], F32R, offset=small_at)
        weighed_high = nc.alloc_sbuf_tensor_at("weighed_high", [P, 2, T], F32R, offset=small_at)
        weighed_low = nc.alloc_sbuf_tensor_at("weighed_low", [P, 2, T], F32R, offset=small_at + 4 * 2 * T)

        class Region:

            def __init__(self, at=0, within=None):
                self.at, self.within = at, big if within is None else within
                self.size = self.within.shape[1]

            def take(self, floats, pattern=None, dt=F32, **sizes):
                ap = self.within[:, self.at:self.at + floats]
                self.at += floats
                assert self.at <= self.size, self.at
                if dt is not F32:
                    ap = ap.bitcast(dt)
                return ap.rearrange(pattern, **sizes) if pattern else ap

        r1 = Region()
        o1 = r1.take(TT * D, "p (i d) -> p i d", i=TT)
        q1 = r1.take(16 * T, "p (c t) -> p c t", c=16)
        k1 = r1.take(5 * T, "p (c t) -> p c t", c=5)
        v1 = r1.take(TT * 384, "p (i c) -> p i c", i=TT)
        gate1 = r1.take(TT * GATES, "p (i h b) -> p i h b", i=TT, b=3)
        bias1 = Region(within=act_place).take(2 * HEADS * T, "p (h y) -> p h y", y=T)
        cbias = r1.take(TT * HEADS * CMP_PAD, "p (i h c) -> p i h c", i=TT, c=CMP_PAD)
        cmp_w1_at = r1.at
        cmp_w1 = r1.take(2 * CMP_LEN * P, "p (v l n) -> p v l n", v=2, n=P)
        cmp_w2 = r1.take(2 * DH, "p (v n) -> p v n", v=2)
        cmp_pos = r1.take(2 * CMP_LEN, "p (v l) -> p v l", v=2)
        r1_between = Region(0)
        cmp_in = r1_between.take(2 * CMP_LEN * 2 * CMP_PAD, "p (v l g c) -> p v l g c", v=2, g=2, c=CMP_PAD)
        cmp_hid_rows = r1_between.take(2 * P, "p (v n) -> p v n", v=2)
        cmp_hid = r1.take(2 * 2 * CMP_PAD, "p (g v c) -> p g v c", g=2, v=2)
        cmp_k = r1_between.take(2 * CMP_PAD, "p (g c) -> p g c", g=2)
        block_of = r1.take(GROUP_HEADS)
        valid_c = r1.take(TT * CMP_PAD, "p (i c) -> p i c", i=TT)
        gate_w = r1.take(KT * GATES, "p (k n) -> p k n", k=KT)
        buckets = r1.take(P)

        def attention_buffers(region):
            return (region.take(2 * 386, "p (b n) -> p b n", b=2), region.take(2 * 384, "p (b n) -> p b n", b=2),
                    region.take(N), region.take(2 * UNITS), region.take(2 * UNITS))

        r1_tables = Region(r1.at)
        onehot_rev = r1_tables.take(3 * P)
        onehot_cmp = r1_tables.take(T - CMP_FIRST)
        by_distance = r1_tables.take(3 * P)
        logits1, probs_t1, share1, negmax1, expsum1 = attention_buffers(r1)
        r1_cmp = Region(cmp_w1_at)
        cmp_hid8 = [r1_cmp.take(GROUP_HEADS * CMP_PAD, "p (h c) -> p h c", c=CMP_PAD) for _ in range(2)]
        cmp_v = r1_cmp.take(2 * N, "p (g n) -> p g n", g=2)
        cmp_logits = r1_cmp.take(2 * TT * GROUP_HEADS * CMP_PAD, "p (g i h c) -> p g i h c", g=2, i=TT, c=CMP_PAD)
        cmp_probs_t = r1_cmp.take(4 * P, "p (n q) -> p n q", q=P)
        cmp_stat = r1_cmp.take(4 * 32, "p (k n) -> p k n", k=4)

        r2 = Region()
        peer_q = r2.take(16 * T, "p (c t) -> p c t", c=16)
        subkeys = r2.take(2 * P, "p (s n) -> p s n", s=2)
        scores = r2.take(TT * 16 * P, "p (r n) -> p r n", n=P)
        scores_left = r2.take(TT * 16 * P, "p (r n) -> p r n", n=P)
        top = r2.take(TT * 16 * TOPK, "p (r k) -> p r k", k=TOPK)
        top_at = r2.take(TT * 16 * TOPK, "p (r k) -> p r k", dt=U32, k=TOPK)
        top_key = r2.take(TT * 16 * TOPK, "p (r k) -> p r k", k=TOPK)
        pairs = r2.take(TT * PEER_HEADS * TOPK * TOPK, "p (r n) -> p r n", n=TOPK * TOPK)
        pairs_left = scores.rearrange("p r n -> p (r n)").rearrange("p (r n) -> p r n", n=TOPK * TOPK)
        best = r2.take(TT * PEER_HEADS * TOPK, "p (r k) -> p r k", k=TOPK)
        best_at = r2.take(TT * PEER_HEADS * TOPK, "p (r k) -> p r k", dt=U32, k=TOPK)
        part_at = r2.take(2 * TT * PEER_HEADS * TOPK, "p (s r) -> p s r", dt=U32, s=2)
        part = r2.take(2 * TT * PEER_HEADS * TOPK, "p (s r) -> p s r", s=2)
        is_part = scores_left.rearrange("p r n -> p (r n)").rearrange("p (r a) -> p r a", a=TOPK)
        picked = r2.take(3 * TT * P, "p (s i k) -> p s i k", s=3, k=P)
        best_sum = r2.take(2 * TT * PEER_HEADS, "p (s r) -> p s r", s=2)

        r3 = Region()
        gates_out = r3.take(2 * EXPERT_TILES * QUARTER, "p (b e t) -> p b e t", b=2, t=QUARTER)
        gates_in = r3.take(2 * T, "p (q e t) -> p q e t", q=T // QUARTER, e=2)
        onehots_from = r3.at
        hidden = r3.take(2 * T, "p (b t) -> p b t", b=2)
        weighed = r3.take(2 * T, "p (b t) -> p b t", b=2)
        onehots_at = big_at + 4 * onehots_from
        second, first, first_high = [
            nc.alloc_sbuf_tensor_at(name, [P, SLOTS, FOUR, P], dt, offset=onehots_at + 4 * n * SLOTS * FOUR * P)
            for n, (name, dt) in enumerate([("second", F32R), ("first", F32), ("first_high", F32R)])]
        first_low = [ap[:, :].rearrange("p (c j n) -> p c j n", c=SLOTS // 2, j=FOUR)[:, c]
                     for ap in (high[LOOKAHEAD], low[LOOKAHEAD]) for c in range(SLOTS // 2)]
        assert onehots_from + 3 * SLOTS * FOUR * P <= BIG and SLOTS // 2 * FOUR * P == HALF and LOOKAHEAD < SPLIT
        final_gain = big[:, 0:D]
        gates_dram = nc.dram_tensor("gates_dram", [T // QUARTER, P, EXPERT_TILES, QUARTER], F32)

        r4 = Region(D)
        qk2 = r4.take(TT * D, "p (i c) -> p i c", i=TT)
        o2 = qk2
        x_tok_at = r4.at
        qk_t = r4.take(16 * T, "p (c t) -> p c t", c=16)
        vz2 = r4.take(TT * D, "p (i c) -> p i c", i=TT)
        qkvz_half = [qk2, vz2]
        xbc_raw_at = r4.at
        xbc_raw = r4.take(XBC_TILES * T, "p (c t) -> p c t", c=XBC_TILES)
        xbc = r4.take(XBC_TILES * T, "p (c t) -> p c t", c=XBC_TILES)
        dt_w = r4.take(KT * SSM_HEADS, "p (k n) -> p k n", k=KT)
        causal = r4.take(T)
        logits2, probs_t2, share2, negmax2, expsum2 = attention_buffers(r4)
        dt_ = r4.take(4 * TT * SSM_HEADS, "p (k n) -> p k n", k=4)
        dt_tmp = r4.take(3 * TT * SSM_HEADS, "p (k n) -> p k n", k=3)
        x_tok = Region(x_tok_at).take(TT * SSM_W, "p (i c) -> p i c", i=TT)
        r4_scan = Region(xbc_raw_at)
        x_dt = r4_scan.take(TT * SSM_W, "p (i c) -> p i c", i=TT)
        cb = r4_scan.take(SSM_GROUPS * 3 * P, "p (g n) -> p g n", g=SSM_GROUPS)
        r4_act = Region(within=act_place)
        decay = r4_act.take(3 * SSM_HEADS * P, "p (b h l) -> p b h l", b=3, h=SSM_HEADS)
        la_triu = r4_act.take(SSM_HEADS * P)
        squares = big[:, 0:D]
        norm2_rows, norm3_rows, norm4_rows = o1, o2, o2

        taps = picked_place
        TURN0 = [8 * n for n in range(8)]
        PARTS0 = [8 * (n - (n > 4)) for n in range(8)]
        BIAS_ROW = 2 * HEADS * 3 * P
        bias_dram = nc.dram_tensor("bias_by_distance", [BIAS_ROW], F32)
        bias_copies = nc.dram_tensor("bias_by_distance_copies", [P, BIAS_ROW], F32)

        CONSTS = [(ident, "c_ident"), (gains, "gains"), (ones, "c_ones"), (iota, "c_iota"), (triu, "c_triu"),
                  (low_mask, "c_low_mask"), (conv1, "conv1"), (conv2, "conv2"), (rows, "rows")]
        TABLES = [(buckets[0:BUCKETS + 2, 0:2 * HEADS], "bias_rows"), (onehot_rev[0:BUCKETS + 2, :], "c_onehot_rev"),
                  (onehot_cmp[0:BUCKETS + 2, :], "c_onehot_cmp")]
        STAGE1 = [(gate_w, "gate_w"), (cmp_w1, "cmp_w1"),
                  (cmp_w2, "cmp_w2"), (cmp_pos, "cmp_pos"), (block_of, "c_block_of"), (valid_c, "c_valid")]
        STAGE4 = [(dt_w, "dt_w"), (causal, "c_causal")]
        CONST_DMAS, STAGE1_DMAS, STAGE4_DMAS = 16 * len(CONSTS), 16 * len(STAGE1), 16 * len(STAGE4)

        x_landed = sem("x_landed")
        consts_landed = sem("consts_landed")
        tables_landed = sem("tables_landed")
        stage1_landed = sem("stage1_landed")
        bias_stored = sem("bias_stored")
        bias_spread = sem("bias_spread")
        bias_landed = sem("bias_landed")
        subkeys_landed = sem("subkeys_landed")
        final_gain_landed = sem("final_gain_landed")
        stage4_landed = sem("stage4_landed")
        out_stored = sem("out_stored")
        raw_landed = [sem(f"raw_landed{r}") for r in range(RAW)]
        high_ready = [sem(f"high_ready{b}") for b in range(SPLIT)]
        low_ready = [sem(f"low_ready{b}") for b in range(SPLIT)]
        half_used = [sem(f"half_used{b}") for b in range(SPLIT)]
        pair_copied = [sem(f"pair_copied{b}") for b in range(2)]
        squared = sem("squared")
        scaled = sem("scaled")
        turned = sem("turned")
        turned_read = sem("turned_read")
        turned_high = sem("turned_high")
        turned_parts = sem("turned_parts")
        tables_done = sem("tables_done")
        tables_copied = sem("tables_copied")
        narrow_split = sem("narrow_split")
        small_done = sem("small_done")
        small_copied = sem("small_copied")
        cmp_pe = sem("cmp_pe")
        cmp_dve = sem("cmp_dve")
        cmp_act = sem("cmp_act")
        cmp_shifted = sem("cmp_shifted")
        scores_done = sem("scores_done")
        logits_written = sem("logits_written")
        logits_ready = sem("logits_ready")
        probs_ready = sem("probs_ready")
        probs_turned = sem("probs_turned")
        probs_copied = sem("probs_copied")
        mixed = sem("mixed")
        set_copied = sem("set_copied")
        subkey_scores_done = sem("subkey_scores_done")
        subkey_scores_copied = sem("subkey_scores_copied")
        best_ready = sem("best_ready")
        best_exp = sem("best_exp")
        picked_ready = sem("picked_ready")
        picked_turned = sem("picked_turned")
        picked_copied = sem("picked_copied")
        onehots_ready = [sem(f"onehots_ready{c}") for c in range(SLOTS)]
        first_high_ready = [sem(f"first_high_ready{c}") for c in range(SLOTS)]
        first_low_ready = [sem(f"first_low_ready{c}") for c in range(SLOTS)]
        gates_done = [sem(f"gates_done{c}") for c in range(SLOTS)]
        gates_copied = [sem(f"gates_copied{b}") for b in range(2)]
        gates_stored = [sem(f"gates_stored{b}") for b in range(2)]
        gates_loaded = sem("gates_loaded")
        weighed_high_ready = [sem(f"weighed_high_ready{e}") for e in range(2)]
        weighed_low_ready = [sem(f"weighed_low_ready{e}") for e in range(2)]
        ff_high_ready = [sem(f"ff_high_ready{b}") for b in range(2)]
        ff_product_ready = [sem(f"ff_product_ready{b}") for b in range(2)]
        gelu_done = [sem(f"gelu_done{e}") for e in range(2)]
        weighed_ready = [sem(f"weighed_ready{e}") for e in range(2)]
        shares_done = sem("shares_done")
        share_added = [sem(f"share_added{o}") for o in range(8)]
        normed = sem("normed")
        scan_pe = sem("scan_pe")
        scan_dve = sem("scan_dve")
        scan_act = sem("scan_act")
        tap_done = [sem(f"tap_done{b}") for b in range(2)]
        conv_done = [sem(f"conv_done{b}") for b in range(2)]
        silu_done = [sem(f"silu_done{b}") for b in range(2)]
        hidden_ready = [sem(f"hidden_ready{b}") for b in range(2)]
        conv_step = [sem(f"conv_step{b}") for b in range(2)]
        root_wanted = sem("root_wanted")
        root_done = sem("root_done")
        dve_step = sem("dve_step")
        act_step = sem("act_step")

        PRIMED = 1

        def prime(eng, semaphores):
            for semaphore in semaphores:
                eng.sem_inc(semaphore, PRIMED)

        ROOTS = [0, 1, 2, 3, "heads 0", "heads 1", "scan", 5]
        quads, groups = {}, {}
        n_quads, n_groups = 0, 0
        for name, tiles, n in STREAM:
            quads[name], groups[name] = n_quads, n_groups
            n_quads += tiles // 4
            n_groups += n

        def half(name, p, quad=0):
            q, p = quad + (quads[name] + p // QUAD), p % QUAD
            return p % SPLIT, p // 2 % RAW, p % 2, 2 * q + p // 4

        def down_half(p, g=0):
            g, p = g + p // DOWN_HALVES, p % DOWN_HALVES
            b, r, used = p % SPLIT, p // 2 % RAW, 2 * quads["w_down_2_t"]
            return b, r, p % 2, used + g * DOWN_USES[b] + p // 4

        def pair(name, g):
            return (groups[name] + g) % 2, (groups[name] + g) // 2

        EXPERT_STEPS = EXPERT_TILES // 2
        DOWN_TILES = FF_TILES // 4
        DOWN_HALVES = 2 * DOWN_TILES
        DOWN_USES = [6, 6, 5, 5]
        DOWN_LOADS = [6, 5]

        def wait_pairs(eng, name):
            n = next(n for which, _, n in STREAM if which == name)
            for g in (n - 2, n - 1):
                b, used = pair(name, g)
                eng.wait_ge(pair_copied[b], 2 * (used + 1) + PRIMED)

        def row(ap, n):
            return ap.unsqueeze(len(ap.shape)).to_broadcast([*ap.shape, n])

        def copies(ap, n, at=1):
            shape = list(ap.shape)
            return ap.unsqueeze(at).to_broadcast([*shape[:at], n, *shape[at:]])

        class Steps:

            def __init__(self, eng, semaphore):
                self.eng, self.semaphore, self.n = eng, semaphore, 0

            def note(self, instruction):
                instruction.then_inc(self.semaphore, 1)
                self.n += 1

            def settle(self):
                self.eng.wait_ge(self.semaphore, self.n)

            def link(self, instruction):
                self.note(instruction)
                self.settle()

        units1 = []
        for branch in range(3):
            for h in range(HEADS):
                g, c = h // GROUP_HEADS, h % GROUP_HEADS
                part_of = slice(DH * g, DH * g + DH)
                units1.append(dict(
                    q=q1[part_of, c + (8 if branch == 2 else 0), :], k=k1[part_of, branch, :],
                    v=[v1[:, i, P * branch + DH * g:P * branch + DH * g + DH] for i in range(TT)],
                    bias=bias1[:, h + (HEADS if branch == 2 else 0), :], scale=DH ** -0.5,
                    sink=rows[:, 0, h:h + 1] if branch == 2 else None, width=DH,
                    set=2 * branch + g, at=DH * c))
        units2 = [dict(q=qk_t[:, h, :], k=qk_t[:, HEADS2 + h, :],
                       v=[qkvz_half[1][:, i, DH2 * h:DH2 * h + DH2] for i in range(TT)],
                       bias=causal, scale=DH2 ** -0.5, sink=None, width=DH2, set=6 + h // 4, at=DH2 * (h % 4))
                  for h in range(HEADS2)]
        attention1 = dict(units=units1, first=0, logits=logits1, probs_t=probs_t1, negmax=negmax1, expsum=expsum1)
        attention2 = dict(units=units2, first=UNITS, logits=logits2, probs_t=probs_t2, negmax=negmax2, expsum=expsum2)

        block = ctx.enter_context(nc.Block())

        @block.sync
        def _(sp):
            def load(name, tile, r, used):
                sp.wait_ge(low_ready[2 * r + 1], used + PRIMED)
                sp.dma_start(raw[r][:, :], ins[name][bass.ds(tile, 1)].rearrange("a p n -> p (a n)")
                             ).then_inc(raw_landed[r], 16)

            for i in range(TT):
                sp.dma_start(resid[:, i, :], ins["x"][0, i * P:(i + 1) * P, :]).then_inc(x_landed, 16)
            for name, tiles, _ in STREAM[:-1]:
                with sp.Fori(0, tiles // 4) as n:
                    for t in range(4):
                        if name == "experts_t" and t == 2:
                            sp.wait_ge(weighed_ready[1], n + PRIMED)
                            sp.wait_ge(gates_stored[0], 16 * 2)
                            sp.wait_ge(gates_stored[1], 16 * 2)
                            sp.dma_start(gates_in, gates_dram[:, :, bass.ds(2 * n, 2), :].rearrange(
                                "q p e t -> p q e t")).then_inc(gates_loaded, 16)
                        load(name, n * 4 + t, t % RAW, n * 2 + (2 * quads[name] + t // 2))
            name = "w_down_2_t"
            with sp.Fori(0, 4) as g:
                for t in range(DOWN_TILES):
                    r = t % RAW
                    load(name, g * DOWN_TILES + t, r, g * DOWN_LOADS[r] + (2 * quads[name] + t // 2))
            for g in range(4):
                b, used = pair(name, g)
                sp.wait_ge(pair_copied[b], 2 * (used + 1) + PRIMED)
                sp.dma_start(out[0].rearrange("(i p) d -> p i d", p=P)[:, :, N * g:N * (g + 1)],
                             resid[:, :, N * g:N * (g + 1)]).then_inc(out_stored, 16)
            sp.wait_ge(out_stored, 16 * 4)

        @block.tensor
        def _(pe):
            prime(pe, [*half_used, *gates_done, shares_done])

            def mm(out_, lhs_t, rhs, start=True, stop=True):
                return pe.matmul(out_, lhs_t, rhs, start=start, stop=stop, skip_group_check=True)

            def mm3(out_, lhs_t, rhs, start, stop):
                mm(out_, lhs_t[0], rhs[0], start=start, stop=False)
                mm(out_, lhs_t[0], rhs[1], start=False, stop=False)
                return mm(out_, lhs_t[1], rhs[0], start=False, stop=stop)

            def parts(pair_, *at):
                return [ap[at] for ap in pair_]

            def take(h):
                b, _, _, used = h
                pe.wait_ge(low_ready[b], used + 1 + PRIMED)
                return [ap[:, :].rearrange("p (k n) -> p k n", k=2) for ap in (high[b], low[b])]

            def product(b, halves, lhs, stationary_weights, between=lambda p: None):
                every = slice(None)
                for p, h in enumerate(halves):
                    w = take(h)
                    for k in range(2):
                        kt = 2 * p + k
                        first, last = kt == 0, kt == 2 * len(halves) - 1
                        if stationary_weights:
                            for n in range(stationary_weights):
                                m = mm3(bank[:, 2 * b + n // 2, T * (n % 2):T * (n % 2) + T],
                                        parts(w, every, k, slice(P * n, P * n + P)), parts(lhs, every, kt, every),
                                        start=first and n % 2 == 0, stop=last)
                        else:
                            for t in range(TT):
                                m = mm3(bank[:, 2 * b + t, :], parts(lhs, every, kt, slice(P * t, P * t + P)),
                                        parts(w, every, k, every), start=first, stop=last)
                    m.then_inc(half_used[h[0]], 1)
                    between(p)

            def product_group(name, g, i=0, stationary_weights=4, between=lambda p: None):
                b, used = pair(name, g)
                pe.wait_ge(pair_copied[b], i * 2 + 2 * used + PRIMED)
                product(b, [half(name, p, i * 2 + g) for p in range(QUAD)], (act_high, act_low), stationary_weights, between)

            def product_loop(name, steps, stationary_weights=4):
                with pe.Fori(0, steps) as i:
                    for j in range(2):
                        product_group(name, j, i, stationary_weights)

            def turn(n, src):
                for b in range(8):
                    i, quarter = b // 4, b % 4
                    if b % 4 == 0:
                        pe.wait_ge(scaled, TT * n + i + 1)
                    if TURN0[n] + b >= 4:
                        pe.wait_ge(turned_read, TURN0[n] + b - 3)
                    for j in range(4):
                        c = 4 * quarter + j
                        m = pe.transpose(bank[:, 4 + b % 4, P * j:P * j + P], src[:, i, P * c:P * c + P], ident[:, :])
                    m.then_inc(turned, 1)

            def attention(a):
                units, first = a["units"], a["first"]

                def scores(n):
                    u, b = units[n], (first + n) % 2
                    if first + n >= 2:
                        pe.wait_ge(logits_ready, 2 * (first + n - 1))
                    mm(bank[:, b, 0:T], u["q"][:, P:T], u["k"][:, 0:T])
                    mm(bank[:, b, T:T + P], u["q"][:, 0:P], u["k"][:, 0:P]).then_inc(scores_done, 1)

                def turn_probs(n):
                    b = (first + n) % 2
                    pe.wait_ge(probs_ready, 2 * (first + n + 1))
                    if first + n >= 2:
                        pe.wait_ge(probs_copied, first + n - 1)
                    for k, at in enumerate((0, P, T + 1)):
                        m = pe.transpose(bank[:, 2 + b, P * k:P * k + P], a["logits"][:, b, at:at + P], ident[:, :])
                    m.then_inc(probs_turned, 1)

                def mix(n):
                    u, b = units[n], (first + n) % 2
                    o, w, at = 4 + 2 * (u["set"] % 2), u["width"], u["at"]
                    pt = a["probs_t"][:, b, :]
                    pe.wait_ge(probs_copied, first + n + 1)
                    if at == 0 and u["set"] >= 2:
                        pe.wait_ge(set_copied, 2 * (u["set"] - 1))
                    mm(bank[:, o + 1, at:at + w], pt[:, 0:P], u["v"][0], stop=False)
                    mm(bank[:, o + 1, at:at + w], pt[:, P:T], u["v"][1], start=False)
                    mm(bank[:, o, at:at + w], pt[:, T:T + P], u["v"][0]).then_inc(mixed, 1)

                scores(0)
                scores(1)
                for n in range(len(units) + 1):
                    if n + 2 < len(units):
                        scores(n + 2)
                    if n < len(units):
                        turn_probs(n)
                    if n >= 1:
                        mix(n - 1)

            pe.wait_ge(tables_landed, 16 * len(TABLES))
            mm(bank[0:2 * HEADS, 0, 0:3 * P], buckets[0:BUCKETS + 2, 0:2 * HEADS], onehot_rev[0:BUCKETS + 2, :])
            for i in range(TT):
                for c in range(CMP_PAD):
                    at = P * i - CMP_STRIDE * c - CMP_LEN + 1 - CMP_FIRST
                    m = mm(bank[:, 1, HEADS * (CMP_PAD * i + c):HEADS * (CMP_PAD * i + c + 1)],
                           onehot_cmp[0:BUCKETS + 2, at:at + P], buckets[0:BUCKETS + 2, 0:HEADS])
            m.then_inc(tables_done, 1)

            pe.wait_ge(x_landed, 16 * TT)
            pe.wait_ge(consts_landed, CONST_DMAS)
            turn(0, o1)
            pe.wait_ge(turned_parts, PARTS0[1])
            pe.wait_ge(tables_copied, 2)
            product_loop("w_in_t", 2)
            product_group("w_in_t", 4)
            b, used = pair("w_in_t", 5)
            pe.wait_ge(pair_copied[b], 2 * used + PRIMED)
            pe.wait_ge(turned_parts, PARTS0[1])
            every = slice(None)
            acts = (act_high, act_low)
            for p in range(QUAD):
                h = half("w_in_t", p, 5)
                w = take(h)
                for k in range(2):
                    kt, first, last = 2 * p + k, p == 0 and k == 0, p == QUAD - 1 and k == 1
                    mm3(bank[:, 4, 0:T], parts(w, every, k, slice(0, P)), parts(acts, every, kt, every), first, last)
                    for t in range(TT):
                        m = mm3(bank[:, 2 * b + t, 0:3 * P], parts(acts, every, kt, slice(P * t, P * t + P)),
                                parts(w, every, k, slice(P, N)), first, last)
                m.then_inc(half_used[h[0]], 1)
            pe.wait_ge(narrow_split, 2)
            for t in range(TT):
                for kt in range(KT):
                    m = mm3(bank[:, 5 + t, 0:GATES], parts(acts, every, kt, slice(P * t, P * t + P)),
                            parts(narrow_w, every, slice(GATES * kt, GATES * kt + GATES)), kt == 0, kt == KT - 1)
            m.then_inc(small_done, 1)

            pe.wait_ge(small_copied, 1)
            pe.wait_ge(cmp_dve, 2)
            for v in range(2):
                for l in range(CMP_LEN):
                    m = mm(bank[0:2 * CMP_PAD, 6 + v, 0:P], cmp_in[:, v, l, :, :].rearrange("p g c -> p (g c)"),
                           cmp_w1[:, v, l, :], start=l == 0, stop=l == CMP_LEN - 1)
            m.then_inc(cmp_pe, 1)
            pe.wait_ge(cmp_act, 1)
            for v in range(2):
                m = pe.transpose(bank[:, 4, 2 * CMP_PAD * v:2 * CMP_PAD * (v + 1)], cmp_hid_rows[0:2 * CMP_PAD, v, :],
                                 ident[0:2 * CMP_PAD, 0:2 * CMP_PAD])
            m.then_inc(cmp_pe, 1)
            pe.wait_ge(cmp_dve, 5)
            for g in range(2):
                m = mm(bank[DH * g:DH * g + DH, 4, 0:CMP_PAD], cmp_w2[:, 0, :], cmp_hid[:, g, 0, :])
            m.then_inc(cmp_pe, 1)
            for g in range(2):
                m = mm(bank[:, 5, DH * g:DH * g + DH], cmp_hid8[g][:, :, :].rearrange("p h c -> p (h c)"), cmp_w2[:, 1, :])
            m.then_inc(cmp_pe, 1)
            pe.wait_ge(cmp_dve, 6)
            for i in range(TT):
                for h in range(GROUP_HEADS):
                    at = 2 * CMP_PAD * (GROUP_HEADS * i + h)
                    m = mm(bank[:, 6, at:at + 2 * CMP_PAD], q1[:, h, P * i:P * i + P],
                           cmp_k[:, :, :].rearrange("p g c -> p (g c)"))
            m.then_inc(cmp_pe, 1)
            pe.wait_ge(cmp_dve, 7)
            for g in range(2):
                for i in range(TT):
                    m = pe.transpose(bank[:, 4, P * (2 * g + i):P * (2 * g + i) + P],
                                     cmp_logits[:, g, i, :, :].rearrange("p h c -> p (h c)"), ident[:, :])
            m.then_inc(cmp_pe, 1)
            pe.wait_ge(cmp_dve, 8)
            for g in range(2):
                for i in range(TT):
                    m = mm(bank[:, 2 * i + g, :], cmp_probs_t[:, 2 * g + i, :], cmp_v[:, g, :])
            m.then_inc(cmp_pe, 1)

            pe.wait_ge(cmp_dve, 9)
            attention(attention1)
            turn(1, o1)
            pe.wait_ge(turned_parts, PARTS0[2])
            product_loop("w_out_t", 2, stationary_weights=0)

            turn(2, norm2_rows)
            pe.wait_ge(turned_parts, PARTS0[3])
            def subkey_scores(g):
                b, used = pair("peer_wq_t", g)
                pe.wait_ge(subkeys_landed, 16)
                pe.wait_ge(pair_copied[b], 2 * (used + 1) + PRIMED)
                for i in range(TT):
                    if g >= 2:
                        pe.wait_ge(subkey_scores_copied, TT * (g - 2) + i + 1)
                    for j in range(4):
                        m = mm(bank[:, 4 + TT * (g % 2) + i, P * j:P * j + P], peer_q[:, 4 * g + j, P * i:P * i + P],
                               subkeys[:, j % 2, :])
                    m.then_inc(subkey_scores_done, 1)

            for g in range(4):
                product_group("peer_wq_t", g, between=lambda p: subkey_scores(g - 1) if g and p == 0 else None)
            subkey_scores(3)
            pe.wait_ge(picked_ready, 1)
            pe.wait_ge(subkey_scores_copied, 8)
            for s in range(3):
                for i in range(TT):
                    n = 2 * s + i
                    m = pe.transpose(bank[:, 4 + n // 4, P * (n % 4):P * (n % 4) + P], picked[:, s, i, :], ident[:, :])
            m.then_inc(picked_turned, 1)
            with pe.Fori(0, T // (SLOTS * FOUR)) as n:
                for c in range(SLOTS):
                    b = c % 2
                    pe.wait_ge(gates_copied[b], SLOTS // 2 * n + (c // 2 + PRIMED))
                    pe.wait_ge(first_high_ready[c], n + 1)
                    pe.wait_ge(first_low_ready[c], n + 1)
                    for j in range(FOUR):
                        at = slice(P * j, P * j + P)
                        mm(bank[:, 6 + b, at], second[:, c, j, :], first_high[:, c, j, :], stop=False)
                        m = mm(bank[:, 6 + b, at], second[:, c, j, :], first_low[c][:, j, :], start=False)
                    m.then_inc(gates_done[c], 1)

            for b in range(2):
                pe.wait_ge(gates_copied[b], T // 8 + PRIMED)
            with pe.Fori(0, EXPERT_STEPS) as n:
                for e in range(2):
                    pe.wait_ge(gelu_done[e], n + PRIMED)
                    for p in (2 * e, 2 * e + 1):
                        h = half("experts_t", p, n)
                        b = h[0]
                        pe.wait_ge(low_ready[b], h[3] + 1 + PRIMED)
                        for k in range(KT // 2):
                            kt = KT // 2 * (p % 2) + k
                            m = mm3(bank[:, e, 0:T], parts((high[b], low[b]), every, slice(P * k, P * k + P)),
                                    parts(acts, every, kt, every), kt == 0, kt == KT - 1)
                        m.then_inc(half_used[b], 1)
                for columns in range(2):
                    for e in range(2):
                        h = half("experts_t", 4 + 2 * columns + e, n)
                        b = h[0]
                        if columns == 0:
                            pe.wait_ge(weighed_low_ready[e], n + 1)
                        pe.wait_ge(low_ready[b], h[3] + 1 + PRIMED)
                        for c in range(4):
                            o = 4 * columns + c
                            t, at = c // 2, N * (c % 2)
                            if e == 0:
                                before = {0: 6, 1: 7, 6: 0, 7: 1}.get(o, o)
                                pe.wait_ge(share_added[before], n + (1 if o >= 6 else 0) + PRIMED)
                            m = mm3(bank[:, 2 + o % 6, :], parts((weighed_high, weighed_low), every, e, slice(P * t, P * t + P)),
                                    parts((high[b], low[b]), every, slice(at, at + N)), e == 0, e == 1)
                            if e == 1 and c < 3:
                                m.then_inc(shares_done, 1)
                        m.then_inc(half_used[b], 1)

            turn(3, norm3_rows)
            pe.wait_ge(turned_parts, PARTS0[4])
            product_loop("w_in_2_t", 4, stationary_weights=0)
            for g in (8, 9):
                product_group("w_in_2_t", g)
            turn(4, qkvz_half[0])
            product_group("w_in_2_t", 10)
            pe.wait_ge(narrow_split, 4)
            pe.wait_ge(turned_read, TURN0[5])
            for t in range(TT):
                for kt in range(KT):
                    m = mm3(bank[:, 6 + t, 0:SSM_HEADS], parts(acts, every, kt, slice(P * t, P * t + P)),
                            parts(narrow_w, every, slice(SSM_HEADS * kt, SSM_HEADS * (kt + 1))), kt == 0, kt == KT - 1)
            m.then_inc(small_done, 1)
            pe.wait_ge(small_copied, 2)
            attention(attention2)

            pe.wait_ge(scan_act, 1)
            pe.wait_ge(set_copied, 2 * 8)
            for n in range(4):
                i = n // 2
                for j in range(4):
                    m = pe.transpose(bank[:, 4 + n, P * j:P * j + P], xbc[:, 4 * (n % 2) + j, P * i:P * i + P], ident[:, :])
            m.then_inc(scan_pe, 1)
            for g in range(SSM_GROUPS):
                mm(bank[:, g, 0:T], xbc[:, 8 + g, 0:P], xbc[:, 10 + g, :])
                m = mm(bank[:, g, T:T + P], xbc[:, 8 + g, P:T], xbc[:, 10 + g, P:T])
            m.then_inc(scan_pe, 1)
            pe.wait_ge(scan_dve, 1)
            mm(bank[:, 2, 0:TT * SSM_HEADS], triu[:, :], dt_[:, 1, :])
            mm(bank[:, 3, 0:SSM_HEADS], ones[:, :], dt_[:, 1, 0:SSM_HEADS]).then_inc(scan_pe, 1)
            for i in range(TT):
                pe.wait_ge(scan_dve, 2 + i)
                for c in range(4):
                    m = mm(bank[:, 4 + c, :], ones[:, :], la_triu[:, N * c:N * c + N])
                m.then_inc(scan_pe, 1)
            for g in range(SSM_GROUPS):
                pe.wait_ge(scan_dve, 4 + g)
                for j in range(GROUP_HEADS):
                    h = GROUP_HEADS * g + j
                    cols = slice(SSM_DH * j, SSM_DH * j + SSM_DH)
                    xs = [x_dt[:, i, SSM_DH * h:SSM_DH * h + SSM_DH] for i in range(TT)]
                    mm(bank[:, g, cols], decay[:, 0, h, :], xs[0])
                    mm(bank[:, 2 + g, cols], decay[:, 2, h, :], xs[0], stop=False)
                    m = mm(bank[:, 2 + g, cols], decay[:, 1, h, :], xs[1], start=False)
            m.then_inc(scan_pe, 1)
            turn(5, o2)
            pe.wait_ge(turned_parts, PARTS0[6])
            product_loop("w_out_2_t", 2, stationary_weights=0)

            turn(6, norm4_rows)
            pe.wait_ge(turned_parts, PARTS0[7])
            product_loop("w_up_2_t", FF_GROUPS // 2)
            for j in range(2):
                pe.wait_ge(hidden_ready[j], FF_GROUPS // 2 + PRIMED)
            with pe.Fori(0, 2) as i:
                for j in range(2):
                    b, used = pair("w_down_2_t", j)
                    pe.wait_ge(pair_copied[b], i * 2 + 2 * used + PRIMED)
                    product(b, [down_half(p, i * 2 + j) for p in range(DOWN_HALVES)], (ff_high, ff_low), 0)

        @block.vector
        def _(dve):
            prime(dve, [*low_ready, *pair_copied, *share_added, *weighed_ready, *hidden_ready])
            steps = Steps(dve, dve_step)
            link, note, settle = steps.link, steps.note, steps.settle

            def rms_scale(e, n_features):
                at = stat[:, 4 * e + 2:4 * e + 4]
                link(dve.tensor_scalar(at, stat[:, 4 * e:4 * e + 2], 1.0 / n_features, EPS, ALU.mult, ALU.add))
                dve.reciprocal(at, at).then_inc(root_wanted, 1)
                dve.wait_ge(root_done, ROOTS.index(e) + 1)

            def scale_rows(e, dst):
                dve.wait_ge(squared, TT * (e + 1))
                rms_scale(e, D)
                for i in range(TT):
                    dve.tensor_scalar(dst[:, i, :], resid[:, i, :], stat[:, 4 * e + 2 + i:4 * e + 3 + i], None,
                                      ALU.mult).then_inc(scaled, 1)

            def as_f32(ap):
                return ap.bitcast(F32)

            def split_low(h):
                b, r, which, used = h
                dve.wait_ge(high_ready[b], used + 1)
                dve.tensor_tensor(low[b][:, :], raw[r][:, HALF * which:HALF * (which + 1)], as_f32(high[b][:, :]),
                                  ALU.subtract).then_inc(low_ready[b], 1)

            def split_turned(n):
                def block(ap, b):
                    return ap[:, 4 * (b % 4):4 * (b % 4) + 4, P * (b // 4):P * (b // 4) + P]

                for b in range(9):
                    if b < 8:
                        c = 4 * (b % 4)
                        dve.wait_ge(turned, TURN0[n] + b + 1)
                        dve.tensor_tensor(block(act_whole, b), bank[:, 4 + b % 4, :].rearrange("p (c t) -> p c t", c=4),
                                          row(gains[:, n, c:c + 4], P), ALU.mult).then_inc(turned_read, 1)
                    if b >= 1:
                        dve.wait_ge(turned_high, PARTS0[n] + b)
                        dve.tensor_tensor(block(act_low, b - 1), block(act_whole, b - 1), as_f32(block(act_high, b - 1)),
                                          ALU.subtract).then_inc(turned_parts, 1)

            def copy_turned(n, dst):
                for b in range(8):
                    i, c = b // 4, 4 * (b % 4)
                    dve.wait_ge(turned, TURN0[n] + b + 1)
                    dve.tensor_tensor(dst[:, c:c + 4, P * i:P * i + P],
                                      bank[:, 4 + b % 4, :].rearrange("p (c t) -> p c t", c=4),
                                      row(gains[:, n, c:c + 4], P), ALU.mult).then_inc(turned_read, 1)

            def group_done(name, g, i=0, between=lambda p: None):
                for p in range(QUAD):
                    split_low(half(name, p + LOOKAHEAD, i * 2 + g))
                    between(p)
                b, _, _, used = half(name, QUAD - 1, i * 2 + g)
                dve.wait_ge(half_used[b], used + 1 + PRIMED)
                return pair(name, g)[0]

            def copy_groups(name, g0, steps_, dst_of):
                with dve.Fori(0, steps_) as i:
                    for j in range(2):
                        b = group_done(name, g0 + j, i)
                        for k in range(2):
                            dve.tensor_copy(dst_of(i, j, k), bank[:, 2 * b + k, :]).then_inc(pair_copied[b], 1)

            def add_groups(name):
                with dve.Fori(0, 2) as i:
                    for j in range(2):
                        b = group_done(name, j, i)
                        for t in range(TT):
                            part_ = resid[:, t, bass.ds(i * 2 * N + j * N, N)]
                            dve.tensor_tensor(part_, bank[:, 2 * b + t, :], part_, ALU.add).then_inc(pair_copied[b], 1)

            def attention(a, set_done):
                units, first, logits = a["units"], a["first"], a["logits"]
                for n, u in enumerate(units):
                    g, b = first + n, (first + n) % 2
                    dve.wait_ge(scores_done, g + 1)
                    if g >= 2:
                        dve.wait_ge(probs_turned, g - 1)
                    at = logits[:, b, :]
                    dve.scalar_tensor_tensor(at[:, 0:T], bank[:, b, 0:T], u["scale"], u["bias"][:, 0:T],
                                             ALU.mult, ALU.add)
                    last = dve.scalar_tensor_tensor(at[:, T + 1:T + 1 + P], bank[:, b, T:T + P], u["scale"],
                                                    u["bias"][:, P:T], ALU.mult, ALU.add)
                    if u["sink"] is not None:
                        last = dve.tensor_copy(at[:, T:T + P + 2:P + 1], u["sink"].to_broadcast([P, 2]))
                    last.then_inc(logits_written, 1)
                    dve.wait_ge(logits_written, g + 1)
                    s = 0 if u["sink"] is None else 1
                    dve.tensor_reduce(a["negmax"][:, UNITS + n:UNITS + n + 1], at[:, 0:T + s], AX.X, ALU.max,
                                      negate=True).then_inc(logits_ready, 1)
                    dve.tensor_reduce(a["negmax"][:, n:n + 1], at[:, T + 1:T + 1 + P + s], AX.X, ALU.max,
                                      negate=True).then_inc(logits_ready, 1)
                    if n >= 2 and units[n - 2]["set"] != units[n - 1]["set"]:
                        set_done(n - 2)
                set_done(len(units) - 1)

            dve.wait_ge(x_landed, 16 * TT)
            scale_rows(0, o1)
            dve.wait_ge(tables_done, 1)
            dve.tensor_copy(by_distance[0:2 * HEADS, :], bank[0:2 * HEADS, 0, 0:3 * P]).then_inc(tables_copied, 1)
            dve.tensor_copy(cbias[:, :, :, :], bank[:, 1, :].rearrange("p (i c h) -> p i h c", i=TT, c=CMP_PAD)
                            ).then_inc(tables_copied, 1)

            dve.wait_ge(consts_landed, CONST_DMAS)
            split_turned(0)
            for p in range(LOOKAHEAD):
                split_low(half("w_in_t", p))
            dve.memset(cmp_k[:, :, :], 0.0)
            dve.memset(cmp_in[:, :, :, :, :], 0.0).then_inc(cmp_dve, 1)
            copy_groups("w_in_t", 0, 2, lambda i, j, k: q1[:, bass.ds(i * 8 + (4 * j + 2 * k), 2), :].rearrange("p c t -> p (c t)"))
            b = group_done("w_in_t", 4)
            for k in range(2):
                dve.tensor_copy(k1[:, 2 * k:2 * k + 2, :].rearrange("p c t -> p (c t)"), bank[:, 2 * b + k, :]).then_inc(pair_copied[b], 1)
            dve.wait_ge(narrow_split, 1)
            dve.tensor_tensor(narrow_w[1][:, :], gate_w.rearrange("p k n -> p (k n)"), as_f32(narrow_w[0][:, :]),
                              ALU.subtract).then_inc(narrow_split, 1)
            b = group_done("w_in_t", 5)
            for t in range(TT):
                dve.tensor_copy(v1[:, t, :], bank[:, 2 * b + t, 0:3 * P]).then_inc(pair_copied[b], 1)
            link(dve.tensor_copy(k1[:, 4, :], bank[:, 4, 0:T]))

            dve.wait_ge(stage1_landed, STAGE1_DMAS)
            for v in range(2):
                src = k1[:, 3 + v, :]
                blocks = bass.AP(tensor=src.tensor, offset=src.offset,
                                 ap=[list(src.ap[0]), [1, CMP_LEN], [CMP_STRIDE, N_CMP]])
                for g in range(2):
                    part_of = slice(DH * g, DH * g + DH)
                    m = dve.tensor_tensor(cmp_in[part_of, v, :, g, 0:N_CMP], blocks[part_of],
                                          row(cmp_pos[part_of, v, :], N_CMP), ALU.add)
            m.then_inc(cmp_dve, 1)
            dve.wait_ge(cmp_pe, 2)
            turned_hid = bank[:, 4, 0:4 * CMP_PAD].rearrange("p (v g c) -> p g v c", v=2, g=2)
            dve.tensor_copy(cmp_hid[:, :, :, :], turned_hid).then_inc(cmp_dve, 1)
            for g in range(2):
                dve.tensor_copy(cmp_hid8[g][:, :, :], copies(turned_hid[:, g, 1, :], GROUP_HEADS)).then_inc(cmp_dve, 1)
            dve.wait_ge(cmp_pe, 4)
            for g in range(2):
                dve.tensor_tensor(cmp_v[:, g, :].rearrange("p (h d) -> p h d", h=GROUP_HEADS),
                                  copies(bank[:, 5, DH * g:DH * g + DH], GROUP_HEADS), row(block_of, DH), ALU.mult)
            for g in range(2):
                part_of = slice(DH * g, DH * g + DH)
                m = dve.tensor_copy(cmp_k[part_of, g, :], bank[part_of, 4, 0:CMP_PAD])
            m.then_inc(cmp_dve, 1)
            dve.wait_ge(cmp_pe, 5)
            rows_c = cmp_logits[:, :, :, :, :].rearrange("p g i h c -> p (g i h) c")
            for g in range(2):
                note(dve.scalar_tensor_tensor(
                    cmp_logits[:, g, :, :, :],
                    bank[:, 6, :].rearrange("p (i h g c) -> p i h g c", i=TT, g=2, c=CMP_PAD)[:, :, :, g, :], DH ** -0.5,
                    cbias[:, :, GROUP_HEADS * g:GROUP_HEADS * (g + 1), :],
                    ALU.mult, ALU.add))
            settle()
            link(dve.tensor_reduce(cmp_stat[:, 0, :], rows_c, AX.X, ALU.max))
            dve.tensor_tensor(rows_c, rows_c, row(cmp_stat[:, 0, :], CMP_PAD), ALU.subtract).then_inc(cmp_shifted, 1)
            dve.wait_ge(cmp_act, 2)
            link(dve.tensor_reduce(cmp_stat[:, 1, :], rows_c, AX.X, ALU.add))
            link(dve.reciprocal(cmp_stat[:, 2, :], cmp_stat[:, 1, :]))
            dve.wait_ge(small_copied, 1)
            for g in range(2):
                note(dve.tensor_tensor(
                    cmp_stat[:, 3, 16 * g:16 * g + 16].rearrange("p (i h) -> p i h", i=TT),
                    cmp_stat[:, 2, 16 * g:16 * g + 16].rearrange("p (i h) -> p i h", i=TT),
                    gate1[:, :, GROUP_HEADS * g:GROUP_HEADS * (g + 1), 0], ALU.mult))
            for g in range(2):
                m = dve.tensor_tensor(cmp_logits[:, g, :, :, :], cmp_logits[:, g, :, :, :],
                                      copies(valid_c, GROUP_HEADS, at=2), ALU.mult)
            m.then_inc(cmp_dve, 1)
            dve.wait_ge(cmp_pe, 6)
            dve.tensor_copy(cmp_probs_t[:, :, :].rearrange("p n q -> p (n q)"), bank[:, 4, :]).then_inc(cmp_dve, 1)
            dve.wait_ge(cmp_pe, 7)
            settle()
            for g in range(2):
                for i in range(TT):
                    at = 16 * g + 8 * i
                    m = dve.tensor_tensor(o1[:, i, N * g:N * g + N].rearrange("p (h d) -> p h d", d=DH),
                                          bank[:, 2 * i + g, :].rearrange("p (h d) -> p h d", d=DH),
                                          row(cmp_stat[:, 3, at:at + 8], DH), ALU.mult)
            m.then_inc(cmp_dve, 1)

            dve.wait_ge(bias_landed, 16)

            def set_done1(n):
                u = units1[n]
                s, n0 = u["set"], n - GROUP_HEADS + 1
                branch, g = s // 2, s % 2
                dve.wait_ge(mixed, n + 1)
                dve.wait_ge(probs_ready, 2 * (n + 1))
                sums = expsum1.rearrange("p (i n) -> p i n", i=TT)[:, :, n0:n0 + GROUP_HEADS]
                dve.wait_ge(cmp_dve, 9)
                link(dve.reciprocal(sums, sums))
                if branch < 2:
                    link(dve.tensor_tensor(sums, sums, gate1[:, :, GROUP_HEADS * g:GROUP_HEADS * (g + 1), 1 + branch],
                                           ALU.mult))
                for i in range(TT):
                    at = N * (s - 2 if branch == 2 else g)
                    part_ = o1[:, i, at:at + N]
                    dst = part_ if branch == 2 else share1
                    dve.tensor_tensor(dst.rearrange("p (h d) -> p h d", d=DH),
                                      bank[:, 4 + 2 * (s % 2) + i, :].rearrange("p (h d) -> p h d", d=DH),
                                      row(sums[:, i, :], DH), ALU.mult).then_inc(set_copied, 1)
                    if branch < 2:
                        dve.wait_ge(set_copied, 2 * s + i + 1)
                        link(dve.tensor_tensor(part_, part_, share1, ALU.add))

            attention(attention1, set_done1)
            dve.wait_ge(set_copied, 2 * 6)
            for i in range(TT):
                dve.tensor_copy(stat[:, 60 + i:61 + i], o1[:, i, D - 1:D]).then_inc(scaled, 1)
            split_turned(1)
            add_groups("w_out_t")

            scale_rows(1, norm2_rows)
            split_turned(2)
            def top16(step, rows_, src, left, values, at):
                for r in rows_:
                    if step == 0:
                        note(dve.max(values[:, r, 0:8], src[:, r, :]))
                    elif step == 1:
                        note(dve.match_replace(left[:, r, :], values[:, r, 0:8], src[:, r, :], LOWEST))
                        note(dve.max_index(at[:, r, 0:8], values[:, r, 0:8], src[:, r, :]))
                    elif step == 2:
                        note(dve.max(values[:, r, 8:16], left[:, r, :]))
                    else:
                        note(dve.max_index(at[:, r, 8:16], values[:, r, 8:16], left[:, r, :]))
                settle()

            def choose(g, p):
                if p == 2:
                    for i in range(TT):
                        n = 4 * i + g
                        dve.wait_ge(subkey_scores_done, TT * g + i + 1)
                        dve.tensor_copy(scores[:, 4 * n:4 * n + 4, :].rearrange("p r n -> p (r n)"),
                                        bank[:, 4 + TT * (g % 2) + i, :]).then_inc(subkey_scores_copied, 1)
                    dve.wait_ge(subkey_scores_copied, TT * (g + 1))
                elif p > 2 and p < 7:
                    top16(p - 3, [*range(4 * g, 4 * g + 4), *range(16 + 4 * g, 20 + 4 * g)], scores, scores_left, top, top_at)

            for g in range(4):
                b = group_done("peer_wq_t", g, between=lambda p: choose(g - 1, p) if g else None)
                for k in range(2):
                    dve.tensor_copy(peer_q[:, 4 * g + 2 * k:4 * g + 2 * k + 2, :].rearrange("p c t -> p (c t)"),
                                    bank[:, 2 * b + k, :]).then_inc(pair_copied[b], 1)
            for p in range(2, 7):
                choose(3, p)
            note(dve.tensor_copy(top_key.rearrange("p r k -> p (r k)"), top_at.rearrange("p r k -> p (r k)")))
            top_side = top.rearrange("p (r s) k -> p r s k", s=2)
            link(dve.tensor_tensor(pairs.rearrange("p r (a b) -> p r a b", a=TOPK), row(top_side[:, :, 0, :], TOPK),
                                   copies(top_side[:, :, 1, :], TOPK, at=2), ALU.add))
            for step in range(4):
                top16(step, range(TT * PEER_HEADS), pairs, pairs_left, best, best_at)
            sub = picked[:, 2, :, :].rearrange("p i (h k) -> p (i h) k", k=TOPK)
            dve.tensor_tensor(sub, best, row(best[:, :, 0], TOPK), ALU.subtract).then_inc(best_ready, 1)
            flat_at = best_at.rearrange("p r k -> p (r k)")
            note(dve.tensor_scalar(part_at[:, 0, :], flat_at, 4, None, ALU.logical_shift_right))
            link(dve.tensor_scalar(part_at[:, 1, :], flat_at, TOPK - 1, None, ALU.bitwise_and))
            link(dve.tensor_copy(part.rearrange("p s r -> p (s r)"), part_at.rearrange("p s r -> p (s r)")))
            keys = top_key.rearrange("p (r s) k -> p r s k", s=2)
            for s in range(2):
                link(dve.tensor_tensor(is_part, row(part[:, s, :], TOPK), copies(iota[:, 0:TOPK], TT * P), ALU.is_equal))
                four = is_part.rearrange("p (r j) a -> p r j a", j=TOPK)
                link(dve.tensor_tensor(four, four, copies(keys[:, :, s, :], TOPK, at=2), ALU.mult))
                link(dve.tensor_reduce(picked[:, s, :, :].rearrange("p i k -> p (i k)"), is_part, AX.X, ALU.add))
            dve.wait_ge(best_exp, 1)
            link(dve.tensor_reduce(best_sum[:, 0, :], sub, AX.X, ALU.add))
            link(dve.reciprocal(best_sum[:, 1, :], best_sum[:, 0, :]))
            dve.tensor_tensor(sub, sub, row(best_sum[:, 1, :], TOPK), ALU.mult).then_inc(picked_ready, 1)
            dve.wait_ge(picked_turned, 1)
            dve.tensor_copy(picked_t[:, 0:2, :].rearrange("p s t -> p (s t)"), bank[:, 4, :]).then_inc(picked_copied, 1)
            dve.tensor_copy(picked_t[:, 2, :], bank[:, 5, 0:T]).then_inc(picked_copied, 1)
            dve.wait_ge(picked_copied, 2)
            link(dve.tensor_copy(gate_high_r[:, :], picked_t[:, 2, :]))
            link(dve.tensor_tensor(picked_low, picked_t[:, 2, :], as_f32(gate_high_r[:, :]), ALU.subtract))
            link(dve.tensor_copy(picked_t[:, 2, :], as_f32(gate_high_r[:, :])))
            with dve.Fori(0, T // (SLOTS * FOUR)) as n:
                for c in range(SLOTS):
                    dve.wait_ge(gates_done[c], n + PRIMED)
                    token = bass.ds(FOUR * SLOTS * n + (FOUR * c + ACT_FIRST), 1)
                    dve.tensor_scalar(first_high[:, c, ACT_FIRST, :], iota[:, :], picked_t[:, 0, token], picked_t[:, 2, token],
                                      ALU.is_equal, ALU.mult)
                    for dst, key in ((second, 1), (first, 0)):
                        m = dve.tensor_tensor(dst[:, c, :, :], row(picked_t[:, key, bass.ds(FOUR * SLOTS * n + FOUR * c, FOUR)], P),
                                              copies(iota[:, :], FOUR), ALU.is_equal)
                    m.then_inc(onehots_ready[c], 1)

            def weigh(n, e):
                dve.wait_ge(gelu_done[e], n + 1 + PRIMED)
                if e == 0:
                    dve.wait_ge(gates_loaded, 16 * n + 16)
                    b, _, _, used = half("experts_t", QUAD - 1, n)
                    dve.wait_ge(half_used[b], used + -1 + PRIMED)
                q = T // QUARTER
                dve.tensor_tensor(weighed[:, e, :].rearrange("p (q t) -> p q t", q=q), hidden[:, e, :].rearrange("p (q t) -> p q t", q=q),
                                  gates_in[:, :, e, :], ALU.mult).then_inc(weighed_ready[e], 1)
                dve.wait_ge(weighed_high_ready[e], n + 1)
                dve.tensor_tensor(weighed_low[:, e, :], weighed[:, e, :], as_f32(weighed_high[:, e, :]), ALU.subtract
                                  ).then_inc(weighed_low_ready[e], 1)

            def add_share(n, o):
                if o % 4 == 3:
                    b, _, _, used = half("experts_t", 4 + o // 2, n)
                    dve.wait_ge(half_used[b], used + 1 + PRIMED)
                else:
                    dve.wait_ge(shares_done, 6 * n + (3 * (o // 4) + o % 4 + 1 + PRIMED))
                dve.wait_ge(share_added[o], n + PRIMED)
                t, at = o % 4 // 2, N * (2 * (o // 4) + o % 2)
                part_ = resid[:, t, at:at + N]
                dve.tensor_tensor(part_, bank[:, 2 + o % 6, :], part_, ALU.add).then_inc(share_added[o], 1)

            with dve.Fori(0, EXPERT_STEPS) as n:
                for p in range(QUAD):
                    if p == 4:
                        weigh(n, 1)
                    split_low(half("experts_t", p + LOOKAHEAD, n))
                    if p == 2:
                        weigh(n, 0)
                    if p in (5, 6):
                        for o in (0, 1) if p == 5 else (2, 3):
                            add_share(n, o)
                for o in range(4, 8):
                    add_share(n, o)

            dve.wait_ge(final_gain_landed, 16)
            dve.wait_ge(squared, TT * 3)
            rms_scale(2, D)
            for i in range(TT):
                dve.scalar_tensor_tensor(resid[:, i, :], resid[:, i, :], stat[:, 10 + i:11 + i], final_gain,
                                         ALU.mult, ALU.mult).then_inc(normed, 1)
            dve.wait_ge(normed, TT)
            scale_rows(3, norm3_rows)
            split_turned(3)
            for side in range(2):
                copy_groups("w_in_2_t", 4 * side, 2, lambda i, j, k: qkvz_half[side][:, k, bass.ds(i * 2 * N + j * N, N)])
            def heads_norm(p):
                i = p // 4
                heads = qk2[:, i, :].rearrange("p (h d) -> p h d", d=DH2)
                if p % 4 == 1:
                    dve.wait_ge(squared, TT * 4 + i + 1)
                    link(dve.tensor_reduce(stat[:, 24:40], squares.rearrange("p (h d) -> p h d", d=DH2), AX.X, ALU.add))
                    link(dve.tensor_scalar(stat[:, 40:56], stat[:, 24:40], 1.0 / DH2, EPS, ALU.mult, ALU.add))
                    dve.reciprocal(stat[:, 40:56], stat[:, 40:56]).then_inc(root_wanted, 1)
                elif p % 4 == 3:
                    dve.wait_ge(root_done, ROOTS.index(f"heads {i}") + 1)
                    dve.tensor_tensor(heads, heads, row(stat[:, 40:56], DH2), ALU.mult).then_inc(scaled, 1)

            def convolve(c):
                link(dve.tensor_scalar(xbc[:, c, :], xbc_raw[:, c, :], conv1[:, c, 3:4], conv1[:, c, 4:5], ALU.mult, ALU.add))
                for tap in range(1, SSM_TAPS):
                    m = dve.scalar_tensor_tensor(xbc[:, c, tap:T], xbc_raw[:, c, 0:T - tap], conv1[:, c, 3 - tap:4 - tap],
                                                 xbc[:, c, tap:T], ALU.mult, ALU.add)
                    if c == XBC_TILES - 1 and tap == SSM_TAPS - 1:
                        m.then_inc(normed, 1)
                    else:
                        link(m)

            def with_group_9(p):
                if p < 4:
                    convolve(p)

            def with_group_10(p):
                if p == 0:
                    copy_turned(4, qk_t)
                elif p < 5:
                    convolve(p + 3)

            for g, between in ((8, heads_norm), (9, with_group_9), (10, with_group_10)):
                b = group_done("w_in_2_t", g, between=between)
                for k in range(2):
                    c = 4 * (g - 8) + 2 * k
                    dve.tensor_copy(xbc_raw[:, c:c + 2, :].rearrange("p c t -> p (c t)"), bank[:, 2 * b + k, :]
                                    ).then_inc(pair_copied[b], 1)
                dve.wait_ge(pair_copied[b], 2 * (pair("w_in_2_t", g)[1] + 1) + PRIMED)
            dve.wait_ge(narrow_split, 3)
            dve.tensor_tensor(narrow_w[1][:, 0:KT * SSM_HEADS], dt_w.rearrange("p k n -> p (k n)"),
                              as_f32(narrow_w[0][:, 0:KT * SSM_HEADS]), ALU.subtract).then_inc(narrow_split, 1)
            for c in range(8, XBC_TILES):
                convolve(c)
            dve.wait_ge(small_done, 2)
            for t in range(TT):
                cols = slice(SSM_HEADS * t, SSM_HEADS * (t + 1))
                m = dve.tensor_tensor(dt_tmp[:, 0, cols], bank[:, 6 + t, 0:SSM_HEADS], rows[:, 1, :], ALU.add)
            m.then_inc(small_copied, 1)

            def set_done2(n):
                u = units2[n]
                s, n0 = u["set"], n - 3
                dve.wait_ge(mixed, UNITS + n + 1)
                dve.wait_ge(probs_ready, 2 * (UNITS + n + 1))
                sums = expsum2.rearrange("p (i n) -> p i n", i=TT)[:, :, n0:n0 + 4]
                link(dve.reciprocal(sums, sums))
                for i in range(TT):
                    dve.tensor_tensor(o2[:, i, N * (s - 6):N * (s - 5)].rearrange("p (h d) -> p h d", d=DH2),
                                      bank[:, 4 + 2 * (s % 2) + i, :].rearrange("p (h d) -> p h d", d=DH2),
                                      row(sums[:, i, :], DH2), ALU.mult).then_inc(set_copied, 1)

            attention(attention2, set_done2)

            dve.wait_ge(small_copied, 2)
            dve.scalar_tensor_tensor(dt_tmp[:, 1, :], dt_tmp[:, 0, :], -1.0, dt_tmp[:, 0, :], ALU.mult, ALU.max).then_inc(normed, 1)
            dve.wait_ge(scan_act, 2)
            link(dve.scalar_tensor_tensor(dt_[:, 0, :], dt_tmp[:, 0, :], 0.0, dt_tmp[:, 1, :], ALU.max, ALU.add))
            la = dt_[:, 1, :]
            dve.scalar_tensor_tensor(la.rearrange("p (i h) -> p i h", i=TT), dt_[:, 0, :].rearrange("p (i h) -> p i h", i=TT),
                                     -1.0, copies(dt_tmp[:, 2, 0:SSM_HEADS], TT), ALU.mult, ALU.mult).then_inc(scan_dve, 1)
            dve.wait_ge(scan_dve, 1)
            triangle = la_triu.rearrange("p (h l) -> p h l", l=P)
            note(dve.tensor_tensor(triangle, row(la[:, 0:SSM_HEADS], P), copies(triu[:, :], SSM_HEADS), ALU.mult))
            dve.wait_ge(scan_pe, 1)
            for n in range(4):
                m = dve.tensor_copy(x_tok[:, n // 2, N * (n % 2):N * (n % 2) + N], bank[:, 4 + n, :])
            m.then_inc(scan_dve, 1)
            dve.wait_ge(scan_pe, 3)
            for g in range(SSM_GROUPS):
                note(dve.tensor_copy(cb[:, g, :], bank[:, g, 0:3 * P]))
            link(dve.tensor_copy(dt_[:, 2, :], bank[:, 2, 0:TT * SSM_HEADS]))
            link(dve.tensor_tensor(dt_[:, 3, 0:SSM_HEADS], bank[:, 3, 0:SSM_HEADS], dt_[:, 2, 0:SSM_HEADS], ALU.subtract))
            for i in range(TT):
                dve.wait_ge(scan_pe, 4 + i)
                for blk, per_key, op in ([(0, dt_[:, 2, 0:SSM_HEADS], ALU.subtract)] if i == 0 else
                                         [(1, dt_[:, 2, SSM_HEADS:], ALU.subtract), (2, dt_[:, 3, 0:SSM_HEADS], ALU.add)]):
                    for c in range(4):
                        m = dve.tensor_tensor(decay[:, blk, 4 * c:4 * c + 4, :],
                                              bank[:, 4 + c, :].rearrange("p (h l) -> p h l", l=P),
                                              row(per_key[:, 4 * c:4 * c + 4], P), op)
                        note(m)
                if i == 0:
                    dve.tensor_tensor(triangle, row(la[:, SSM_HEADS:], P), copies(triu[:, :], SSM_HEADS),
                                      ALU.mult).then_inc(scan_dve, 1)
                settle()
                dve.tensor_tensor(decay[:, i, :, :], decay[:, i, :, :], copies(low_mask[:, :], SSM_HEADS), ALU.add
                                  ).then_inc(normed, 1)
            link(dve.tensor_tensor(x_dt.rearrange("p i (h d) -> p (i h) d", d=SSM_DH),
                                   x_tok.rearrange("p i (h d) -> p (i h) d", d=SSM_DH), row(dt_[:, 0, :], SSM_DH), ALU.mult))
            dve.wait_ge(scan_act, 3)
            for g in range(SSM_GROUPS):
                for blk, at in ((0, 0), (1, 2), (2, 1)):
                    part_ = decay[:, blk, GROUP_HEADS * g:GROUP_HEADS * (g + 1), :]
                    m = dve.tensor_tensor(part_, part_, copies(cb[:, g, P * at:P * at + P], GROUP_HEADS), ALU.mult)
                m.then_inc(scan_dve, 1)
            for i in range(TT):
                heads = x_tok[:, i, :].rearrange("p (h d) -> p h d", d=SSM_DH)
                note(dve.tensor_tensor(heads, heads, row(rows[:, 3, :], SSM_DH), ALU.mult))
            settle()
            dve.wait_ge(scan_pe, 6)
            for i in range(TT):
                for g in range(SSM_GROUPS):
                    note(dve.tensor_tensor(o2[:, i, SSM_W + N * g:SSM_W + N * (g + 1)], bank[:, 2 * i + g, :],
                                           x_tok[:, i, N * g:N * (g + 1)], ALU.add))
            settle()
            dve.wait_ge(scan_act, 4)
            y = o2[:, :, SSM_W:]
            link(dve.tensor_tensor(y, y, vz2[:, :, SSM_W:], ALU.mult))
            link(dve.tensor_tensor(squares.rearrange("p (i d) -> p i d", i=TT), y, y, ALU.mult))
            link(dve.tensor_reduce(stat[:, 24:28], squares.rearrange("p (n d) -> p n d", d=N), AX.X, ALU.add))
            link(dve.tensor_scalar(stat[:, 28:32], stat[:, 24:28], 1.0 / N, EPS, ALU.mult, ALU.add))
            dve.reciprocal(stat[:, 28:32], stat[:, 28:32]).then_inc(root_wanted, 1)
            dve.wait_ge(root_done, ROOTS.index("scan") + 1)
            for i in range(TT):
                part_ = y[:, i, :].rearrange("p (g d) -> p g d", d=N)
                dve.tensor_tensor(part_, part_, row(stat[:, 28 + 2 * i:30 + 2 * i], N), ALU.mult).then_inc(scaled, 1)
            split_turned(5)
            add_groups("w_out_2_t")

            scale_rows(5, norm4_rows)
            split_turned(6)
            def conv_step_of(i, j, step):
                b, used = pair("w_up_2_t", j)
                w = conv2[:, bass.ds(2 * i + j, 1), :].rearrange("p a n -> p (a n)")
                at = bass.ds(4 * i + 2 * j, 2)
                if step in (0, 1):
                    if step == 0:
                        dve.wait_ge(tap_done[j], i + 1)
                    else:
                        dve.wait_ge(conv_step[j], 4 * i + 4)
                    tap = step + 1
                    for q in range(4):
                        plain = bank[:, 2 * b + q // 2, T * (q % 2):T * (q % 2) + T - tap]
                        m = dve.scalar_tensor_tensor(taps[:, j, q, tap:T], plain, w[:, 4 * q + 2 - tap:4 * q + 3 - tap],
                                                     taps[:, j, q, tap:T], ALU.mult, ALU.add)
                        m.then_inc(conv_step[j] if tap == 1 else conv_done[j] if q < 2 else pair_copied[b], 1)
                elif step == 2:
                    dve.wait_ge(silu_done[j], i + 1)
                    dve.wait_ge(pair_copied[b], 2 * i + 2 * (used + 1) + PRIMED)
                    dve.tensor_tensor(taps[:, j, 0:2, :], taps[:, j, 0:2, :], taps[:, j, 2:4, :],
                                      ALU.mult).then_inc(ff_product_ready[j], 1)
                else:
                    dve.wait_ge(ff_high_ready[j], i + 1)
                    dve.tensor_tensor(ff_low[:, at, :], taps[:, j, 0:2, :], as_f32(ff_high[:, at, :]), ALU.subtract
                                      ).then_inc(hidden_ready[j], 1)

            def up_group(g, i=0, before=True):
                for p in range(QUAD):
                    split_low(half("w_up_2_t", p + LOOKAHEAD, i * 2 + g))
                    if before and p < 4:
                        conv_step_of(i + (g - 1) // 2, (g - 1) % 2, p)

            up_group(0, before=False)
            with dve.Fori(0, FF_GROUPS // 2 - 1) as i:
                for g in (1, 2):
                    up_group(g, i)
            up_group(1, FF_GROUPS // 2 - 1)
            for step in range(4):
                conv_step_of(FF_GROUPS // 2 - 1, 1, step)

            def down_group(b, g, column, last=False):
                for p in range(DOWN_HALVES):
                    if not last or p + LOOKAHEAD < DOWN_HALVES:
                        split_low(down_half(p + LOOKAHEAD, g))
                sb_, _, _, used = down_half(DOWN_HALVES - 1, g)
                dve.wait_ge(half_used[sb_], used + 1 + PRIMED)
                for t in range(TT):
                    part_ = resid[:, t, column]
                    dve.tensor_tensor(part_, bank[:, 2 * b + t, :], part_, ALU.add).then_inc(pair_copied[b], 1)

            for g in range(4):
                down_group(pair("w_down_2_t", g)[0], g, slice(N * g, N * g + N), last=g == 3)

        @block.scalar
        def _(act):
            prime(act, [*gates_copied, *gelu_done])
            for dst, name in TABLES:
                act.dma_start(dst, ins[name]).then_inc(tables_landed, 16)
            for dst, name in CONSTS:
                act.dma_start(dst[:], ins[name]).then_inc(consts_landed, 16)
            for dst, name in STAGE1:
                act.dma_start(dst, ins[name]).then_inc(stage1_landed, 16)

            def split_high(h):
                b, r, which, used = h
                act.wait_ge(raw_landed[r], 16 * used + 16)
                act.wait_ge(half_used[b], used + PRIMED)
                act.activation(high[b][:, :], raw[r][:, HALF * which:HALF * (which + 1)], ACT.Copy
                               ).then_inc(high_ready[b], 1)

            def split_groups(name, groups_, i=0):
                for g in groups_:
                    for p in range(QUAD):
                        split_high(half(name, p + LOOKAHEAD, i * 2 + g))

            def split_loop(name, steps_):
                with act.Fori(0, steps_) as i:
                    split_groups(name, range(2), i)

            def root(which, at):
                act.wait_ge(root_wanted, ROOTS.index(which) + 1)
                act.activation(at, at, ACT.Sqrt).then_inc(root_done, 1)

            def square_rows(e, dst):
                for i in range(TT):
                    act.activation(dst[:, i, :], resid[:, i, :], ACT.Square, accum_out=stat[:, 4 * e + i:4 * e + i + 1]
                                   ).then_inc(squared, 1)
                root(e, stat[:, 4 * e + 2:4 * e + 4])

            def split_turned(n):
                for b in range(8):
                    at = slice(4 * (b % 4), 4 * (b % 4) + 4), slice(P * (b // 4), P * (b // 4) + P)
                    act.wait_ge(turned_read, TURN0[n] + b + 1)
                    act.activation(act_high[:, at[0], at[1]], act_whole[:, at[0], at[1]], ACT.Copy
                                   ).then_inc(turned_high, 1)

            def attention(a):
                units, first, logits = a["units"], a["first"], a["logits"]

                def exps(n):
                    g, b = first + n, (first + n) % 2
                    s = 0 if units[n]["sink"] is None else 1
                    act.wait_ge(logits_ready, 2 * (g + 1))
                    for at, width, col in ((0, T + s, UNITS + n), (T + 1, P + s, n)):
                        part_ = logits[:, b, at:at + width]
                        act.activation(part_, part_, ACT.Exp, bias=a["negmax"][:, col:col + 1],
                                       accum_out=a["expsum"][:, col:col + 1]).then_inc(probs_ready, 1)

                def copy_probs(n):
                    g, b = first + n, (first + n) % 2
                    act.wait_ge(probs_turned, g + 1)
                    if g >= 2:
                        act.wait_ge(mixed, g - 1)
                    act.activation(a["probs_t"][:, b, :], bank[:, 2 + b, 0:3 * P], ACT.Copy).then_inc(probs_copied, 1)

                for n in range(len(units) + 1):
                    if n < len(units):
                        exps(n)
                    if n >= 1:
                        copy_probs(n - 1)

            act.wait_ge(x_landed, 16 * TT)
            square_rows(0, o1)
            split_turned(0)
            for p in range(LOOKAHEAD):
                split_high(half("w_in_t", p))
            act.wait_ge(tables_copied, 1)
            act.dma_start(bias_dram[:].rearrange("(h j) -> h j", j=3 * P), by_distance[0:2 * HEADS, :]).then_inc(bias_stored, 16)
            split_loop("w_in_t", 2)
            act.wait_ge(stage1_landed, STAGE1_DMAS)
            act.activation(narrow_w[0][:, :], gate_w.rearrange("p k n -> p (k n)"), ACT.Copy).then_inc(narrow_split, 1)
            act.wait_ge(bias_stored, 16)
            act.dma_start(bias_copies[:, :], bias_dram[:].partition_broadcast(P)).then_inc(bias_spread, 16)
            split_groups("w_in_t", (4, 5))
            act.wait_ge(bias_spread, 16)
            act.wait_ge(small_done, 1)
            act.dma_start(bias1, bass.AP(tensor=bias_copies, offset=P - 1, ap=[[BIAS_ROW - 1, P], [3 * P, 2 * HEADS], [1, T]])
                          ).then_inc(bias_landed, 16)
            act.wait_ge(small_done, 1)
            for t in range(TT):
                m = act.activation(gate1[:, t, :, :].rearrange("p h b -> p (h b)"), bank[:, 5 + t, 0:GATES], ACT.Sigmoid)
            m.then_inc(small_copied, 1)
            act.wait_ge(cmp_pe, 1)
            act.activation(cmp_hid_rows[0:2 * CMP_PAD, :, :], bank[0:2 * CMP_PAD, 6:8, 0:P], ACT.Gelu_apprx_tanh
                           ).then_inc(cmp_act, 1)
            act.wait_ge(cmp_shifted, 1)
            flat = cmp_logits[:, :, :, :, :].rearrange("p g i h c -> p (g i h c)")
            act.activation(flat, flat, ACT.Exp).then_inc(cmp_act, 1)
            attention(attention1)

            split_turned(1)
            split_loop("w_out_t", 2)
            wait_pairs(act, "w_out_t")
            square_rows(1, norm2_rows)
            split_turned(2)
            split_loop("peer_wq_t", 2)
            act.wait_ge(best_ready, 1)
            flat = picked[:, 2, :, :].rearrange("p i k -> p (i k)")
            act.activation(flat, flat, ACT.Exp).then_inc(best_exp, 1)
            steps = QUARTER // (SLOTS * FOUR)

            def gate_first(q, n, c):
                act.wait_ge(onehots_ready[c], n + (steps * q + 1))
                for j in range(ACT_FIRST):
                    m = act.activation(first_high[:, c, j, :], first[:, c, j, :], ACT.Copy,
                                       scale=picked_t[:, 2, bass.ds(SLOTS * FOUR * n + (QUARTER * q + FOUR * c + j), 1)])
                m.then_inc(first_high_ready[c], 1)

            def copy_gates(q, n, c):
                act.wait_ge(gates_done[c], n + (steps * q + 1 + PRIMED))
                act.activation(gates_out[:, q % 2, :, bass.ds(SLOTS * FOUR * n + FOUR * c, FOUR)],
                               bank[:, 6 + c % 2, :].rearrange("p (t e) -> p e t", t=FOUR), ACT.Copy
                               ).then_inc(gates_copied[c % 2], 1)

            for q in range(T // QUARTER):
                if q >= 2:
                    act.wait_ge(gates_stored[q % 2], 16 * (q // 2))
                for c in range(2):
                    gate_first(q, 0, c)
                with act.Fori(0, steps - 1) as n:
                    for c in range(SLOTS):
                        gate_first(q, n + (c + 2) // SLOTS, (c + 2) % SLOTS)
                        copy_gates(q, n, c)
                for c in range(SLOTS):
                    if c + 2 < SLOTS:
                        gate_first(q, steps - 1, c + 2)
                    copy_gates(q, steps - 1, c)
                for b in range(2):
                    act.wait_ge(gates_copied[b], QUARTER // 8 * (q + 1) + PRIMED)
                act.dma_start(gates_dram[q], gates_out[:, q % 2, :, :]).then_inc(gates_stored[q % 2], 16)

            def gelu(n, e):
                b, _, _, used = half("experts_t", 2 * e + 1, n)
                act.wait_ge(half_used[b], used + 1 + PRIMED)
                act.wait_ge(weighed_ready[e], n + PRIMED)
                act.activation(hidden[:, e, :], bank[:, e, 0:T], ACT.Gelu_apprx_tanh).then_inc(gelu_done[e], 1)

            def weigh(n, e):
                act.wait_ge(weighed_ready[e], n + 1 + PRIMED)
                act.activation(weighed_high[:, e, :], weighed[:, e, :], ACT.Copy).then_inc(weighed_high_ready[e], 1)

            with act.Fori(0, EXPERT_STEPS) as n:
                for p in range(QUAD):
                    if p == 4:
                        gelu(n, 1)
                        weigh(n, 1)
                    split_high(half("experts_t", p + LOOKAHEAD, n))
                    if p == 2:
                        gelu(n, 0)
                        weigh(n, 0)

            for o in range(8):
                act.wait_ge(share_added[o], EXPERT_STEPS + PRIMED)
            square_rows(2, o2)
            act.wait_ge(normed, TT)
            square_rows(3, norm3_rows)
            split_turned(3)
            split_loop("w_in_2_t", 4)
            for p in range(QUAD):
                i = p // 4
                split_high(half("w_in_2_t", p + LOOKAHEAD, 8))
                if p % 4 == 0:
                    if i == 0:
                        for g in (2, 3):
                            b, used = pair("w_in_2_t", g)
                            act.wait_ge(pair_copied[b], 2 * (used + 1) + PRIMED)
                    else:
                        act.wait_ge(scaled, TT * 4 + i)
                    act.activation(squares, qk2[:, i, :], ACT.Square).then_inc(squared, 1)
                elif p % 4 == 2:
                    root(f"heads {i}", stat[:, 40:56])
            split_groups("w_in_2_t", (9, 10))
            act.wait_ge(stage4_landed, STAGE4_DMAS)
            act.activation(narrow_w[0][:, 0:KT * SSM_HEADS], dt_w.rearrange("p k n -> p (k n)"), ACT.Copy).then_inc(narrow_split, 1)
            attention(attention2)
            act.wait_ge(normed, TT + 1)
            flat = xbc.rearrange("p c t -> p (c t)")
            act.activation(flat, flat, ACT.Silu).then_inc(scan_act, 1)
            act.wait_ge(normed, TT + 2)
            act.activation(dt_tmp[:, 1, :], dt_tmp[:, 1, :], ACT.Exp, scale=-1.0).then_inc(act_step, 1)
            act.wait_ge(act_step, 1)
            act.activation(dt_tmp[:, 2, 0:SSM_HEADS], rows[:, 2, :], ACT.Exp)
            act.activation(dt_tmp[:, 1, :], dt_tmp[:, 1, :], ACT.Ln, bias=1.0).then_inc(scan_act, 1)
            act.wait_ge(normed, TT + 4)
            for blk in range(3):
                flat = decay[:, blk, :, :].rearrange("p h l -> p (h l)")
                m = act.activation(flat, flat, ACT.Exp)
            m.then_inc(scan_act, 1)
            z = vz2[:, :, SSM_W:]
            act.activation(z, z, ACT.Silu).then_inc(scan_act, 1)
            root("scan", stat[:, 28:32])
            split_turned(5)
            split_loop("w_out_2_t", 2)
            wait_pairs(act, "w_out_2_t")
            square_rows(5, norm4_rows)
            split_turned(6)

            def conv_step_of(i, j, step):
                b, used = pair("w_up_2_t", j)
                w = conv2[:, bass.ds(2 * i + j, 1), :].rearrange("p a n -> p (a n)")
                if step == 0:
                    sb_, _, _, used_ = half("w_up_2_t", QUAD - 1, i * 2 + j)
                    act.wait_ge(half_used[sb_], used_ + 1 + PRIMED)
                    act.wait_ge(hidden_ready[j], i + PRIMED)
                    for q in range(4):
                        m = act.activation(taps[:, j, q, :], bank[:, 2 * b + q // 2, T * (q % 2):T * (q % 2) + T],
                                           ACT.Identity, scale=w[:, 4 * q + 2:4 * q + 3], bias=w[:, 4 * q + 3:4 * q + 4])
                    m.then_inc(tap_done[j], 1)
                elif step == 2:
                    act.wait_ge(conv_done[j], 2 * i + 2)
                    gate_taps = taps[:, j, 0:2, :].rearrange("p q t -> p (q t)")
                    act.activation(gate_taps, gate_taps, ACT.Silu).then_inc(silu_done[j], 1)
                elif step == 3:
                    act.wait_ge(ff_product_ready[j], i + 1)
                    act.activation(ff_high[:, bass.ds(4 * i + 2 * j, 2), :], taps[:, j, 0:2, :], ACT.Copy).then_inc(ff_high_ready[j], 1)

            def up_group(g, i=0, before=True):
                for p in range(QUAD):
                    split_high(half("w_up_2_t", p + LOOKAHEAD, i * 2 + g))
                    if before and p < 4:
                        conv_step_of(i + (g - 1) // 2, (g - 1) % 2, p)

            up_group(0, before=False)
            with act.Fori(0, FF_GROUPS // 2 - 1) as i:
                for g in (1, 2):
                    up_group(g, i)
            up_group(1, FF_GROUPS // 2 - 1)
            for step in range(4):
                conv_step_of(FF_GROUPS // 2 - 1, 1, step)
            for g in range(4):
                for p in range(DOWN_HALVES):
                    if g < 3 or p + LOOKAHEAD < DOWN_HALVES:
                        split_high(down_half(p + LOOKAHEAD, g))

        @block.gpsimd
        def _(pool):
            wait_pairs(pool, "w_out_t")
            pool.dma_start(subkeys, ins["subkeys"]).then_inc(subkeys_landed, 16)
            with pool.Fori(0, T // (SLOTS * FOUR)) as n:
                for c in range(SLOTS):
                    pool.wait_ge(onehots_ready[c], n + 1)
                    pool.tensor_tensor(first_low[c], first[:, c, :, :],
                                       row(picked_low[:, bass.ds(SLOTS * FOUR * n + FOUR * c, FOUR)], P), ALU.mult
                                       ).then_inc(first_low_ready[c], 1)
            pool.wait_ge(gates_stored[0], 16 * 2)
            pool.dma_start(final_gain, ins["final_norm"].partition_broadcast(P)).then_inc(final_gain_landed, 16)
            pool.wait_ge(weighed_ready[1], EXPERT_STEPS + PRIMED)
            for dst, name in STAGE4:
                pool.dma_start(dst, ins[name]).then_inc(stage4_landed, 16)


def bucket_of(distance):
    d = np.maximum(distance, 0)
    large = EXACT + (np.log(np.maximum(d, 1).astype(np.float32) / np.float32(EXACT))
                     / np.float32(math.log(MAX_DIST / EXACT)) * (BUCKETS - EXACT)).astype(np.int32)
    return np.where(d < EXACT, d, np.minimum(large, BUCKETS - 1))


def one_hot(distances):
    distances = np.asarray(distances)
    table = np.zeros((BUCKETS + 2, distances.size), np.float32)
    ok = distances >= 0
    table[bucket_of(distances[ok]), np.nonzero(ok)[0]] = 1.0
    table[BUCKETS, ~ok] = 1.0
    table[BUCKETS + 1, distances >= SWA_WINDOW] = 1.0
    return table


def constants():
    p = np.arange(P)
    c = np.arange(CMP_PAD)
    t = np.arange(T).reshape(TT, P).T
    valid = (t[:, :, None] >= CMP_STRIDE * c + CMP_LEN - 1) & (c < N_CMP)
    upper = p[:, None] <= p[None, :]
    return {
        "c_ident": np.eye(P), "c_ones": np.ones((P, P)), "c_iota": np.tile(p, (P, 1)), "c_triu": upper,
        "c_low_mask": np.where(upper, 0.0, NEG),
        "c_causal": np.where(p[:, None] + P >= np.arange(T)[None, :], 0.0, NEG),
        "c_onehot_rev": one_hot(T - 1 - np.arange(3 * P)), "c_onehot_cmp": one_hot(np.arange(CMP_FIRST, T)),
        "c_block_of": p[:, None] // CMP_PAD == np.arange(GROUP_HEADS)[None, :], "c_valid": valid,
    }


def tiles_of(w, n):
    k, columns = w.shape
    w = w.reshape(k // 512, 4, P, columns // n, n).transpose(3, 0, 2, 1, 4)
    return np.ascontiguousarray(w).reshape(-1, P, 4 * n)


def laid_out(a):
    def column(v):
        return v.reshape(-1, P).T

    def in_rows(v):
        return np.broadcast_to(v, (P, v.size))

    w_in = a["w_in"][0]
    at = np.cumsum([0, HEADS * DH, P, P, P, P, P, P, GATES, HEADS * DH, P, P])
    q_a, kc, vc, ks, vs, kw, vw, gate, q_b, k_b, v_b = (w_in[:, x:y] for x, y in zip(at[:-1], at[1:]))

    def by_pairs(q):
        return q.reshape(D, 2, GROUP_HEADS, DH).transpose(0, 2, 1, 3).reshape(D, HEADS * DH)

    w_in = np.concatenate([by_pairs(q_a), by_pairs(q_b), ks, kw, k_b, kc, vc, vs, vw, v_b], axis=1)
    w_in_2 = a["w_in_2"][0]
    w_up = a["w_up_2"][0].reshape(D, 2, FF_GROUPS, 2 * P).transpose(0, 2, 1, 3).reshape(D, -1)
    u = a["peer_u"][0].reshape(EXPERT_STEPS_, 2, P, KT, P).transpose(0, 1, 4, 3, 2).reshape(EXPERT_STEPS_, 2, P, TILE)
    v = a["peer_v"][0].reshape(EXPERT_STEPS_, 2, P, 2, HALF).transpose(0, 3, 2, 1, 4).reshape(EXPERT_STEPS_, 2, P, TILE)
    rel = np.concatenate([a["rel_bias"], np.full((1, 2 * HEADS), NEG, np.float32),
                          np.concatenate([np.zeros((1, HEADS), np.float32), np.full((1, HEADS), NEG, np.float32)], axis=1)])

    def w1(w):
        return np.tile(w[0].reshape(CMP_LEN, DH, CMP_HIDDEN).transpose(1, 0, 2), (2, 1, 1))

    ones = np.ones((P, KT), np.float32)
    conv2 = np.concatenate([a["ffn_conv_w_2"][0], a["ffn_conv_b_2"]], axis=0)
    out = {
        "x": a["x"], "w_in_t": tiles_of(w_in, N), "w_out_t": tiles_of(a["w_out"][0], N),
        "peer_wq_t": tiles_of(a["peer_wq"][0], N), "experts_t": np.concatenate([u, v], axis=1).reshape(-1, P, TILE),
        "w_in_2_t": tiles_of(w_in_2[:, :-SSM_HEADS], N), "w_out_2_t": tiles_of(a["w_out_2"][0], N),
        "w_up_2_t": tiles_of(w_up, N), "w_down_2_t": tiles_of(a["w_down_2"][0], N),
        "gate_w": gate.reshape(KT, P, GATES).transpose(1, 0, 2),
        "dt_w": w_in_2[:, -SSM_HEADS:].reshape(KT, P, SSM_HEADS).transpose(1, 0, 2),
        "gains": np.stack([column(a["attn_norm"]), ones, column(a["ffn_norm"]), column(a["norm1_w_2"]),
                           np.concatenate([np.repeat(a["q_norm_w_2"].T, 8, 1), np.repeat(a["k_norm_w_2"].T, 8, 1)], axis=1),
                           np.concatenate([ones[:, :8], column(a["ssm_norm_w_2"])], axis=1), column(a["norm2_w_2"])], axis=1),
        "conv1": np.concatenate([a["ssm_conv_w_2"][0], a["ssm_conv_b_2"]], axis=0).reshape(5, XBC_TILES, P).transpose(2, 1, 0),
        "conv2": conv2.reshape(4, 2, FF_GROUPS, 2, P).transpose(4, 2, 1, 3, 0).reshape(P, FF_GROUPS, 16),
        "rows": np.stack([in_rows(a[n]) for n in ("sinks", "dt_bias_2", "a_log_2", "d_skip_2")], axis=1),
        "bias_rows": rel, "cmp_w1": np.stack([w1(a["cmp_w1_k"]), w1(a["cmp_w1_v"])], axis=1),
        "cmp_w2": np.stack([a["cmp_w2_k"][0], a["cmp_w2_v"][0]], axis=1),
        "cmp_pos": np.stack([np.tile(a["cmp_pos_k"][0].T, (2, 1)), np.tile(a["cmp_pos_v"][0].T, (2, 1))], axis=1),
        "subkeys": a["peer_subkeys"][0].transpose(2, 0, 1), "final_norm": a["final_norm"],
        **constants(),
    }
    return {k: np.ascontiguousarray(v, dtype=np.float32) for k, v in out.items()}


EXPERT_STEPS_ = EXPERT_TILES // 2


def kernel(**inputs):
    import concourse.bacc as bacc
    from concourse.bass_utils import run_bass_kernel_spmd as run

    nc = bacc.Bacc("TRN2", target_bir_lowering=False, num_devices=1)
    arrays = laid_out({k: np.asarray(v) for k, v in inputs.items()})
    ins = {k: nc.dram_tensor("in_" + k, list(v.shape), F32, kind="ExternalInput").ap() for k, v in arrays.items()}
    out = nc.dram_tensor("out", [1, T, D], F32, kind="ExternalOutput").ap()
    build(nc, ins, out)
    return run(nc, [{"in_" + k: v for k, v in arrays.items()}], core_ids=[0]).results[0]["out"]
```
